# Optimizing a Trainium2 kernel written in Bass

```python
import math
import jax, jax.numpy as jnp
from jax import lax
import numpy as np

D_MODEL = 1024
BATCH = 1
SEQ = 1024
DEPTH = 1
DEC_BATCH = 8
DEC_SEQ = 1
PAST_LEN = 1024
PAGE_SIZE = 128

GLA_HEADS = 4
GLA_DK = D_MODEL // 16
GLA_DV = D_MODEL // 8
GLA_RANK = 16
GLA_TAU = 16.0
GLA_CHUNK = 16
DIFF_HEADS = 4
DIFF_HEAD_DIM = D_MODEL // 16
DIFF_V_DIM = 2 * DIFF_HEAD_DIM
Q_BLOCK = 128
GLA_QK = GLA_HEADS * GLA_DK
GLA_V = GLA_HEADS * GLA_DV
DIFF_QK = DIFF_HEADS * 2 * DIFF_HEAD_DIM
DIFF_V = DIFF_HEADS * DIFF_V_DIM
D_IN = 2 * GLA_QK + 2 * GLA_V + GLA_RANK + 2 * DIFF_QK + DIFF_V
D_MIX = GLA_V + DIFF_V
N_GROUPS = 4
EXPERTS_PER_GROUP = 4
N_EXPERTS = N_GROUPS * EXPERTS_PER_GROUP
EXPERT_FF = D_MODEL // 4
TOP_K_IN_GROUP = 2
EPS = 1e-6

kernel_name = 'hymba_gla_diffattn_hier_moe_step'

def rmsnorm(x, g):
    xf = x.astype(jnp.float32)
    y = xf * lax.rsqrt(jnp.mean(xf * xf, axis=-1, keepdims=True) + EPS)
    return (y * g.astype(jnp.float32)).astype(x.dtype)

def project_heads(h, w_in, w_a2, b_a):
    B, L, _ = h.shape
    z = h @ w_in
    sizes = (GLA_QK, GLA_QK, GLA_V, GLA_V, GLA_RANK, DIFF_QK, DIFF_QK, DIFF_V)
    idx = [int(i) for i in np.cumsum(sizes)[:-1]]
    gq, gk, gv, gr, g_lr, dq, dk, dv = jnp.split(z, idx, axis=-1)
    log_a = jax.nn.log_sigmoid((g_lr @ w_a2 + b_a).astype(jnp.float32)) / GLA_TAU
    return (gq.reshape(B, L, GLA_HEADS, GLA_DK), gk.reshape(B, L, GLA_HEADS, GLA_DK),
            gv.reshape(B, L, GLA_HEADS, GLA_DV), gr,
            log_a.reshape(B, L, GLA_HEADS, GLA_DK),
            dq.reshape(B, L, DIFF_HEADS, 2 * DIFF_HEAD_DIM),
            dk.reshape(B, L, DIFF_HEADS, 2 * DIFF_HEAD_DIM),
            dv.reshape(B, L, DIFF_HEADS, DIFF_V_DIM))

def gla_chunked(q, k, v, log_a, s0):
    B, L, H, DK = q.shape
    DV = v.shape[-1]
    C = GLA_CHUNK
    pad = (-L) % C
    NC = (L + pad) // C

    def blocks(t):
        t = jnp.pad(t.astype(jnp.float32), ((0, 0), (0, pad), (0, 0), (0, 0)))
        return t.reshape(B, NC, C, H, t.shape[-1]).transpose(0, 3, 1, 2, 4)

    qc = blocks(q) * (GLA_DK ** -0.5)
    kc = blocks(k)
    vc = blocks(v)
    bc = jnp.cumsum(blocks(log_a), axis=3)
    causal = jnp.tril(jnp.ones((C, C), dtype=bool))[:, :, None]
    rel = bc[..., :, None, :] - bc[..., None, :, :]
    decay = jnp.where(causal, jnp.exp(jnp.where(causal, rel, 0.0)), 0.0)
    scores = jnp.einsum('bhnid,bhnjd,bhnijd->bhnij', qc, kc, decay)
    o_intra = jnp.einsum('bhnij,bhnjv->bhniv', scores, vc)
    b_last = bc[..., -1:, :]
    u = jnp.einsum('bhncd,bhncv->nbhdv', kc * jnp.exp(b_last - bc), vc)
    a_chunk = jnp.exp(b_last[..., 0, :]).transpose(2, 0, 1, 3)

    def step(s, inp):
        a, uu = inp
        return a[..., None] * s + uu, s

    s_final, s_start = lax.scan(step, s0.astype(jnp.float32), (a_chunk, u))
    o_inter = jnp.einsum('bhncd,nbhdv->bhncv', qc * jnp.exp(bc), s_start)
    o = (o_intra + o_inter).transpose(0, 2, 3, 1, 4).reshape(B, NC * C, H, DV)[:, :L]
    return o.astype(v.dtype), s_final.astype(s0.dtype)

def diff_attend(q, k, v, lam, q_pos, k_pos):
    q1, q2 = jnp.split(q, 2, axis=-1)
    k1, k2 = jnp.split(k, 2, axis=-1)
    mask = k_pos[None, :] <= q_pos[:, None]
    scale = DIFF_HEAD_DIM ** -0.5

    def probs(qa, ka):
        s = jnp.einsum('bqhd,bkhd->bhqk', qa, ka).astype(jnp.float32) * scale
        return jax.nn.softmax(jnp.where(mask, s, -jnp.inf), axis=-1)

    w = probs(q1, k1) - lam * probs(q2, k2)
    return jnp.einsum('bhqk,bkhv->bqhv', w.astype(v.dtype), v)

def diff_attn_prompt(q, k, v, lam):
    B, L, H, E = q.shape
    nb = L // Q_BLOCK
    qb = q.reshape(B, nb, Q_BLOCK, H, E).transpose(1, 0, 2, 3, 4)
    k_pos = jnp.arange(L)

    def one(args):
        i, qi = args
        return diff_attend(qi, k, v, lam, i * Q_BLOCK + jnp.arange(Q_BLOCK), k_pos)

    o = lax.map(one, (jnp.arange(nb), qb))
    return o.transpose(1, 0, 2, 3, 4).reshape(B, L, H, -1)

def hier_moe(h, w_rg, b_rg, w_re, b_re, w_gate, w_up, w_down):
    B, L, D = h.shape
    t = h.reshape(B * L, D)
    lg = (t @ w_rg).astype(jnp.float32) + b_rg
    pg = jax.nn.softmax(lg, axis=-1)
    g = jnp.argmax(lg, axis=-1)
    p_top = jnp.take_along_axis(pg, g[:, None], axis=-1)
    le_all = jnp.einsum('td,gde->tge', t, w_re)
    le = jnp.take_along_axis(le_all, g[:, None, None], axis=1)[:, 0].astype(jnp.float32) + b_re[g]
    top_v, top_i = lax.top_k(le, TOP_K_IN_GROUP)
    w2 = jax.nn.softmax(top_v, axis=-1) * p_top
    ids = g[:, None] * EXPERTS_PER_GROUP + top_i
    gates = jnp.sum(jax.nn.one_hot(ids, N_EXPERTS, dtype=jnp.float32) * w2[..., None], axis=1)
    hid = jax.nn.silu(jnp.einsum('td,edf->tef', t, w_gate)) * jnp.einsum('td,edf->tef', t, w_up)
    hid = hid * gates[..., None].astype(hid.dtype)
    out = jnp.einsum('tef,efd->td', hid, w_down)
    return out.reshape(B, L, D)

def hybrid_layer(x, p, lam, lam_init, s0, past_k, past_v):
    (norm1, w_in, w_a2, b_a, gla_g, diff_g, w_out, norm2,
     w_rg, b_rg, w_re, b_re, w_gate, w_up, w_down) = p
    B, L, _ = x.shape
    h = rmsnorm(x, norm1)
    gq, gk, gv, gr, log_a, dq, dk, dv = project_heads(h, w_in, w_a2, b_a)
    gla_o, s_new = gla_chunked(gq, gk, gv, log_a, s0)
    gla_o = rmsnorm(gla_o, gla_g) * jax.nn.silu(gr).reshape(B, L, GLA_HEADS, GLA_DV)
    if past_k is None:
        diff_o = diff_attn_prompt(dq, dk, dv, lam)
    else:
        past_len = past_k.shape[1]
        keys = jnp.concatenate([past_k, dk], axis=1)
        vals = jnp.concatenate([past_v, dv], axis=1)
        diff_o = diff_attend(dq, keys, vals, lam, past_len + jnp.arange(L), jnp.arange(past_len + L))
    diff_o = rmsnorm(diff_o, diff_g) * (1.0 - lam_init)
    mix = jnp.concatenate([gla_o.reshape(B, L, GLA_V), diff_o.reshape(B, L, DIFF_V)], axis=-1)
    x = x + mix @ w_out
    x = x + hier_moe(rmsnorm(x, norm2), w_rg, b_rg, w_re, b_re, w_gate, w_up, w_down)
    return x, dk, dv, s_new

def setup_inputs(seed: int = 0) -> dict:
    key = jax.random.key(seed)
    ks = jax.random.split(key, 32)
    n_pages = PAST_LEN // PAGE_SIZE
    n_used = DEC_BATCH * n_pages
    n_pool = n_used + max(1, n_used // 4)

    def nrm(k, shape, scale):
        return jax.random.normal(k, shape, jnp.float32) * scale

    return {
        'x_prompt': nrm(ks[0], (BATCH, SEQ, D_MODEL), 1.0),
        'x_sample': nrm(ks[1], (DEC_BATCH, DEC_SEQ, D_MODEL), 1.0),
        'cache_k': nrm(ks[2], (DEPTH, n_pool, PAGE_SIZE, DIFF_HEADS, 2 * DIFF_HEAD_DIM), 1.0),
        'cache_v': nrm(ks[3], (DEPTH, n_pool, PAGE_SIZE, DIFF_HEADS, DIFF_V_DIM), 1.0),
        'state_gla': nrm(ks[4], (DEPTH, DEC_BATCH, GLA_HEADS, GLA_DK, GLA_DV), 1.0),
        'page_table': jax.random.permutation(ks[5], n_pool)[:n_used].reshape(DEC_BATCH, n_pages).astype(jnp.int32),
        'norm1_g': 1.0 + nrm(ks[6], (DEPTH, D_MODEL), 0.05),
        'w_in': nrm(ks[7], (DEPTH, D_MODEL, D_IN), D_MODEL ** -0.5),
        'w_a2': nrm(ks[8], (DEPTH, GLA_RANK, GLA_QK), GLA_RANK ** -0.5),
        'b_a': nrm(ks[9], (DEPTH, GLA_QK), 0.1),
        'gla_norm_g': 1.0 + nrm(ks[10], (DEPTH, GLA_DV), 0.05),
        'lambda_q1': nrm(ks[11], (DEPTH, DIFF_HEAD_DIM), 0.1),
        'lambda_k1': nrm(ks[12], (DEPTH, DIFF_HEAD_DIM), 0.1),
        'lambda_q2': nrm(ks[13], (DEPTH, DIFF_HEAD_DIM), 0.1),
        'lambda_k2': nrm(ks[14], (DEPTH, DIFF_HEAD_DIM), 0.1),
        'diff_norm_g': 1.0 + nrm(ks[15], (DEPTH, DIFF_V_DIM), 0.05),
        'w_out': nrm(ks[16], (DEPTH, D_MIX, D_MODEL), D_MIX ** -0.5),
        'norm2_g': 1.0 + nrm(ks[17], (DEPTH, D_MODEL), 0.05),
        'w_router_g': nrm(ks[18], (DEPTH, D_MODEL, N_GROUPS), D_MODEL ** -0.5),
        'b_router_g': nrm(ks[19], (DEPTH, N_GROUPS), 0.01),
        'w_router_e': nrm(ks[20], (DEPTH, N_GROUPS, D_MODEL, EXPERTS_PER_GROUP), D_MODEL ** -0.5),
        'b_router_e': nrm(ks[21], (DEPTH, N_GROUPS, EXPERTS_PER_GROUP), 0.01),
        'w_gate': nrm(ks[22], (DEPTH, N_EXPERTS, D_MODEL, EXPERT_FF), D_MODEL ** -0.5),
        'w_up': nrm(ks[23], (DEPTH, N_EXPERTS, D_MODEL, EXPERT_FF), D_MODEL ** -0.5),
        'w_down': nrm(ks[24], (DEPTH, N_EXPERTS, EXPERT_FF, D_MODEL), EXPERT_FF ** -0.5),
        'norm_f_g': 1.0 + nrm(ks[25], (D_MODEL,), 0.05),
    }

def reference(x_prompt, x_sample, cache_k, cache_v, state_gla, page_table,
              norm1_g, w_in, w_a2, b_a, gla_norm_g, lambda_q1, lambda_k1, lambda_q2, lambda_k2,
              diff_norm_g, w_out, norm2_g, w_router_g, b_router_g, w_router_e, b_router_e,
              w_gate, w_up, w_down, norm_f_g):
    dec_b, n_pages = page_table.shape
    page = cache_k.shape[2]
    past_len = n_pages * page
    xp, xs = x_prompt, x_sample
    kp_l, vp_l, sp_l, ks_l, vs_l, ss_l = [], [], [], [], [], []
    for l in range(DEPTH):
        lam_init = 0.8 - 0.6 * math.exp(-0.3 * l)
        lam = (jnp.exp(jnp.sum((lambda_q1[l] * lambda_k1[l]).astype(jnp.float32)))
               - jnp.exp(jnp.sum((lambda_q2[l] * lambda_k2[l]).astype(jnp.float32))) + lam_init)
        p = (norm1_g[l], w_in[l], w_a2[l], b_a[l], gla_norm_g[l], diff_norm_g[l], w_out[l], norm2_g[l],
             w_router_g[l], b_router_g[l], w_router_e[l], b_router_e[l], w_gate[l], w_up[l], w_down[l])
        s0 = jnp.zeros((xp.shape[0], GLA_HEADS, GLA_DK, GLA_DV), xp.dtype)
        xp, kp, vp, sp = hybrid_layer(xp, p, lam, lam_init, s0, None, None)
        past_k = cache_k[l, page_table].reshape(dec_b, past_len, DIFF_HEADS, 2 * DIFF_HEAD_DIM)
        past_v = cache_v[l, page_table].reshape(dec_b, past_len, DIFF_HEADS, DIFF_V_DIM)
        xs, ks_, vs_, ss = hybrid_layer(xs, p, lam, lam_init, state_gla[l], past_k, past_v)
        kp_l.append(kp); vp_l.append(vp); sp_l.append(sp)
        ks_l.append(ks_); vs_l.append(vs_); ss_l.append(ss)
    y_prompt = rmsnorm(xp, norm_f_g)
    y_sample = rmsnorm(xs, norm_f_g)
    k_prompt = jnp.stack(kp_l, axis=0)
    v_prompt = jnp.stack(vp_l, axis=0)
    gla_prompt = jnp.stack(sp_l, axis=0)
    k_sample = jnp.stack(ks_l, axis=0)
    v_sample = jnp.stack(vs_l, axis=0)
    gla_sample = jnp.stack(ss_l, axis=0)
    return (y_prompt, y_sample, k_prompt, v_prompt, gla_prompt, k_sample, v_sample, gla_sample)


_drawn_inputs = setup_inputs


def setup_inputs(seed=0):
    import zlib

    import numpy as np

    out = dict(_drawn_inputs(seed))
    spreads = {}
    factors = {'b_router_g': 4.384, 'b_router_e': 5.61}
    for name, (base, spread) in spreads.items():
        noise = np.random.default_rng([zlib.crc32(name.encode()), seed]).standard_normal(out[name].shape)
        drawn = base * np.exp(spread * noise) if base else spread * noise
        out[name] = __import__('jax').numpy.asarray(drawn.astype(out[name].dtype))
    for name, factor in factors.items():
        out[name] = (out[name] * factor).astype(out[name].dtype)
    return out
```

```python
import math
from contextlib import ExitStack

import concourse.bass as bass
from concourse import mybir

F32 = mybir.dt.float32
F16 = mybir.dt.float16
I32 = mybir.dt.int32
ALU = mybir.AluOpType
ACT = mybir.ActivationFunctionType
AX = mybir.AxisListType.X

P = 128
D = 1024
KC = D // P
SEQ = 1024
NB = 8
T = SEQ + NB
NT = SEQ // P
H = 4
DK, DV = 64, 128
RANK = 16
PAST = 1024
PAGE = 128
NPG = PAST // PAGE
CH = 344
NG, EPG, NE = 4, 4, 16
FF = 256
CAP = 208
CAP1 = CAP - P
NOV = 16
COLS = 2 * NE + NOV
SC = 64.0
ISC2 = 1.0 / (SC * SC)
EPS = 1e-6
TAU = 16.0
LAM_INIT = 0.8 - 0.6 * math.exp(-0.3 * 0)
NEG = -1e30

GQK, CODE, GV, GR, DQ, DKG, DVG = range(7)
GROUPS = [("T", 0, 512), ("T", 1536, RANK), ("N", 512, 512), ("N", 1024, 512),
          ("T", 1552, 512), ("T", 2064, 512), ("N", 2576, 512)]
HALVES = []
for g, (_, c0, w) in enumerate(GROUPS):
    for o in range(0, w, 256):
        HALVES.append((g, c0 + o, min(256, w - o), o))
HALVES_TO = [max(i for i, h in enumerate(HALVES) if h[0] <= g) + 1 for g in range(len(GROUPS))]


def rows(t):
    return P if t < NT else NB


def span(t):
    return slice(t * P, t * P + rows(t))


def proj_units():
    units = []
    for g, (kind, _, w) in enumerate(GROUPS):
        if kind == "T":
            units += [(g, c, j) for c in range(max(1, w // P)) for j in range(3)]
        else:
            units += [(g, t, 0) for t in range(NT + 1)]
    return units


UNITS = proj_units()
UNIT_AT = {u: i for i, u in enumerate(UNITS)}
UNITS_TO = [sum(1 for u in UNITS if u[0] <= g) for g in range(len(GROUPS))]
DEC = {n: i + 1 for i, n in enumerate(("max", "exp_in", "sums", "new_weights", "new_weights_spread", "out",
                                      "normed"))}
OV_ACT = {n: i + 1 for i, n in enumerate(("weights_hi", "tokens_hi", "exp", "hidden_hi", "y"))}
OV_VEC = {n: i + 1 for i, n in enumerate(("weights_lo", "tokens_lo", "plus_one", "sigmoid", "silu", "hidden",
                                          "hidden_lo", "y"))}
OV_PE = {n: i + 1 for i, n in enumerate(("tokens", "gate_up", "down"))}
MIXED = NT + 1
N_PAR = 3 + 1 + 4 + 1 + NG + 3
X_GROUP = [(0, 1)] + [(1, 2)] * 2 + [(2, 3)] * 3 + [(3, 3)] * 3
PB = 4


def build(nc, I, O):
    ctx = ExitStack()
    with ctx:
        def sb(name, shape, dt=F32):
            return ctx.enter_context(nc.sbuf_tensor(name, shape, dt))

        def sem(name):
            return ctx.enter_context(nc.semaphore(name))

        ps = ctx.enter_context(nc.psum_tensor("ps", [P, 8, 512], F32))

        hT_reg = sb("hT_reg", [P, 8 * T])
        mix_reg = sb("mix_reg", [P, 8 * T])
        w_reg = sb("w_reg", [P, 2 * 2048 + 2 * 4096])
        dg_reg = sb("dg_reg", [P, 8 * T + 9 * 512])

        hTh = hT_reg[:, 0:4 * T].bitcast(F16).rearrange("p (k t) -> p k t", k=KC)
        hTl = hT_reg[:, 4 * T:8 * T].bitcast(F16).rearrange("p (k t) -> p k t", k=KC)
        xin = mix_reg[:, 0:NT * D].rearrange("p (t d) -> p t d", t=NT)
        mixh = mix_reg[:, 0:4 * T].bitcast(F16).rearrange("p (k t) -> p k t", k=KC)
        mixl = mix_reg[:, 4 * T:8 * T].bitcast(F16).rearrange("p (k t) -> p k t", k=KC)
        stage = [w_reg[:, 2048 * s:2048 * (s + 1)] for s in range(2)]
        slot_h = [w_reg[:, 4096 * (s + 1):4096 * (s + 1) + 2048].bitcast(F16).rearrange(
            "p (k n) -> p k n", k=KC) for s in range(2)]
        slot_l = [w_reg[:, 4096 * (s + 1) + 2048:4096 * (s + 2)].bitcast(F16).rearrange(
            "p (k n) -> p k n", k=KC) for s in range(2)]
        qdh, qdl, kdh, kdl = [dg_reg[:, 2 * T * i:2 * T * (i + 1)].bitcast(F16).rearrange(
            "p (h t) -> p h t", h=H) for i in range(4)]
        vd = dg_reg[:, 8 * T:].rearrange("p (t c) -> p t c", t=9)
        gq = dg_reg[:, 0:2 * T].rearrange("p (a t) -> p a t", a=2)
        gk = dg_reg[:, 2 * T:4 * T].rearrange("p (a t) -> p a t", a=2)
        gv = dg_reg[:, 4 * T:4 * T + 4608].rearrange("p (t c) -> p t c", t=9)
        o = 4 * T + 4608
        ea = dg_reg[:, o:o + 1024]
        qmask = dg_reg[:, o:o + 256].rearrange("p (a h b c) -> p a h b c", a=2, h=2, b=NB)
        ek = dg_reg[:, o + 1024:o + 2048]
        ed = dg_reg[:, o + 2048:o + 3072]
        eb = dg_reg[:, o + 3072:o + 3584]
        bc = mix_reg[:, 0:T]
        la = mix_reg[:, T:2 * T]
        qs = la
        es = mix_reg[:, 2 * T:3 * T]
        qa = mix_reg[:, 3 * T:3 * T + 2048].rearrange("p (c h i) -> p c h i", c=8, h=2)
        qb = mix_reg[:, 3 * T + 2048:3 * T + 3072].rearrange("p (c h i) -> p c h i", c=8, h=2)
        kmask = mix_reg[0:NB, 3 * T:3 * T + 2048].rearrange("p (b c) -> p b c", b=NB)
        st = mix_reg[:, 6 * T:6 * T + 2048].rearrange("p (a b v) -> p a b v", a=2, b=NB)
        code = mix_reg[0:RANK, 6 * T:7 * T]

        ident = sb("ident", [P, P])
        ident16 = sb("ident16", [P, P], F16)
        maskneg = sb("maskneg", [P, P])
        mask_ji = sb("mask_ji", [P, P])
        ones = sb("ones", [P, P])
        gbc = sb("gbc", [P, D])
        ba_col = sb("ba_col", [P, 2])
        glag = sb("glag", [P, DV])
        wa2 = sb("wa2", [RANK, 2 * P])
        gs_reg = sb("gs_reg", [P, 1280])
        sbd = gs_reg[:, 0:512].rearrange("p (a h v) -> p a h v", a=2, h=2)
        scb = gs_reg[:, 512:1024].rearrange("p (s h i) -> p s h i", s=2, h=2)
        kdn = gs_reg[:, 1024:1280].rearrange("p (s c) -> p s c", s=2)
        diagm = sb("diagm", [P, 2, NB, NB])
        junk = sb("junk", [P, D])
        ss = sb("ss", [P, 40])
        rst = sb("rst", [P, 40])
        a_s = sb("a_s", [P, 2, NB])
        gt = sb("gt", [P, 2, 512])
        knat = junk[:].rearrange("p (s c) -> p s c", s=2)
        xs = gt[0:NB].rearrange("p s c -> p (s c)")
        neghalf = sb("neghalf", [P, 40])

        prob = hT_reg[:, 0:4096].rearrange("p (s m n) -> p s m n", s=2, m=2)
        wT = hT_reg[:, 4096:6144].rearrange("p (s j q) -> p s j q", s=2, j=NT)
        qbc = hT_reg[:, 6144:7168].rearrange("p (s c) -> p s c", s=2)
        kv = sb("kv", [P, 2, 2048])
        dgain = sb("dgain", [P, DV])
        lams = kv[:, 0, 0:4 * DK].rearrange("p (i d) -> p i d", i=4)
        lamw = sb("lamw", [P, 8])
        nlam = lamw[:, 4:5]
        mxn = sb("mxn", [P, 2, 2])
        rsum = sb("rsum", [P, 3, H, 2])
        rinv = sb("rinv", [P, 3, H, 2])
        comb = sb("comb", [P, 4])
        comb4 = sb("comb4", [P, 2, H])
        qn = gt[0:NB, 0]
        snew = sb("snew", [NB, 8])
        dsc = hT_reg[:, 7168:7744].rearrange("p (b m g) -> p b m g", b=NB, m=8)
        dw = dg_reg[:, 9 * D:9 * D + 288].rearrange("p (b h g) -> p b h g", b=NB, h=H)
        dmx = sb("dmx", [P, NB * 8])
        dmb = sb("dmb", [P, NB * 8])
        wz = gs_reg[:, 0:576].rearrange("p (s g w) -> p s g w", s=2, g=NPG + 1)
        wn = sb("wn", [NB, H])
        wnz = sb("wnz", [NB, NB, H])
        ptab = sb("ptab", [1, NB * NPG], I32)
        dmask = gs_reg[0:4 * NB, 640:1152].rearrange("p (h v) -> p h v", h=H)
        dod = sb("dod", [4 * NB, DV])
        xr = hT_reg[:, 0:2048].rearrange("p (s d) -> p s d", s=2)
        h2 = hT_reg[:, 2048:4096].rearrange("p (s d) -> p s d", s=2)
        h2s = hT_reg[:, 4096:6144].bitcast(F16).rearrange("p (s d) -> p s d", s=2)
        h2T = hT_reg[:, 6144:8192].bitcast(F16).rearrange("p (s l k t) -> p s l k t", s=2, l=2, k=KC)
        x1 = dg_reg[:, 0:9 * D].rearrange("p (t d) -> p t d", t=9)
        woh = w_reg[:, 4096:8192].bitcast(F16).rearrange("p (k n) -> p k n", k=KC)
        wol = w_reg[:, 8192:12288].bitcast(F16).rearrange("p (k n) -> p k n", k=KC)
        wr = sb("wr", [P, KC, NG + NE])
        wrh = sb("wrh", [P, KC, NG + NE], F16)
        wrl = sb("wrl", [P, KC, NG + NE], F16)
        br = sb("br", [P, NG + NE])
        lg = sb("lg", [P, 9, NG + NE])
        gates = sb("gates", [P, 2, 9])
        ogates = sb("ogates", [P, 2, 9])
        yrow = sb("yrow", [P, 2, 9], I32)
        orow = sb("orow", [P, 2, 9], I32)
        tok = sb("tok", [P, COLS], I32)
        oexp = sb("oexp", [1, NOV + 1], I32)
        iof = sb("iof", [P, P])
        tokid = sb("tokid", [P, 9])
        strict = sb("strict", [P, P])
        mst = [w_reg[:, 6144 * i:6144 * (i + 1)] for i in range(2)]
        f16 = lambda ap: ap.bitcast(F16)
        gu = [[mix_reg[:, 0:1024], mix_reg[:, 1024:2048], mix_reg[:, 2048:3072], mix_reg[:, 3072:4096],
               mix_reg[:, 4096:5120], mix_reg[:, 5120:6144]],
              [mix_reg[:, 6144:7168], mix_reg[:, 7168:8192], dg_reg[:, 9216:10240], dg_reg[:, 10240:11264],
               dg_reg[:, 11264:12288], gs_reg[:, 0:1024]]]
        egh, egl, euh, eul = [[f16(gu[i][j]).rearrange("p (k f) -> p k f", k=KC) for i in range(2)]
                              for j in range(4)]
        edh, edl = [[f16(gu[i][j]).rearrange("p (k f) -> p k f", k=2) for i in range(2)] for j in (4, 5)]
        xg = hT_reg[:, 0:4096].bitcast(F16).rearrange("p (s g c) -> p s g c", s=2, g=2)
        xT = hT_reg[:, 4096:4096 + 2 * KC * CAP].bitcast(F16).rearrange("p (s l k t) -> p s l k t", s=2, l=2, k=KC)
        yb = kv
        eg = junk[:, 0:2 * CAP]
        hid = junk[:, 2 * CAP:4 * CAP]
        hidh = gt[:, 0, 0:2 * CAP].bitcast(F16).rearrange("p (s f t) -> p s f t", s=2, f=2)
        hidl = gt[:, 1, 0:2 * CAP].bitcast(F16).rearrange("p (s f t) -> p s f t", s=2, f=2)
        gt2 = gt[:].rearrange("p s c -> p (s c)")
        ovxT = xT[:, 0, :, :, 0:P]
        ovhh, ovhl = [v[:, 0, :, 0:P] for v in (hidh, hidl)]
        ove, ovhid = eg[:, 0:2 * P], hid[:, 0:2 * P]
        yg = mix_reg[:, 0:4096].rearrange("p (s c d) -> p s c d", s=2, c=2)
        fin = mix_reg[:, 4096:6144].rearrange("p (s d) -> p s d", s=2)

        def xt(t):
            return xin[:, t, :] if t < NT else xs

        s_x = [sem(f"x_in{i}") for i in range(4)]
        s_g1 = sem("gains_in")
        s_par = sem("parameters_in")
        s_const = sem("consts")
        s_dv = sem("vector_chain")
        s_ac = sem("scalar_chain")
        s_pl = sem("pool_chain")
        s_ss = sem("x_then_gla_squares")
        s_ms = sem("mean_squares")
        s_rs = sem("rstds")
        s_xn = sem("x_normed")
        s_xT = sem("x_transposed")
        s_hh = sem("h_hi")
        s_hl = sem("h_lo")
        s_w = [sem(f"w_stage{i}") for i in range(2)]
        s_wh = sem("w_hi")
        s_wl = sem("w_lo")
        s_mm = sem("proj_unit")
        s_ev = [sem(f"proj_bank_free{i}") for i in range(PB)]
        s_hi = sem("proj_hi")
        s_z = sem("gla_z")
        s_zr = sem("gla_z_read")
        s_ln = sem("gla_ln")
        s_arg = sem("gla_args")
        s_qz = sem("gla_q_zeroed")
        s_exp = sem("gla_exps")
        s_prep = sem("gla_operands")
        s_sc = sem("gla_scores")
        s_scm = sem("gla_scores_masked")
        s_kdn = sem("gla_k_natural")
        s_o = sem("gla_out")
        s_S = sem("gla_state")
        s_oev = sem("gla_out_read")
        s_st = sem("state_in")
        s_ks = sem("gla_sample_k_then_out")
        s_km = sem("gla_sample_kmask")
        s_op = sem("gla_sample_outer")
        s_sn = sem("gla_sample_state")
        s_osr = sem("gla_sample_out_read")
        s_ge = sem("gate_exp")
        s_mx = sem("gla_mixed")
        s_mT = sem("mix_transposed")
        s_mh = sem("mix_hi")
        s_ml = sem("mix_lo")
        s_kn = sem("k_natural")
        s_knr = sem("k_natural_read")
        s_kout = [sem(f"k_out{i}") for i in range(2)]
        s_out = sem("outputs")

        s_ldot = sem("lambda_dots")
        s_lexp = sem("lambda_exps")
        s_spout = sem("state_prompt_out")
        s_qd = sem("q_scratch_out")
        s_snew = sem("new_key_scores")
        s_snin = sem("new_key_scores_placed")
        s_qb = [sem(f"q_broadcast_in{i}") for i in range(2)]
        s_kp = [sem(f"pages_in{i}") for i in range(2)]
        s_kh = sem("page_scores")
        s_qk = sem("scores")
        s_nm = sem("scores_max")
        s_p = sem("probs")
        s_wc = sem("probs_combined")
        s_wT = sem("probs_transposed")
        s_wTe = sem("probs_transposed_read")
        s_pv = sem("attn_out")
        s_dsq = sem("attn_squares")
        s_dn = sem("attn_normed")
        s_dsz = sem("decode_scores_cleared")
        s_wrs = sem("router_split")
        s_s1 = sem("gate_steps")
        s_wo = [sem(f"w_out_stage{i}") for i in range(2)]
        s_woh = sem("w_out_hi")
        s_wol = sem("w_out_lo")
        s_dec = sem("decode_vector_steps")
        s_deca = sem("decode_exp_and_square")
        s_mbb = sem("decode_max_all")
        s_dsa = sem("decode_sums_all")
        s_wni = sem("decode_new_weights_in")
        s_wz = sem("decode_weights")
        s_vp = [sem(f"v_pages_in{i}") for i in range(2)]
        s_pvd = sem("decode_pv")
        s_dmk = sem("decode_mask")
        s_xr = [sem(f"x_again{i}") for i in range(2)]
        s_om = sem("out_proj")
        s_x1 = sem("x_plus_mixer")
        s_x1q = sem("x1_squares")
        s_h2 = sem("h2_normed")
        s_h2h = sem("h2_hi")
        s_h2l = sem("h2_lo")
        s_h2o = [sem(f"h2_out{i}") for i in range(2)]
        s_h2T = sem("h2_transposed")
        s_hTh = sem("h2T_hi_read")
        s_hTl = sem("h2T_lo_read")
        s_rt = sem("router_products")
        s_rtr = sem("router_read")
        s_re = sem("route_exp_in")
        s_rex = sem("route_exp")
        s_rc = sem("route_counts")
        s_rs1 = sem("route_onehots")
        s_rsu = sem("route_onehots_used")
        s_rtk = sem("route_tokens")
        s_route = sem("routed")
        s_mw = [sem(f"expert_stage{i}") for i in range(2)]
        s_mh2 = sem("expert_hi")
        s_mfree = sem("expert_lo")
        s_gx = [sem(f"tokens_in{i}") for i in range(2)]
        s_eT = sem("tokens_transposed")
        s_ea = sem("tokens_read_act")
        s_ev2 = sem("tokens_read_vec")
        s_gup = sem("gate_up")
        s_sg = sem("gate_exp_moe")
        s_hf = sem("hidden")
        s_hh2 = sem("hidden_hi")
        s_hl2 = sem("hidden_lo")
        s_down = sem("down")
        s_ya = sem("y_read_act")
        s_yv = sem("y_read_vec")
        s_yo = [sem(f"y_out{i}") for i in range(2)]
        s_ovw = sem("overflow_weights_in")
        s_ovx = sem("overflow_tokens_in")
        s_ovy = sem("overflow_out")
        s_ova = sem("overflow_scalar_steps")
        s_ovv = sem("overflow_vector_steps")
        s_ovp = sem("overflow_tensor_steps")
        s_yg = [sem(f"y_gathered{i}") for i in range(2)]
        s_fq = sem("final_sum")
        s_fs = sem("final_square")
        s_fo = sem("final_normed")
        s_fout = [sem(f"final_out{i}") for i in range(2)]

        qd = nc.dram_tensor("q_scratch", [NB, 512], F32, kind="Internal").ap()
        h2d = nc.dram_tensor("h2_scratch", [T, 2 * D], F16, kind="Internal").ap()
        yd = nc.dram_tensor("y_scratch", [NE * CAP, D], F32, kind="Internal").ap()
        od = nc.dram_tensor("overflow_scratch", [NOV * P, D], F32, kind="Internal").ap()
        ck = I["cache_k"][0].rearrange("n p h e -> n p (h e)")
        cv = I["cache_v"][0].rearrange("n p h e -> n p (h e)")
        n_pool = I["cache_k"].shape[1]
        w_o = I["w_out"][0].rearrange("(k p) n -> p k n", p=P)

        UN = NT * H
        KHALF = NPG // 2

        def fills(u):
            return (u // H + 1 + 3) // 4

        FILL0 = [sum(fills(v) for v in range(u)) for u in range(UN + 1)]

        def score_bank(u, m):
            return 2 * (u % 2) + m if u < 16 else 2 * m

        def scores(u, m):
            n = (u // H + 1) * P
            b = score_bank(u, m)
            return ps[:, b:b + 2].rearrange("p b c -> p (b c)")[:, 0:n] if n > 512 else ps[:, b, 0:n]

        REQ = [("d", i) for i in range(NT)] + [("x", t) for t in range(NT)] + [("dec", 0), ("x", NT)] \
            + [("f", t) for t in range(NT + 1)]

        def rcol(kind, t):
            if kind == "d":
                return slice(0, P), slice(4 * t, 4 * t + 4)
            if kind == "dec":
                return slice(0, 4 * NB), slice(36, 37)
            c = {"x": 0, "f": 16}[kind] + t
            return slice(0, rows(t)), slice(c, c + 1)

        kvf = kv[:].rearrange("p s c -> p (s c)")
        taken = [0]

        def work(*shape):
            n = math.prod(shape)
            v = kvf[:, taken[0]:taken[0] + n]
            taken[0] += n
            if len(shape) == 2:
                v = v.rearrange("p (a b) -> p a b", a=shape[0])
            return v

        r_m, r_s, r_pt, r_mi, r_m1, r_m2, dd, r_tokv, r_valid = [work(9) for _ in range(9)]
        eg4, r_cand, ohg, r_le, oh1, oh2 = [work(9, 4) for _ in range(6)]
        r_prod = work(9, 16)
        cho = work(18, 16)
        r_tmp = work(18, 16)
        r_a, r_pos = work(9, 16), work(9, 16)
        r_ne, r_oc, r_inc, r_ost = [work(16) for _ in range(4)]
        r_thr = work(8)
        r_cmp = work(16, 8)
        r_cmj = work(NOV, 16)
        r_r, r_e, r_o, r_g, r_f, r_q, r_p, r_c, r_po, r_co, r_x, r_y = [work(18) for _ in range(12)]
        r_q3 = work(18, 8)
        oneh_p = work(2, P)
        oneh_c = work(2, 96)
        iom = work(4)
        r_oe = work(NOV + 1)

        def expert_parts(s, lo):
            dst = (egl, eul, edl) if lo else (egh, euh, edh)
            return [(dst[j][s], mst[s][:, 2048 * j:2048 * (j + 1)].rearrange("p (k f) -> p k f", k=2 if j == 2 else KC),
                     (egh, euh, edh)[j][s]) for j in range(3)]

        x_p = I["x_prompt"][0].rearrange("(t p) d -> t p d", p=P)
        x_s = I["x_sample"].rearrange("b l d -> (b l) d")
        w_in = I["w_in"][0].rearrange("(k p) n -> p k n", p=P)
        state = I["state_gla"][0].rearrange("b (a h) k v -> a (h k) b v", a=2)

        def w_stage(n):
            wd = HALVES[n][2]
            return stage[n % 2][:, 0:KC * wd].rearrange("p (k n) -> p k n", k=KC)

        def w_slot(sl, n):
            g, _, wd, off = HALVES[n]
            return sl[g % 2][:, :, off:off + wd]

        def bank16(b):
            return ps[:, b, :].bitcast(F16)

        def plain_target(g, blk, j):
            u = UNIT_AT[(g, blk, j)]
            if g == GQK:
                dst = (gq if blk < 2 else gk)[:, blk % 2, CH * j:CH * (j + 1)]
                return dst, ps[:, u % PB, 0:CH]
            if g == CODE:
                return code[:, CH * j:CH * (j + 1)], ps[0:RANK, u % PB, 0:CH]
            r = rows(blk)
            return {GV: gv, DVG: vd}[g][0:r, blk, :], ps[0:r, u % PB, :]

        def plain_scale(g, blk):
            return ISC2 * (DK ** -0.5 if g == GQK and blk < 2 else 1.0)

        def mix_hi(act, n, t, half):
            r = rows(t)
            act.wait_ge(s_mT, n + 1)
            act.activation(mixh[:, 4 * half:4 * half + 4, span(t)],
                           ps[:, 4 + n % 2, 0:4 * r].rearrange("p (k t) -> p k t", k=4),
                           ACT.Copy).then_inc(s_mh, 1)

        def mix_lo(dve, n, t, half):
            r = rows(t)
            ks = slice(4 * half, 4 * half + 4)
            dve.wait_ge(s_mh, n + 1)
            dve.tensor_tensor(mixl[:, ks, span(t)],
                              ps[:, 4 + n % 2, 0:4 * r].rearrange("p (k t) -> p k t", k=4),
                              mixh[:, ks, span(t)], ALU.subtract).then_inc(s_ml, 1)

        def attn_lo_on(dve, i):
            dve.wait_ge(s_mh, MIXED + i + 1)
            dve.tensor_tensor(mixl[:, 4:8, span(i)], ps[:, 6 + i % 2, :].rearrange("p (k t) -> p k t", k=4),
                              mixh[:, 4:8, span(i)], ALU.subtract).then_inc(s_ml, 1)

        def when_overflow(eng, body):
            eng.wait_ge(s_route, 1)
            eng.wait_ge(s_yo[0], 16 * NE)
            eng.wait_ge(s_yo[1], 16 * NE)
            tiles = eng.value_load(oexp[0:1, NOV:NOV + 1], min_val=0, max_val=NOV)
            with eng.If(tiles > 0):
                body()

        block = ctx.enter_context(nc.Block())

        @block.sync
        def _(sp):
            for t in range(NT + 1):
                sp.dma_start(xt(t), x_p[t] if t < NT else x_s).then_inc(s_x[X_GROUP[t][0]], 16)

            def load_half(n):
                if n >= 2:
                    sp.wait_ge(s_wl, n - 1)
                _, c0, wd, _ = HALVES[n]
                sp.dma_start(w_stage(n), w_in[:, :, c0:c0 + wd]).then_inc(s_w[n % 2], 16)

            for n in range(HALVES_TO[GR]):
                load_half(n)
            sp.wait_ge(s_z, 6)
            for a in range(2):
                sp.dma_start(st[:, a], state[a]).then_inc(s_st, 16)
            for n in range(HALVES_TO[GR], len(HALVES)):
                load_half(n)
            sp.wait_ge(s_S, 2 * NT)
            for h in range(H):
                hp = slice(64 * (h % 2), 64 * (h % 2) + 64)
                sp.dma_start(O["gla_prompt"][0, 0, h], sbd[hp, h // 2, h % 2, :]).then_inc(s_spout, 16)
            sp.wait_ge(s_sn, NB)
            for a in range(2):
                sp.dma_start(O["gla_sample"][0].rearrange("b (a h) k v -> a (h k) b v", a=2)[a],
                             st[:, a]).then_inc(s_out, 16)
            for t in range(NT + 1):
                u = UNIT_AT[(DVG, t, 0)]
                sp.wait_ge(s_ev[u % PB], u // PB + 1)
                dst = O["v_prompt"][0, 0, t * P:(t + 1) * P].rearrange("p h e -> p (h e)") if t < NT \
                    else O["v_sample"][0, :, 0].rearrange("b h e -> b (h e)")
                sp.dma_start(dst, vd[0:rows(t), t]).then_inc(s_out, 16)

            def pages(cache, n, sems):
                b, half = n // 2, n % 2
                for g in range(KHALF):
                    i = NPG * b + KHALF * half + g
                    page = sp.value_load(ptab[0:1, i:i + 1], min_val=0, max_val=n_pool - 1)
                    sp.dma_start(kv[:, n % 2, 512 * g:512 * g + 512],
                                 cache[bass.ds(page, 1)].rearrange("n p c -> p (n c)")).then_inc(sems[n % 2], 16)

            def load_wo(c):
                if c >= 2:
                    sp.wait_ge(s_wol, c - 1)
                else:
                    sp.wait_ge(s_wl, len(HALVES))
                sp.dma_start(stage[c % 2].rearrange("p (k n) -> p k n", k=2),
                             w_o[:, 2 * c:2 * c + 2]).then_inc(s_wo[c % 2], 16)

            sp.wait_ge(s_par, 16 * N_PAR)
            sp.wait_ge(s_qd, 16)
            sp.wait_ge(s_mm, len(UNITS))
            sp.wait_ge(s_ldot, 1)
            sp.wait_ge(s_dsz, 1)
            sp.wait_ge(s_snew, 1)
            with nc.allow_non_contiguous_dma(reason="64 scores"):
                sp.dma_start(dsc[0:1, :, :, NPG].rearrange("p b m -> p (b m)"), snew[:]).then_inc(s_snin, 16)
            for n in range(2 * NB):
                if n >= 2:
                    sp.wait_ge(s_kh, n - 1)
                if n % 2 == 0:
                    if n >= 4:
                        sp.wait_ge(s_kh, n - 2)
                    sp.dma_start(qbc[:, n // 2 % 2], qd[n // 2].partition_broadcast(P)).then_inc(s_qb[n // 2 % 2], 16)
                pages(ck, n, s_kp)
                if n == 2:
                    load_wo(0)
                    load_wo(1)
                if n in (9, 12):
                    load_wo(2 + (n == 12))
            sp.wait_ge(s_kh, 2 * NB)
            sp.wait_ge(s_wTe, FILL0[UN])
            sp.wait_ge(s_pv, UN)
            for t in range(NT + 3):
                if t <= NT:
                    if t >= 2:
                        sp.wait_ge(s_x1, 2 * (t - 1))
                    sp.dma_start(xr[0:rows(t), t % 2], x_p[t] if t < NT else x_s).then_inc(s_xr[t % 2], 16)
                if t >= 2:
                    v = t - 2
                    sp.wait_ge(s_h2h, v + 1)
                    sp.wait_ge(s_h2l, v + 1)
                    sp.dma_start(h2d[v * P:v * P + rows(v)], h2s[0:rows(v), v % 2]).then_inc(s_h2o[v % 2], 16)
                if t < NT:
                    for n in (2 * t, 2 * t + 1):
                        if n >= 2:
                            sp.wait_ge(s_pvd, n - 1)
                        pages(cv, n, s_vp)

            def load_expert(e, s, free):
                if free is not None:
                    sp.wait_ge(s_mfree, free)
                for j, w in enumerate((I["w_gate"], I["w_up"], I["w_down"])):
                    src = w[0, bass.ds(e, 1)].rearrange("e (k p) f -> p (e k) f", p=P)
                    sp.dma_start(mst[s][:, 2048 * j:2048 * (j + 1)].rearrange("p (k f) -> p k f", k=src.shape[1]),
                                 src).then_inc(s_mw[s], 16)

            def store_y(e, s, n_ya):
                sp.wait_ge(s_ya, n_ya)
                sp.wait_ge(s_yv, n_ya)
                for g, r in ((0, P), (1, CAP1)):
                    dst = yd[bass.ds(e * CAP + P * g, r)]
                    sp.dma_start(dst, yb[0:r, s, D * g:D * g + D]).then_inc(s_yo[s], 16)

            sp.wait_ge(s_om, 2 * (NT + 1))
            load_expert(0, 0, None)
            load_expert(1, 1, None)
            with sp.Fori(0, NE // 2 - 1) as i:
                for s in range(2):
                    load_expert(2 * i + (2 + s), s, 6 * i + (3 * s + 3))
                    store_y(2 * i + s, s, 2 * i + (s + 1))
            for s in range(2):
                store_y(NE - 2 + s, s, NE - 1 + s)
            def overflow():
                sp.wait_ge(s_ovv, 1)
                for j in range(NOV):
                    sp.dma_start(od[P * j:P * j + P], junk[:]).then_inc(s_ovy, 16)
                with sp.Fori(0, NOV) as j:
                    sp.wait_ge(s_ovy, 16 * j + 16 * NOV)
                    e = sp.value_load(oexp[0:1, bass.ds(j, 1)], min_val=0, max_val=NE - 1)
                    for i, w in enumerate((I["w_gate"], I["w_up"], I["w_down"])):
                        src = w[0, bass.ds(e, 1)].rearrange("e (k p) f -> p (e k) f", p=P)
                        sp.dma_start(mst[0][:, 2048 * i:2048 * (i + 1)].rearrange("p (k f) -> p k f", k=src.shape[1]),
                                     src).then_inc(s_ovw, 16)
                    sp.wait_ge(s_ova, len(OV_ACT) * j + OV_ACT["y"])
                    sp.wait_ge(s_ovv, len(OV_VEC) * j + (1 + OV_VEC["y"]))
                    sp.dma_start(od[bass.ds(j * P, P)], yb[:, 0, 0:D]).then_inc(s_ovy, 16)

            when_overflow(sp, overflow)
            for t in range(NT + 1):
                sp.wait_ge(s_fo, t + 1)
                dst = O["y_prompt"][0, t * P:(t + 1) * P] if t < NT else O["y_sample"].rearrange("b l d -> (b l) d")
                sp.dma_start(dst, fin[0:rows(t), t % 2]).then_inc(s_fout[t % 2], 16)
            sp.wait_ge(s_fout[0], 16 * 5)
            sp.wait_ge(s_fout[1], 16 * 4)
            sp.wait_ge(s_out, 16 * (NT + 3))
            sp.wait_ge(s_spout, 16 * H)

        @block.gpsimd
        def _(pool):
            chain = [0]

            def link(ins):
                chain[0] += 1
                ins.then_inc(s_pl, 1)
                pool.wait_ge(s_pl, chain[0])

            for m in (ident, maskneg, gs_reg, diagm):
                pool.memset(m[:], 0.0)
            pool.memset(mask_ji[:], 1.0)
            pool.memset(neghalf[:], -0.5)
            link(pool.memset(ones[:], 1.0))
            pool.affine_select(out=ident[:], in_=ident[:], compare_op=ALU.not_equal, fill=1.0, base=0,
                               pattern=[[-1, P]], channel_multiplier=1)
            pool.affine_select(out=maskneg[:], in_=maskneg[:], compare_op=ALU.is_ge, fill=NEG, base=0,
                               pattern=[[-1, P]], channel_multiplier=1)
            pool.affine_select(out=mask_ji[:], in_=mask_ji[:], compare_op=ALU.is_ge, fill=0.0, base=0,
                               pattern=[[1, P]], channel_multiplier=-1)
            pool.iota(iof[:], pattern=[[1, P]], base=0, channel_multiplier=0, allow_small_or_imprecise_dtypes=True)
            pool.iota(tokid[:], pattern=[[P, 9]], base=0, channel_multiplier=1, allow_small_or_imprecise_dtypes=True)
            pool.memset(lg[:], 0.0)
            pool.affine_select(out=diagm[:], in_=diagm[:], compare_op=ALU.not_equal, fill=1.0, base=0,
                               pattern=[[0, 2], [1, NB], [-1, NB]], channel_multiplier=0).then_inc(s_const, 1)
            for t in range(NT + 1):
                r = rows(t)
                pool.wait_ge(s_ms, t + 1)
                pool.tensor_tensor(rst[0:r, t:t + 1], rst[0:r, t:t + 1], neghalf[0:r, 0:1],
                                   ALU.pow).then_inc(s_rs, 1)
            pool.wait_ge(s_xT, NT + 1)
            pool.memset(qa, 0.0)
            pool.memset(qb, 0.0).then_inc(s_qz, 1)
            pool.wait_ge(s_ms, NT + 2)
            pool.tensor_tensor(rst[:, 0:32], rst[:, 0:32], neghalf[:, 0:32], ALU.pow).then_inc(s_rs, 1)
            pool.wait_ge(s_ms, NT + 3)
            pool.tensor_tensor(rst[0:NB, 32:36], rst[0:NB, 32:36], neghalf[0:NB, 32:36],
                               ALU.pow).then_inc(s_rs, 1)
            pool.wait_ge(s_spout, 16 * H)
            pool.wait_ge(s_o, 2 * NT)
            link(pool.memset(dmask, 0.0))
            for b in range(NB):
                ins = pool.affine_select(out=dmask, in_=dmask, compare_op=ALU.not_equal, fill=1.0, base=-4 * b,
                                         pattern=[[-1, H], [0, DV]], channel_multiplier=1)
                if b < NB - 1:
                    link(ins)
            ins.then_inc(s_dmk, 1)

            def power(kind, t):
                pool.wait_ge(s_ms, NT + 3 + REQ.index((kind, t)) + 1)
                pr, cr = rcol(kind, t)
                pool.tensor_tensor(rst[pr, cr], rst[pr, cr], neghalf[pr, cr], ALU.pow).then_inc(s_rs, 1)

            done = REQ.index(("x", NT - 1)) + 1
            for r in REQ[:NT]:
                power(*r)
            pool.wait_ge(s_dec, DEC["max"])
            pool.partition_all_reduce(dmb[:], dmx[:], P, bass.bass_isa.ReduceOp.max).then_inc(s_mbb, 1)
            for r in REQ[NT:REQ.index(("f", 0))]:
                power(*r)

            def gather(e):
                if e >= 2:
                    pool.wait_ge(s_eT, 4 * (e - 1))
                for g, r in ((0, P), (1, CAP1)):
                    pool.indirect_dma_start(out=xg[0:r, e % 2, g, :], out_offset=None, in_=h2d[:, :],
                                            in_offset=bass.IndirectOffsetOnAxis(ap=tok[0:r, 2 * e + g:2 * e + g + 1],
                                                                                axis=0)).then_inc(s_gx[e % 2], 16)

            pool.wait_ge(s_route, 1)
            pool.wait_ge(s_h2o[0], 16 * 5)
            pool.wait_ge(s_h2o[1], 16 * 4)
            for e in range(NE):
                gather(e)

            def overflow():
                for j in range(NOV):
                    pool.wait_ge(s_ovy, 16 * (NOV + j))
                    pool.indirect_dma_start(out=xg[:, 0, 0, :], out_offset=None, in_=h2d[:, :],
                                            in_offset=bass.IndirectOffsetOnAxis(
                                                ap=tok[:, 2 * NE + j:2 * NE + j + 1], axis=0)).then_inc(s_ovx, 16)
                pool.wait_ge(s_ovy, 32 * NOV)
                for t in range(NT + 1):
                    if t:
                        pool.wait_ge(s_ovv, 1 + len(OV_VEC) * NOV + 2 * t)
                    for c in range(2):
                        pool.indirect_dma_start(out=yg[0:rows(t), 0, c], out_offset=None, in_=od[:, :],
                                                in_offset=bass.IndirectOffsetOnAxis(ap=orow[0:rows(t), c, t:t + 1],
                                                                                    axis=0)).then_inc(s_ovx, 16)
                pool.wait_ge(s_ovv, 1 + len(OV_VEC) * NOV + 2 * (NT + 1))

            when_overflow(pool, overflow)

            def gather_y(t):
                if t >= 2:
                    pool.wait_ge(s_fq, t - 1)
                for c in range(2):
                    pool.indirect_dma_start(out=yg[0:rows(t), t % 2, c], out_offset=None, in_=yd[:, :],
                                            in_offset=bass.IndirectOffsetOnAxis(ap=yrow[0:rows(t), c, t:t + 1], axis=0)
                                            ).then_inc(s_yg[t % 2], 16)

            gather_y(0)
            for t in range(NT + 1):
                if t + 1 <= NT:
                    gather_y(t + 1)
                power("f", t)

        @block.scalar
        def _(act):
            chain = [0]

            def link(ins):
                chain[0] += 1
                ins.then_inc(s_ac, 1)
                act.wait_ge(s_ac, chain[0])

            with nc.allow_non_contiguous_dma(reason="small parameters"):
                act.dma_start(gbc[:], I["norm1_g"][0].partition_broadcast(P)).then_inc(s_g1, 16)
                act.dma_start(ba_col[:], I["b_a"][0].rearrange("(a p) -> p a", p=P)).then_inc(s_par, 16)
                act.dma_start(glag[:], I["gla_norm_g"][0].partition_broadcast(P)).then_inc(s_par, 16)
                act.dma_start(wa2[:], I["w_a2"][0]).then_inc(s_par, 16)
                act.dma_start(ptab[:], I["page_table"].rearrange("b g -> (b g)").unsqueeze(0)).then_inc(s_par, 16)
                for i, n in enumerate(("lambda_q1", "lambda_k1", "lambda_q2", "lambda_k2")):
                    act.dma_start(lams[:, i], I[n][0].partition_broadcast(P)).then_inc(s_par, 16)
                act.dma_start(dgain[:], I["diff_norm_g"][0].partition_broadcast(P)).then_inc(s_par, 16)
                act.dma_start(wr[:, :, 0:NG], I["w_router_g"][0].rearrange("(k p) g -> p k g", p=P)).then_inc(s_par, 16)
                for g in range(NG):
                    act.dma_start(wr[:, :, NG + EPG * g:NG + EPG * (g + 1)],
                                  I["w_router_e"][0, g].rearrange("(k p) e -> p k e", p=P)).then_inc(s_par, 16)
                act.dma_start(br[:, 0:NG], I["b_router_g"][0].partition_broadcast(P)).then_inc(s_par, 16)
                act.dma_start(br[:, NG:], I["b_router_e"][0].rearrange("g e -> (g e)").partition_broadcast(P)
                              ).then_inc(s_par, 16)

            for t in range(NT + 1):
                r = rows(t)
                act.wait_ge(s_x[X_GROUP[t][0]], 16 * X_GROUP[t][1])
                if t:
                    act.wait_ge(s_ss, t)
                act.activation(junk[0:r, :], xt(t)[0:r], ACT.Square, accum_out=ss[0:r, t:t + 1]).then_inc(s_ss, 1)

            def split_w(n):
                g = HALVES[n][0]
                if g >= 2:
                    act.wait_ge(s_mm, UNITS_TO[g - 2])
                act.wait_ge(s_w[n % 2], 16 * (n // 2 + 1))
                act.activation(w_slot(slot_h, n), w_stage(n), ACT.Copy, scale=SC).then_inc(s_wh, 1)

            def split_group(g):
                for n in range(HALVES_TO[g - 1] if g else 0, HALVES_TO[g]):
                    split_w(n)

            split_group(0)
            for t in range(NT + 1):
                r = rows(t)
                for b in range(2):
                    bank = 4 + 2 * (t % 2) + b
                    act.wait_ge(s_xT, t + 1)
                    act.activation(hTh[:, 4 * b:4 * b + 4, span(t)],
                                   ps[:, bank, 0:4 * r].rearrange("p (k t) -> p k t", k=4),
                                   ACT.Copy).then_inc(s_hh, 1)

            def read_proj(g, blk, j, out, in_, scale, **kw):
                u = UNIT_AT[(g, blk, j)]
                act.wait_ge(s_mm, u + 1)
                return act.activation(out, in_, ACT.Copy, scale=scale, **kw), u

            def plain_reads(g):
                kind, _, wd = GROUPS[g]
                for (gg, blk, j) in UNITS:
                    u = UNIT_AT[(gg, blk, j)]
                    if gg != g or u % 2:
                        continue
                    act.wait_ge(s_mm, u + 1)
                    act.activation(*plain_target(g, blk, j), ACT.Copy,
                                   scale=plain_scale(g, blk)).then_inc(s_ev[u % PB], 1)

            act.wait_ge(s_xn, NT + 1)
            act.dma_start(gbc[:], I["norm2_g"][0].partition_broadcast(P)).then_inc(s_g1, 16)
            act.wait_ge(s_ldot, 1)
            act.activation(lamw[:, 2:4], lamw[:, 0:2], ACT.Exp).then_inc(s_lexp, 1)
            split_group(1)
            plain_reads(GQK)
            split_group(2)
            plain_reads(CODE)
            split_group(3)
            plain_reads(GV)

            for p in range(2):
                act.wait_ge(s_zr, 3 * p + 3)
                if p:
                    act.wait_ge(s_S, NT)
                link(act.activation(es, la, ACT.Abs))
                link(act.activation(es, es, ACT.Exp, scale=-1.0))
                act.activation(es, es, ACT.Ln, bias=1.0).then_inc(s_ln, 1)
                for i, buf in enumerate((ea, ek, eb, ed)):
                    act.wait_ge(s_arg, 4 * p + i + 1)
                    act.activation(buf, buf, ACT.Exp, scale=1.0 / TAU).then_inc(s_exp, 1)
                act.activation(es, bc, ACT.Exp, scale=1.0 / TAU).then_inc(s_exp, 1)
                for c in range(NT + 1):
                    if c < NT:
                        n = p * NT + c
                        act.wait_ge(s_sc, n + 1)
                        if n >= 2:
                            act.wait_ge(s_o, n - 1)
                        act.activation(kdn[:, n % 2], ps[:, n % 2, 0:P], ACT.Copy).then_inc(s_kdn, 1)
                    if c >= 1:
                        n = p * NT + c - 1
                        act.wait_ge(s_o, n + 1)
                        act.activation(gv[:, c - 1, 256 * p:256 * p + 256], ps[:, 6 + n % 2, 0:256],
                                       ACT.Copy).then_inc(s_oev, 1)
            act.wait_ge(s_ks, 2)
            act.activation(gv[0:NB, NT, :], ps[0:NB, 4, :], ACT.Copy).then_inc(s_osr, 1)
            act.wait_ge(s_oev, 2 * NT)
            act.wait_ge(s_osr, 1)
            for t in range(NT + 1):
                r = rows(t)
                for h in range(H):
                    if t or h:
                        act.wait_ge(s_ss, NT + 1 + H * t + h)
                    act.activation(junk[0:r, 0:DV], gv[0:r, t, DV * h:DV * h + DV], ACT.Square,
                                   accum_out=ss[0:r, H * t + h:H * t + h + 1]).then_inc(s_ss, 1)
            split_group(4)
            for t in range(NT + 1):
                r = rows(t)
                u = UNIT_AT[(GR, t, 0)]
                act.wait_ge(s_mm, u + 1)
                if t >= 2:
                    act.wait_ge(s_mT, t - 1)
                act.activation(gt[0:r, t % 2], ps[0:r, u % PB, :], ACT.Exp, scale=-ISC2).then_inc(s_ge, 1)
                if t >= 1:
                    mix_hi(act, t - 1, t - 1, 0)
            mix_hi(act, NT, NT, 0)

            def split_reads(g, hi, prev):
                for blk in range(4):
                    for j in range(3):
                        u = UNIT_AT[(g, blk, j)]
                        act.wait_ge(s_mm, u + 1)
                        act.activation(hi[:, blk, CH * j:CH * (j + 1)], ps[:, u % PB, 0:CH], ACT.Copy,
                                       scale=SC * ISC2).then_inc(s_hi, 1)

            split_group(5)
            split_reads(DQ, qdh, 0)
            split_group(6)
            split_reads(DKG, kdh, 12)
            for t in range(NT + 1):
                r = rows(t)
                act.wait_ge(s_kn, t + 1)
                if t >= 2:
                    act.wait_ge(s_kout[t % 2], 16 * (t // 2))
                act.activation(knat[0:r, t % 2], ps[0:r, 4 + t % 4, :], ACT.Copy,
                               scale=1.0 / SC).then_inc(s_knr, 1)
                act.wait_ge(s_knr, t + 1)
                dst = O["k_prompt"][0, 0, t * P:(t + 1) * P].rearrange("p h e -> p (h e)") if t < NT \
                    else O["k_sample"][0, :, 0].rearrange("b h e -> b (h e)")
                act.dma_start(dst, knat[0:r, t % 2]).then_inc(s_kout[t % 2], 16)
            act.wait_ge(s_kn, NT + 2)
            act.activation(qn, ps[0:NB, 4 + (NT + 1) % 4, :], ACT.Copy, scale=1.0 / SC).then_inc(s_knr, 1)
            act.wait_ge(s_knr, NT + 2)
            act.dma_start(qd, qn).then_inc(s_qd, 16)
            plain_reads(DVG)
            act.wait_ge(s_kout[0], 16 * 5)
            act.wait_ge(s_kout[1], 16 * 4)
            act.wait_ge(s_qd, 16)
            act.wait_ge(s_snew, 1)

            def split_wo(c):
                act.wait_ge(s_wo[c % 2], 16 * (c // 2 + 1))
                act.activation(woh[:, 2 * c:2 * c + 2], stage[c % 2].rearrange("p (k n) -> p k n", k=2), ACT.Copy,
                               scale=SC).then_inc(s_woh, 1)

            for u in range(UN + 8):
                if u < UN:
                    i, h = u // H, u % H
                    n = (i + 1) * P
                    for m in range(2):
                        act.wait_ge(s_nm, 2 * u + m + 1)
                        if u >= 2 and m == 0:
                            act.wait_ge(s_wT, FILL0[u - 1])
                        act.activation(prob[:, u % 2, m, 0:n], scores(u, m), ACT.Exp, scale=DK ** -0.5 * ISC2,
                                       bias=mxn[:, u % 2, m:m + 1],
                                       accum_out=rsum[:, i % 3, h, m:m + 1]).then_inc(s_p, 1)
                if 1 <= u <= UN:
                    v = u - 1
                    i = v // H
                    for f in range(fills(v)):
                        w = min(4, i + 1 - 4 * f)
                        act.wait_ge(s_wT, FILL0[v] + f + 1)
                        if v >= 2 and f == 0:
                            act.wait_ge(s_pv, v - 1)
                        act.activation(wT[:, v % 2, 4 * f:4 * f + w], ps[:, 4 + (FILL0[v] + f) % 2, 0:P * w].rearrange(
                            "p (j q) -> p j q", j=w), ACT.Copy).then_inc(s_wTe, 1)
                if u in (8, 12, 21, 27):
                    split_wo({8: 0, 12: 1, 21: 2, 27: 3}[u])
                if u % H == 2 and u >= 6 and (u - 6) // H < NT:
                    i = (u - 6) // H
                    act.wait_ge(s_pv, H * (i + 1))
                    for h in range(H):
                        if i or h:
                            act.wait_ge(s_dsq, H * i + h)
                        act.activation(junk[:, 0:DV], ps[:, 6 + i % 2, DV * h:DV * h + DV], ACT.Square,
                                       scale=rinv[:, i % 3, h, 0:1], accum_out=ss[:, 4 * i + h:4 * i + h + 1]
                                       ).then_inc(s_dsq, 1)
                if u % H == 1 and u >= 9 and (u - 9) // H < NT:
                    i = (u - 9) // H
                    act.wait_ge(s_mT, MIXED + i + 1)
                    act.activation(mixh[:, 4:8, span(i)], ps[:, 6 + i % 2, :].rearrange("p (k t) -> p k t", k=4),
                                   ACT.Copy).then_inc(s_mh, 1)
            act.wait_ge(s_dec, DEC["exp_in"])
            act.activation(dsc, dsc, ACT.Exp, scale=DK ** -0.5).then_inc(s_deca, 1)
            act.wait_ge(s_dec, DEC["new_weights"])
            with nc.allow_non_contiguous_dma(reason="32 weights"):
                act.dma_start(wn[:], dmx[0:1, 0:4 * NB]).then_inc(s_wni, 16)
            for t in range(NT + 2):
                if t == NT:
                    act.wait_ge(s_dec, DEC["out"])
                    act.activation(junk[0:4 * NB, 0:DV], dod[:], ACT.Square, accum_out=ss[0:4 * NB, 36:37]
                                   ).then_inc(s_deca, 1)
                    act.wait_ge(s_mT, MIXED + NT + 1)
                    act.activation(mixh[:, 4:8, SEQ:T], ps[:, 7, 0:4 * NB].rearrange("p (b h) -> p h b", h=H),
                                   ACT.Copy).then_inc(s_mh, 1)
                if t <= NT:
                    r = rows(t)
                    act.wait_ge(s_x1, 2 * (t + 1))
                    if t == NT:
                        act.wait_ge(s_deca, 2)
                    elif t:
                        act.wait_ge(s_x1q, t)
                    else:
                        act.wait_ge(s_dsq, UN)
                    act.activation(junk[0:r], x1[0:r, t], ACT.Square, accum_out=ss[0:r, t:t + 1]).then_inc(s_x1q, 1)
                    act.wait_ge(s_h2, t + 1)
                    if t >= 2:
                        act.wait_ge(s_h2o[t % 2], 16 * (t // 2))
                        act.wait_ge(s_h2T, t - 1)
                    act.activation(h2s[0:r, t % 2, 0:D], h2[0:r, t % 2], ACT.Copy).then_inc(s_h2h, 1)
                if t >= 1:
                    v = t - 1
                    r = rows(v)
                    act.wait_ge(s_h2T, v + 1)
                    if v >= 2:
                        act.wait_ge(s_rt, v - 1)
                    act.activation(h2T[:, v % 2, 0, :, 0:r], bank16(4)[:, 0:8 * r].rearrange("p (k t) -> p k t", k=KC),
                                   ACT.Copy).then_inc(s_hTh, 1)
            act.wait_ge(s_h2, NT + 1)
            act.dma_start(gbc[:], I["norm_f_g"].partition_broadcast(P)).then_inc(s_g1, 16)
            for i in range(2):
                act.wait_ge(s_re, i + 1)
                act.activation(*((eg4, eg4) if i == 0 else (dd, dd)), ACT.Exp).then_inc(s_rex, 1)

            def split_expert(s, loaded):
                act.wait_ge(s_mw[s], loaded)
                for dst, src, _ in expert_parts(s, 0):
                    act.activation(dst, src, ACT.Copy, scale=SC).then_inc(s_mh2, 1)

            def read_tokens(s, f, n):
                act.wait_ge(s_eT, n)
                act.activation(xT[:, s, f // 2, 4 * (f % 2):4 * (f % 2) + 4],
                               bank16(0)[:, 0:4 * CAP].rearrange("p (k t) -> p k t", k=4), ACT.Copy).then_inc(s_ea, 1)

            def expert(i, s, first=False, last=False):
                def at(k, c):
                    return k * 2 * i + (k * s + c)

                act.wait_ge(s_gup, at(1, 1))
                act.activation(eg, ps[:, 2, 0:2 * CAP], ACT.Exp, scale=-ISC2).then_inc(s_sg, 1)
                if not (last and s):
                    read_tokens(1 - s, 0, at(4, 5))
                act.wait_ge(s_hf, at(1, 1))
                act.activation(hidh[:, s], hid.rearrange("p (f t) -> p f t", f=2), ACT.Copy).then_inc(s_hh2, 1)
                if not (last and s):
                    read_tokens(1 - s, 2, at(4, 7))
                if not first:
                    act.wait_ge(s_yo[s], 32 * i)
                act.wait_ge(s_down, at(4, 1))
                act.activation(yb[:, s, 0:512], ps[:, 4, :], ACT.Copy, scale=ISC2)
                act.wait_ge(s_down, at(4, 3))
                act.activation(yb[0:CAP1, s, D:D + 512], ps[0:CAP1, 6, :], ACT.Copy, scale=ISC2).then_inc(s_ya, 1)
                if not last:
                    act.wait_ge(s_down, at(4, 4))
                    split_expert(s, 48 * i + 96)

            split_expert(0, 48)
            split_expert(1, 48)
            read_tokens(0, 0, 1)
            read_tokens(0, 2, 3)
            for s in range(2):
                expert(0, s, first=True)
            with act.Fori(1, NE // 2 - 1) as i:
                for s in range(2):
                    expert(i, s)
            for s in range(2):
                expert(NE // 2 - 1, s, last=True)
            def overflow():
                with act.Fori(0, NOV) as j:
                    def v(n):
                        return len(OV_VEC) * j + (1 + OV_VEC[n])

                    def p(n):
                        return len(OV_PE) * j + OV_PE[n]

                    act.wait_ge(s_ovw, 48 * j + 48)
                    for dst, src, _ in expert_parts(0, 0):
                        ins = act.activation(dst, src, ACT.Copy, scale=SC)
                    ins.then_inc(s_ova, 1)
                    act.wait_ge(s_ovp, p("tokens"))
                    act.activation(ovxT[:, 0], bank16(0).rearrange("p (k t) -> p k t", k=KC), ACT.Copy).then_inc(s_ova, 1)
                    act.wait_ge(s_ovp, p("gate_up"))
                    act.activation(ove, ps[:, 2, 0:2 * P], ACT.Exp, scale=-ISC2).then_inc(s_ova, 1)
                    act.wait_ge(s_ovv, v("hidden"))
                    act.activation(ovhh, ovhid.rearrange("p (f t) -> p f t", f=2), ACT.Copy).then_inc(s_ova, 1)
                    act.wait_ge(s_ovp, p("down"))
                    act.activation(yb[:, 0, 0:512], ps[:, 4, :], ACT.Copy, scale=ISC2).then_inc(s_ova, 1)

            when_overflow(act, overflow)
            for t in range(NT + 1):
                act.wait_ge(s_fq, t + 1)
                if t:
                    act.wait_ge(s_fs, t)
                act.activation(gt2[0:rows(t)], x1[0:rows(t), t], ACT.Square,
                               accum_out=ss[0:rows(t), 16 + t:17 + t]).then_inc(s_fs, 1)

        @block.vector
        def _(dve):
            chain = [0]

            def link(ins):
                chain[0] += 1
                ins.then_inc(s_dv, 1)
                dve.wait_ge(s_dv, chain[0])

            dve.wait_ge(s_const, 1)
            dve.memset(diagm[64:P, 0], 0.0)
            dve.memset(diagm[0:64, 1], 0.0)
            dve.tensor_copy(ident16[:], ident[:]).then_inc(s_const, 1)
            dve.wait_ge(s_g1, 16)
            link(dve.tensor_scalar(gbc[:], gbc[:], SC, None, ALU.mult))
            for t in range(NT + 1):
                r = rows(t)
                dve.wait_ge(s_ss, t + 1)
                dve.tensor_scalar(rst[0:r, t:t + 1], ss[0:r, t:t + 1], 1.0 / D, EPS, ALU.mult,
                                  ALU.add).then_inc(s_ms, 1)

            def x_norm(t):
                r = rows(t)
                dve.wait_ge(s_rs, t + 1)
                dve.scalar_tensor_tensor(xt(t)[0:r], xt(t)[0:r], rst[0:r, t:t + 1], gbc[0:r, :], ALU.mult,
                                         ALU.mult).then_inc(s_xn, 1)

            def split_w(n):
                dve.wait_ge(s_wh, n + 1)
                dve.scalar_tensor_tensor(w_slot(slot_l, n), w_stage(n), SC, w_slot(slot_h, n), ALU.mult,
                                         ALU.subtract).then_inc(s_wl, 1)

            def split_group(g):
                for n in range(HALVES_TO[g - 1] if g else 0, HALVES_TO[g]):
                    split_w(n)

            x_norm(0)
            x_norm(1)
            split_group(0)
            dve.wait_ge(s_par, 16 * N_PAR)
            for i in range(2):
                ins = dve.tensor_tensor_reduce(kv[:, 1, DK * i:DK * i + DK], lams[:, 2 * i], lams[:, 2 * i + 1], 1.0, 0.0,
                                               ALU.mult, ALU.add, lamw[:, i:i + 1])
            ins.then_inc(s_ldot, 1)
            for t in range(NT + 1):
                r = rows(t)
                if t + 2 <= NT:
                    x_norm(t + 2)
                for b in range(2):
                    bank = 4 + 2 * (t % 2) + b
                    dve.wait_ge(s_hh, 2 * t + b + 1)
                    dve.tensor_tensor(hTl[:, 4 * b:4 * b + 4, span(t)],
                                      ps[:, bank, 0:4 * r].rearrange("p (k t) -> p k t", k=4),
                                      hTh[:, 4 * b:4 * b + 4, span(t)], ALU.subtract).then_inc(s_hl, 1)

            def plain_reads(g):
                for (gg, blk, j) in UNITS:
                    u = UNIT_AT[(gg, blk, j)]
                    if gg != g or u % 2 == 0:
                        continue
                    dve.wait_ge(s_mm, u + 1)
                    dve.tensor_scalar(*plain_target(g, blk, j), plain_scale(g, blk), None,
                                      ALU.mult).then_inc(s_ev[u % PB], 1)

            split_group(1)
            plain_reads(GQK)
            split_group(2)
            plain_reads(CODE)
            split_group(3)
            plain_reads(GV)

            def per_chunk(buf, n=P):
                return buf.rearrange("p (c i) -> p c i", c=NT)

            dve.wait_ge(s_par, 16 * N_PAR)
            for p in range(2):
                for j in range(3):
                    cs = slice(CH * j, CH * (j + 1))
                    dve.wait_ge(s_z, 3 * p + j + 1)
                    dve.tensor_scalar(la[:, cs], ps[:, 4 + j, 0:CH], ba_col[:, p:p + 1], None,
                                      ALU.add).then_inc(s_zr, 1)
                dve.wait_ge(s_ln, p + 1)
                dve.wait_ge(s_zr, 3 * p + 3)
                link(dve.scalar_tensor_tensor(la, la, 0.0, es, ALU.min, ALU.subtract))
                for c in range(NT):
                    dve.tensor_tensor_scan(bc[:, span(c)], ones[:], la[:, span(c)], 0.0, ALU.mult, ALU.add)
                link(dve.tensor_copy(bc[:, SEQ:T], la[:, SEQ:T]))
                b3 = per_chunk(bc[:, 0:SEQ])
                m0 = b3[:, :, 31:32]
                m1 = b3[:, :, 95:96]
                last = b3[:, :, 127:128]
                k3 = per_chunk(ek)
                dve.tensor_tensor(per_chunk(ea), b3, m0.to_broadcast([P, NT, P]), ALU.subtract).then_inc(s_arg, 1)
                dve.tensor_tensor(k3[:, :, 0:64], m0.to_broadcast([P, NT, 64]), b3[:, :, 0:64], ALU.subtract)
                dve.tensor_tensor(k3[:, :, 64:P], m1.to_broadcast([P, NT, 64]), b3[:, :, 64:P],
                                  ALU.subtract).then_inc(s_arg, 1)
                dve.tensor_tensor(per_chunk(eb), b3[:, :, 64:P], m1.to_broadcast([P, NT, 64]),
                                  ALU.subtract).then_inc(s_arg, 1)
                dve.tensor_tensor(per_chunk(ed), last.to_broadcast([P, NT, P]), b3, ALU.subtract).then_inc(s_arg, 1)
                q3 = per_chunk(gq[:, p, 0:SEQ])
                dve.wait_ge(s_exp, 5 * p + 1)
                if p == 0:
                    dve.wait_ge(s_qz, 1)
                else:
                    dve.wait_ge(s_o, NT)
                for h in range(2):
                    hp = slice(64 * h, 64 * h + 64)
                    dve.tensor_tensor(qa[hp, :, h, :], q3[hp], per_chunk(ea)[hp], ALU.mult)
                dve.wait_ge(s_exp, 5 * p + 2)
                dve.tensor_tensor(ek, ek, gk[:, p, 0:SEQ], ALU.mult)
                dve.wait_ge(s_exp, 5 * p + 3)
                for h in range(2):
                    hp = slice(64 * h, 64 * h + 64)
                    dve.tensor_tensor(qb[hp, :, h, :], q3[hp, :, 64:P], per_chunk(eb)[hp], ALU.mult)
                dve.wait_ge(s_exp, 5 * p + 4)
                dve.tensor_tensor(ed, ed, gk[:, p, 0:SEQ], ALU.mult)
                dve.wait_ge(s_exp, 5 * p + 5)
                dve.tensor_copy(a_s[:, p], es[:, SEQ:T])
                dve.tensor_tensor(qs[:, 0:SEQ], gq[:, p, 0:SEQ], es[:, 0:SEQ], ALU.mult).then_inc(s_prep, 1)
                for c in range(NT + 1):
                    if c < NT:
                        n = p * NT + c
                        bank = 4 + n % 2
                        dve.wait_ge(s_sc, n + 1)
                        if n >= 2:
                            dve.wait_ge(s_o, n - 1)
                        dve.tensor_tensor(scb[0:64, n % 2], ps[0:64, bank, 0:256].rearrange("p (h i) -> p h i", h=2),
                                          mask_ji[0:64].unsqueeze(1).to_broadcast([64, 2, P]), ALU.mult)
                        dve.tensor_tensor(scb[64:P, n % 2, :, 64:P],
                                          ps[64:P, bank, 256:384].rearrange("p (h i) -> p h i", h=2),
                                          mask_ji[64:P, 64:P].unsqueeze(1).to_broadcast([64, 2, 64]),
                                          ALU.mult).then_inc(s_scm, 1)
                    if c >= 1:
                        n = p * NT + c - 1
                        dve.wait_ge(s_o, n + 1)
                        if c >= 2:
                            dve.wait_ge(s_S, n)
                        for h in range(2):
                            hp = slice(64 * h, 64 * h + 64)
                            ins = dve.scalar_tensor_tensor(
                                sbd[hp, p, h, :], sbd[hp, p, h, :], es[hp, P * c - 1:P * c],
                                ps[hp, 2 + n % 2, P * h:P * h + P], ALU.mult, ALU.add)
                        ins.then_inc(s_S, 1)
            dve.wait_ge(s_ks, 1)
            for p in range(2):
                dve.tensor_tensor(kmask[:, :, P * p:P * p + P],
                                  ps[0:NB, 4, P * p:P * p + P].unsqueeze(1).to_broadcast([NB, NB, P]),
                                  ident[0:NB, 0:NB].unsqueeze(2).to_broadcast([NB, NB, P]), ALU.mult)
            for p in range(2):
                ins = dve.tensor_tensor(
                    qmask[:, p], gq[:, p, SEQ:T].unsqueeze(1).unsqueeze(1).to_broadcast([P, 2, NB, NB]),
                    diagm[:], ALU.mult)
            ins.then_inc(s_km, 1)
            dve.wait_ge(s_st, 32)
            for m in range(2 * NB):
                p, b = m // NB, m % NB
                dve.wait_ge(s_op, m // 2 + 1)
                for h in range(2):
                    hp = slice(64 * h, 64 * h + 64)
                    ins = dve.scalar_tensor_tensor(
                        st[hp, p, b, :], st[hp, p, b, :], a_s[hp, p, b:b + 1],
                        ps[hp, 4 + m // 2 % 4, 256 * (m % 2) + P * h:256 * (m % 2) + P * h + P], ALU.mult, ALU.add)
                if m % 2:
                    ins.then_inc(s_sn, 1)
            dve.wait_ge(s_par, 16 * N_PAR)
            link(dve.tensor_scalar(glag[:], glag[:], SC, None, ALU.mult))
            dve.wait_ge(s_ss, NT + 1 + H * (NT + 1))
            dve.tensor_scalar(rst[:, 0:32], ss[:, 0:32], 1.0 / DV, EPS, ALU.mult, ALU.add).then_inc(s_ms, 1)
            dve.tensor_scalar(rst[0:NB, 32:36], ss[0:NB, 32:36], 1.0 / DV, EPS, ALU.mult, ALU.add).then_inc(s_ms, 1)
            split_group(4)
            for t in range(NT + 1):
                r = rows(t)
                u = UNIT_AT[(GR, t, 0)]
                g = gt[0:r, t % 2]
                g4 = g.rearrange("p (h v) -> p h v", h=H)
                dve.wait_ge(s_ge, t + 1)
                link(dve.tensor_scalar(g, g, 1.0, None, ALU.add))
                link(dve.reciprocal(g, g))
                ins = dve.scalar_tensor_tensor(g, ps[0:r, u % PB, :], ISC2, g, ALU.mult, ALU.mult)
                ins.then_inc(s_ev[u % PB], 1)
                dve.wait_ge(s_ev[u % PB], u // PB + 1)
                link(dve.tensor_tensor(g4, g4, glag[0:r].unsqueeze(1).to_broadcast([r, H, DV]), ALU.mult))
                if t == 0:
                    dve.wait_ge(s_rs, NT + 3)
                for h in range(H):
                    hs = slice(DV * h, DV * h + DV)
                    ins = dve.scalar_tensor_tensor(g[:, hs], gv[0:r, t, hs], rst[0:r, H * t + h:H * t + h + 1],
                                                   g[:, hs], ALU.mult, ALU.mult)
                ins.then_inc(s_mx, 1)
                if t >= 1:
                    mix_lo(dve, t - 1, t - 1, 0)
            mix_lo(dve, NT, NT, 0)

            def split_reads(g, hi, lo, prev):
                for blk in range(4):
                    for j in range(3):
                        u = UNIT_AT[(g, blk, j)]
                        cs = slice(CH * j, CH * (j + 1))
                        dve.wait_ge(s_hi, prev + 3 * blk + j + 1)
                        dve.scalar_tensor_tensor(lo[:, blk, cs], ps[:, u % PB, 0:CH], SC * ISC2, hi[:, blk, cs],
                                                 ALU.mult, ALU.subtract).then_inc(s_ev[u % PB], 1)

            split_group(5)
            split_reads(DQ, qdh, qdl, 0)
            split_group(6)
            split_reads(DKG, kdh, kdl, 12)
            dve.wait_ge(s_knr, NT + 2)
            qk = gt[0:NB, 1]
            link(dve.tensor_tensor(qk, qn, knat[0:NB, NT % 2], ALU.mult))
            dve.tensor_reduce(snew[:], qk.rearrange("p (m d) -> p m d", m=8), AX, ALU.add).then_inc(s_snew, 1)
            plain_reads(DVG)
            dve.wait_ge(s_mm, len(UNITS))
            dve.memset(dsc, NEG).then_inc(s_dsz, 1)
            dve.wait_ge(s_lexp, 1)
            link(dve.scalar_tensor_tensor(nlam, lamw[:, 3:4], -LAM_INIT, lamw[:, 2:3], ALU.add, ALU.subtract))
            dve.wait_ge(s_par, 16 * N_PAR)
            dve.wait_ge(s_g1, 32)
            link(dve.tensor_scalar(dgain[:], dgain[:], SC * (1.0 - LAM_INIT), None, ALU.mult))
            link(dve.tensor_scalar(gbc[:], gbc[:], SC, None, ALU.mult))

            def split_wo(c):
                dve.wait_ge(s_woh, c + 1)
                dve.scalar_tensor_tensor(wol[:, 2 * c:2 * c + 2], stage[c % 2].rearrange("p (k n) -> p k n", k=2), SC,
                                         woh[:, 2 * c:2 * c + 2], ALU.mult, ALU.subtract).then_inc(s_wol, 1)

            def normed(kind, t, n):
                pr, cr = rcol(kind, t)
                k = REQ.index((kind, t))
                dve.tensor_scalar(rst[pr, cr], ss[pr, cr], 1.0 / n, EPS, ALU.mult, ALU.add).then_inc(s_ms, 1)
                dve.wait_ge(s_rs, NT + 3 + k + 1)

            for u in range(UN + 8):
                if u < UN:
                    i = u // H
                    for m in range(2):
                        dve.wait_ge(s_qk, 2 * u + m + 1)
                        sc = scores(u, m)
                        link(dve.tensor_tensor(sc[:, P * i:P * i + P], sc[:, P * i:P * i + P], maskneg[:], ALU.add))
                        link(dve.tensor_reduce(comb[:, 2 + m:3 + m], sc, AX, ALU.max))
                        dve.tensor_scalar(mxn[:, u % 2, m:m + 1], comb[:, 2 + m:3 + m], -DK ** -0.5 * ISC2, None,
                                          ALU.mult).then_inc(s_nm, 1)
                if 1 <= u <= UN:
                    v = u - 1
                    i, h = v // H, v % H
                    n = (i + 1) * P
                    dve.wait_ge(s_p, 2 * v + 2)
                    link(dve.reciprocal(rinv[:, i % 3, h], rsum[:, i % 3, h]))
                    link(dve.scalar_tensor_tensor(comb[:, 0:1], rinv[:, i % 3, h, 1:2], rsum[:, i % 3, h, 0:1], nlam,
                                                  ALU.mult, ALU.mult))
                    dve.scalar_tensor_tensor(prob[:, v % 2, 0, 0:n], prob[:, v % 2, 1, 0:n], comb[:, 0:1],
                                             prob[:, v % 2, 0, 0:n], ALU.mult, ALU.add).then_inc(s_wc, 1)
                if u in (8, 12, 21, 27):
                    split_wo({8: 0, 12: 1, 21: 2, 27: 3}[u])
                if u % 2 == 1 and u < 4 * NB:
                    k = u // 2
                    b, half = k // 2, k % 2
                    pg = kv[:, k % 2].rearrange("p (g c) -> p g c", g=KHALF)
                    dve.wait_ge(s_kp[k % 2], 64 * (k // 2 + 1))
                    dve.wait_ge(s_qb[b % 2], 16 * (b // 2 + 1))
                    link(dve.tensor_tensor(pg, pg, qbc[:, b % 2].unsqueeze(1).to_broadcast([P, KHALF, 512]), ALU.mult))
                    dve.tensor_reduce(dsc[:, b, :, KHALF * half:KHALF * half + KHALF].rearrange("p m g -> p g m"),
                                      kv[:, k % 2].rearrange("p (g m d) -> p g m d", g=KHALF, m=8), AX,
                                      ALU.add).then_inc(s_kh, 1)
                if u % H == 3 and 7 <= u < UN + 7:
                    i = (u - 7) // H
                    dve.wait_ge(s_dsq, H * (i + 1))
                    normed("d", i, DV)
                    f = comb4[:, i % 2]
                    link(dve.tensor_tensor(f, rst[:, 4 * i:4 * i + 4], rinv[:, i % 3, :, 0], ALU.mult))
                    if i >= 2:
                        dve.wait_ge(s_mT, MIXED + i - 1)
                    for h in range(H):
                        hs = slice(DV * h, DV * h + DV)
                        ins = dve.scalar_tensor_tensor(gt[:, i % 2, hs], ps[:, 6 + i % 2, hs], f[:, h:h + 1], dgain[:],
                                                       ALU.mult, ALU.mult)
                    ins.then_inc(s_dn, 1)
                if u % H == 2 and 10 <= u < UN + 10:
                    i = (u - 10) // H
                    attn_lo_on(dve, i)
            dve.wait_ge(s_snin, 16)
            dve.wait_ge(s_kh, 2 * NB)
            d3 = dsc.rearrange("p b m g -> p (b m) g")
            dve.tensor_reduce(dmx[:], d3, AX, ALU.max).then_inc(s_dec, 1)
            dve.wait_ge(s_mbb, 1)
            dve.tensor_tensor(d3, d3, dmb[:].unsqueeze(2).to_broadcast([P, NB * 8, NPG + 1]),
                              ALU.subtract).then_inc(s_dec, 1)
            dve.wait_ge(s_deca, 1)
            dve.tensor_reduce(dmx[:], d3, AX, ALU.add).then_inc(s_dec, 1)
            dve.wait_ge(s_dsa, 1)
            link(dve.reciprocal(dmb[:], ps[:, 6, 0:NB * 8]))
            r2 = dmb[:].rearrange("p (b m) -> p b m", m=2)
            link(dve.tensor_scalar(r2[:, :, 1], r2[:, :, 1], nlam, None, ALU.mult))
            link(dve.tensor_tensor(d3, d3, dmb[:].unsqueeze(2).to_broadcast([P, NB * 8, NPG + 1]), ALU.mult))
            d4 = dsc.rearrange("p b (h m) g -> p (b h) m g", m=2)
            dve.wait_ge(s_pv, UN)
            link(dve.tensor_tensor(dw.rearrange("p b h g -> p (b h) g"), d4[:, :, 0, :], d4[:, :, 1, :], ALU.add))
            dve.tensor_copy(dmx[0:1, 0:4 * NB], dw[0:1, :, :, NPG].rearrange("p b h -> p (b h)")).then_inc(s_dec, 1)
            dve.wait_ge(s_wni, 16)
            dve.tensor_tensor(wnz[:], wn[:].unsqueeze(1).to_broadcast([NB, NB, H]),
                              ident[0:NB, 0:NB].unsqueeze(2).to_broadcast([NB, NB, H]), ALU.mult).then_inc(s_dec, 1)
            dve.wait_ge(s_par, 16 * N_PAR)
            link(dve.tensor_scalar(wrh[:], wr[:], SC, None, ALU.mult))
            dve.scalar_tensor_tensor(wrl[:], wr[:], SC, wrh[:], ALU.mult, ALU.subtract).then_inc(s_wrs, 1)
            dve.wait_ge(s_spout, 16 * H)
            for t in range(NT + 2):
                if t < NT:
                    if t >= 2:
                        dve.wait_ge(s_pvd, 2 * (t - 1))
                    link(dve.memset(wz[:, t % 2], 0.0))
                    dve.tensor_copy(wz[:, t % 2, :, H * t:H * t + H],
                                    dw[:, t].rearrange("p h g -> p g h")).then_inc(s_wz, 1)
                if t == NT:
                    dtmp = gs_reg[0:4 * NB, 0:512]
                    dve.wait_ge(s_pvd, 2 * NB + 1)
                    dve.wait_ge(s_dmk, 1)
                    link(dve.tensor_tensor(dtmp, ps[0:4 * NB, 7, :], dmask.rearrange("p h v -> p (h v)"), ALU.mult))
                    dve.tensor_reduce(dod[:], dtmp.rearrange("p (h v) -> p v h", h=H), AX, ALU.add).then_inc(s_dec, 1)
                    dve.wait_ge(s_deca, 2)
                    normed("dec", 0, DV)
                    dve.scalar_tensor_tensor(dod[:], dod[:], rst[0:4 * NB, 36:37], dgain[0:4 * NB], ALU.mult,
                                             ALU.mult).then_inc(s_dec, 1)
                    dve.wait_ge(s_mh, MIXED + NT + 1)
                    dve.tensor_tensor(mixl[:, 4:8, SEQ:T], ps[:, 7, 0:4 * NB].rearrange("p (b h) -> p h b", h=H),
                                      mixh[:, 4:8, SEQ:T], ALU.subtract).then_inc(s_ml, 1)
                if t <= NT:
                    r = rows(t)
                    dve.wait_ge(s_xr[t % 2], 16 * (t // 2 + 1))
                    for half in range(2):
                        cs = slice(512 * half, 512 * half + 512)
                        dve.wait_ge(s_om, 2 * t + half + 1)
                        dve.scalar_tensor_tensor(x1[0:r, t, cs], ps[0:r, 2 * (t % 2) + half, :], ISC2, xr[0:r, t % 2, cs],
                                                 ALU.mult, ALU.add).then_inc(s_x1, 1)
                    dve.wait_ge(s_x1q, t + 1)
                    normed("x", t, D)
                    dve.scalar_tensor_tensor(h2[0:r, t % 2], x1[0:r, t], rst[0:r, t:t + 1], gbc[0:r], ALU.mult,
                                             ALU.mult).then_inc(s_h2, 1)
                    if t >= 2:
                        dve.wait_ge(s_h2o[t % 2], 16 * (t // 2))
                        dve.wait_ge(s_h2T, t - 1)
                    dve.wait_ge(s_h2h, t + 1)
                    dve.tensor_tensor(h2s[0:r, t % 2, D:2 * D], h2[0:r, t % 2], h2s[0:r, t % 2, 0:D],
                                      ALU.subtract).then_inc(s_h2l, 1)
                if t >= 1:
                    v = t - 1
                    r = rows(v)
                    dve.wait_ge(s_h2T, v + 1)
                    if v >= 2:
                        dve.wait_ge(s_rt, v - 1)
                    dve.tensor_copy(h2T[:, v % 2, 1, :, 0:r],
                                    bank16(5)[:, 0:8 * r].rearrange("p (k t) -> p k t", k=KC)).then_inc(s_hTl, 1)
                    dve.wait_ge(s_rt, v + 1)
                    dve.scalar_tensor_tensor(lg[0:r, v], ps[0:r, 6, 0:NG + NE], ISC2, br[0:r], ALU.mult,
                                             ALU.add).then_inc(s_rtr, 1)
            dve.wait_ge(s_rtr, NT + 1)
            link(dve.tensor_scalar(iom, iof[:, 0:4], -64.0, None, ALU.add))

            def first_max(x, m, out):
                link(dve.tensor_tensor(r_cand, x, m.unsqueeze(2).to_broadcast([P, 9, 4]), ALU.is_ge))
                link(dve.tensor_tensor(r_cand, r_cand, iom.unsqueeze(1).to_broadcast([P, 9, 4]), ALU.mult))
                link(dve.tensor_reduce(r_mi, r_cand, AX, ALU.min))
                link(dve.tensor_tensor(out, r_cand, r_mi.unsqueeze(2).to_broadcast([P, 9, 4]), ALU.is_equal))

            lgg = lg[:, :, 0:NG]
            link(dve.tensor_reduce(r_m, lgg, AX, ALU.max))
            dve.tensor_tensor(eg4, lgg, r_m.unsqueeze(2).to_broadcast([P, 9, 4]), ALU.subtract).then_inc(s_re, 1)
            first_max(lgg, r_m, ohg)
            prod4 = r_prod.rearrange("p t (g e) -> p t g e", g=NG)
            link(dve.tensor_tensor(prod4, lg[:, :, NG:].rearrange("p t (g e) -> p t g e", g=NG),
                                   ohg.unsqueeze(3).to_broadcast([P, 9, NG, EPG]), ALU.mult))
            link(dve.tensor_reduce(r_le, r_prod.rearrange("p t (g e) -> p t e g", g=NG), AX, ALU.add))
            link(dve.tensor_reduce(r_m1, r_le, AX, ALU.max))
            first_max(r_le, r_m1, oh1)
            link(dve.scalar_tensor_tensor(r_le, oh1, NEG, r_le, ALU.mult, ALU.add))
            link(dve.tensor_reduce(r_m2, r_le, AX, ALU.max))
            dve.tensor_tensor(dd, r_m2, r_m1, ALU.subtract).then_inc(s_re, 1)
            first_max(r_le, r_m2, oh2)
            link(dve.tensor_scalar(r_valid, tokid[:], float(T), None, ALU.is_lt))
            link(dve.tensor_tensor(ohg, ohg, r_valid.unsqueeze(2).to_broadcast([P, 9, 4]), ALU.mult))
            for c, oh in enumerate((oh1, oh2)):
                link(dve.tensor_tensor(cho[:, 9 * c:9 * c + 9].rearrange("p t (g e) -> p t g e", g=NG),
                                       ohg.unsqueeze(3).to_broadcast([P, 9, NG, EPG]),
                                       oh.unsqueeze(2).to_broadcast([P, 9, NG, EPG]), ALU.mult))
            link(dve.tensor_tensor(strict[:], mask_ji[:], ident[:], ALU.subtract))
            dve.tensor_tensor(r_a, cho[:, 0:9], cho[:, 9:18], ALU.add).then_inc(s_re, 1)
            dve.wait_ge(s_rex, 2)
            link(dve.tensor_reduce(r_s, eg4, AX, ALU.add))
            link(dve.reciprocal(r_pt, r_s))
            link(dve.tensor_scalar(r_s, dd, 1.0, None, ALU.add))
            link(dve.reciprocal(r_s, r_s))
            link(dve.tensor_tensor(gates[:, 0], r_s, r_pt, ALU.mult))
            link(dve.tensor_tensor(gates[:, 1], gates[:, 0], dd, ALU.mult))
            dve.wait_ge(s_rc, 1)
            link(dve.tensor_copy(r_pos, ps[:, 0, 0:144].rearrange("p (t e) -> p t e", t=9)))
            link(dve.memset(r_ne, 0.0))
            for t in range(NT + 1):
                link(dve.tensor_tensor(r_pos[:, t], r_pos[:, t], r_ne, ALU.add))
                link(dve.tensor_tensor(r_ne, r_ne, ps[:, 1, 16 * t:16 * t + 16], ALU.add))
            link(dve.tensor_scalar(r_thr, iof[:, 0:8], float(P), float(CAP), ALU.mult, ALU.add))
            link(dve.tensor_tensor(r_cmp, r_ne.unsqueeze(2).to_broadcast([P, 16, 8]),
                                   r_thr.unsqueeze(1).to_broadcast([P, 16, 8]), ALU.is_gt))
            link(dve.tensor_reduce(r_oc, r_cmp, AX, ALU.add))
            link(dve.tensor_tensor_scan(r_inc, ones[:, 0:16], r_oc, 0.0, ALU.mult, ALU.add))
            link(dve.tensor_tensor(r_ost, r_inc, r_oc, ALU.subtract))
            for dst, src in ((r_r, None), (r_e, iof[:, 0:16]), (r_o, r_ost)):
                for c in range(2):
                    in1 = r_pos if src is None else src.unsqueeze(1).to_broadcast([P, 9, 16])
                    link(dve.tensor_tensor(r_tmp[:, 9 * c:9 * c + 9], cho[:, 9 * c:9 * c + 9], in1, ALU.mult))
                link(dve.tensor_reduce(dst, r_tmp, AX, ALU.add))
            link(dve.tensor_scalar(r_g, r_r, float(P), None, ALU.is_ge))
            link(dve.tensor_scalar(r_f, r_r, float(CAP), None, ALU.is_ge))
            link(dve.tensor_tensor(r_q3, r_r.unsqueeze(2).to_broadcast([P, 18, 8]),
                                   r_thr.unsqueeze(1).to_broadcast([P, 18, 8]), ALU.is_ge))
            link(dve.tensor_reduce(r_q, r_q3, AX, ALU.add))
            link(dve.scalar_tensor_tensor(r_p, r_g, -float(P), r_r, ALU.mult, ALU.add))
            link(dve.scalar_tensor_tensor(r_c, r_e, 2.0, r_g, ALU.mult, ALU.add))
            link(dve.scalar_tensor_tensor(r_po, r_q, -float(P), r_r, ALU.mult, ALU.add))
            link(dve.tensor_scalar(r_po, r_po, float(P - CAP), None, ALU.add))
            link(dve.tensor_tensor(r_co, r_o, r_q, ALU.add))
            link(dve.tensor_scalar(r_co, r_co, float(2 * NE - 1), None, ALU.add))
            link(dve.scalar_tensor_tensor(r_x, r_e, float(CAP), r_r, ALU.mult, ALU.add))
            link(dve.tensor_tensor(r_y, r_x, r_f, ALU.mult))
            link(dve.tensor_tensor(yrow[:].rearrange("p c t -> p (c t)"), r_x, r_y, ALU.subtract))
            link(dve.scalar_tensor_tensor(r_x, r_co, float(P), r_po, ALU.mult, ALU.add))
            link(dve.tensor_scalar(r_x, r_x, float(-2 * NE * P), None, ALU.add))
            link(dve.tensor_tensor(orow[:].rearrange("p c t -> p (c t)"), r_x, r_f, ALU.mult))
            link(dve.tensor_tensor(ogates[:], gates[:], r_f.rearrange("p (c t) -> p c t", c=2), ALU.mult))
            link(dve.tensor_tensor(gates[:], gates[:], ogates[:], ALU.subtract))
            for a, b in ((r_p, r_po), (r_c, r_co)):
                link(dve.tensor_tensor(b, b, a, ALU.subtract))
                link(dve.tensor_tensor(b, b, r_f, ALU.mult))
                link(dve.tensor_tensor(a, a, b, ALU.add))
            link(dve.tensor_tensor(r_cmj, iof[:, 0:NOV].unsqueeze(2).to_broadcast([P, NOV, 16]),
                                   r_inc.unsqueeze(1).to_broadcast([P, NOV, 16]), ALU.is_ge))
            link(dve.tensor_reduce(r_oe[:, 0:NOV], r_cmj, AX, ALU.add))
            link(dve.tensor_scalar(r_oe[:, 0:NOV], r_oe[:, 0:NOV], float(NE - 1), None, ALU.min))
            link(dve.tensor_copy(r_oe[:, NOV:NOV + 1], r_inc[:, 15:16]))
            link(dve.tensor_copy(oexp[:], r_oe[0:1]))
            link(dve.tensor_tensor(r_tokv, tokid[:], r_valid, ALU.mult))
            for n in range(18):
                if n >= 2:
                    dve.wait_ge(s_rsu, n - 1)
                dve.tensor_scalar(oneh_p[:, n % 2], iof[:], r_p[:, n:n + 1], None, ALU.is_equal)
                dve.tensor_scalar(oneh_c[:, n % 2], iof[:, 0:96], r_c[:, n:n + 1], r_tokv[:, n % 9:n % 9 + 1],
                                  ALU.is_equal, ALU.mult).then_inc(s_rs1, 1)
            dve.wait_ge(s_rsu, 18)
            dve.tensor_copy(tok[:], ps[:, 2, 0:COLS]).then_inc(s_route, 1)

            def split_expert(s, n):
                for j, (dst, src, hi) in enumerate(expert_parts(s, 1)):
                    dve.wait_ge(s_mh2, n + (j + 1))
                    dve.scalar_tensor_tensor(dst, src, SC, hi, ALU.mult, ALU.subtract).then_inc(s_mfree, 1)

            def read_tokens(s, f, n):
                dve.wait_ge(s_eT, n)
                dve.tensor_copy(xT[:, s, f // 2, 4 * (f % 2):4 * (f % 2) + 4],
                                bank16(1)[:, 0:4 * CAP].rearrange("p (k t) -> p k t", k=4)).then_inc(s_ev2, 1)

            def expert(i, s, first=False, last=False):
                def at(k, c):
                    return k * 2 * i + (k * s + c)

                dve.wait_ge(s_sg, at(1, 1))
                dve.tensor_scalar(eg, eg, 1.0, None, ALU.add).then_inc(s_s1, 1)
                dve.wait_ge(s_s1, at(3, 1))
                dve.reciprocal(eg, eg).then_inc(s_s1, 1)
                dve.wait_ge(s_s1, at(3, 2))
                dve.scalar_tensor_tensor(eg, ps[:, 2, 0:2 * CAP], ISC2, eg, ALU.mult, ALU.mult).then_inc(s_s1, 1)
                dve.wait_ge(s_s1, at(3, 3))
                dve.scalar_tensor_tensor(hid, ps[:, 3, 0:2 * CAP], ISC2 * SC, eg, ALU.mult, ALU.mult).then_inc(s_hf, 1)
                if not (last and s):
                    read_tokens(1 - s, 1, at(4, 6))
                dve.wait_ge(s_hf, at(1, 1))
                dve.wait_ge(s_hh2, at(1, 1))
                dve.tensor_tensor(hidl[:, s], hid.rearrange("p (f t) -> p f t", f=2), hidh[:, s],
                                  ALU.subtract).then_inc(s_hl2, 1)
                if not (last and s):
                    read_tokens(1 - s, 3, at(4, 8))
                if not first:
                    dve.wait_ge(s_yo[s], 32 * i)
                dve.wait_ge(s_down, at(4, 2))
                dve.tensor_scalar(yb[:, s, 512:D], ps[:, 5, :], ISC2, None, ALU.mult)
                dve.wait_ge(s_down, at(4, 4))
                dve.tensor_scalar(yb[0:CAP1, s, D + 512:2 * D], ps[0:CAP1, 7, :], ISC2, None, ALU.mult).then_inc(s_yv, 1)
                if not last:
                    split_expert(s, at(3, 6))

            split_expert(0, 0)
            read_tokens(0, 1, 2)
            read_tokens(0, 3, 4)
            split_expert(1, 3)
            for s in range(2):
                expert(0, s, first=True)
            with dve.Fori(1, NE // 2 - 1) as i:
                for s in range(2):
                    expert(i, s)
            for s in range(2):
                expert(NE // 2 - 1, s, last=True)

            def overflow():
                dve.memset(junk[:], 0.0).then_inc(s_ovv, 1)
                with dve.Fori(0, NOV) as j:
                    def v(n):
                        return len(OV_VEC) * j + (1 + OV_VEC[n])

                    def a(n):
                        return len(OV_ACT) * j + OV_ACT[n]

                    def p(n):
                        return len(OV_PE) * j + OV_PE[n]

                    dve.wait_ge(s_ova, a("weights_hi"))
                    for dst, src, hi in expert_parts(0, 1):
                        ins = dve.scalar_tensor_tensor(dst, src, SC, hi, ALU.mult, ALU.subtract)
                    ins.then_inc(s_ovv, 1)
                    dve.wait_ge(s_ovp, p("tokens"))
                    dve.tensor_copy(ovxT[:, 1], bank16(1).rearrange("p (k t) -> p k t", k=KC)).then_inc(s_ovv, 1)
                    dve.wait_ge(s_ova, a("exp"))
                    dve.tensor_scalar(ove, ove, 1.0, None, ALU.add).then_inc(s_ovv, 1)
                    dve.wait_ge(s_ovv, v("plus_one"))
                    dve.reciprocal(ove, ove).then_inc(s_ovv, 1)
                    dve.wait_ge(s_ovv, v("sigmoid"))
                    dve.scalar_tensor_tensor(ove, ps[:, 2, 0:2 * P], ISC2, ove, ALU.mult, ALU.mult).then_inc(s_ovv, 1)
                    dve.wait_ge(s_ovv, v("silu"))
                    dve.scalar_tensor_tensor(ovhid, ps[:, 3, 0:2 * P], ISC2 * SC, ove, ALU.mult,
                                             ALU.mult).then_inc(s_ovv, 1)
                    dve.wait_ge(s_ova, a("hidden_hi"))
                    dve.wait_ge(s_ovv, v("hidden"))
                    dve.tensor_tensor(ovhl, ovhid.rearrange("p (f t) -> p f t", f=2), ovhh,
                                      ALU.subtract).then_inc(s_ovv, 1)
                    dve.wait_ge(s_ovp, p("down"))
                    dve.tensor_scalar(yb[:, 0, 512:D], ps[:, 5, :], ISC2, None, ALU.mult).then_inc(s_ovv, 1)
                n = 1 + len(OV_VEC) * NOV
                for t in range(NT + 1):
                    r = rows(t)
                    dve.wait_ge(s_ovx, 16 * NOV + 32 * (t + 1))
                    for c in range(2):
                        dve.scalar_tensor_tensor(x1[0:r, t], yg[0:r, 0, c], ogates[0:r, c, t:t + 1], x1[0:r, t],
                                                 ALU.mult, ALU.add).then_inc(s_ovv, 1)
                        dve.wait_ge(s_ovv, n + 2 * t + c + 1)

            when_overflow(dve, overflow)
            def gather_sum(t):
                r = rows(t)
                dve.wait_ge(s_yg[t % 2], 32 * (t // 2 + 1))
                link(dve.scalar_tensor_tensor(x1[0:r, t], yg[0:r, t % 2, 0], gates[0:r, 0, t:t + 1], x1[0:r, t],
                                              ALU.mult, ALU.add))
                dve.scalar_tensor_tensor(x1[0:r, t], yg[0:r, t % 2, 1], gates[0:r, 1, t:t + 1], x1[0:r, t],
                                         ALU.mult, ALU.add).then_inc(s_fq, 1)

            gather_sum(0)
            dve.wait_ge(s_g1, 48)
            for t in range(NT + 1):
                r = rows(t)
                if t + 1 <= NT:
                    gather_sum(t + 1)
                dve.wait_ge(s_fs, t + 1)
                normed("f", t, D)
                if t >= 2:
                    dve.wait_ge(s_fout[t % 2], 16 * (t // 2))
                dve.scalar_tensor_tensor(fin[0:r, t % 2], x1[0:r, t], rst[0:r, 16 + t:17 + t], gbc[0:r], ALU.mult,
                                         ALU.mult).then_inc(s_fo, 1)

        @block.tensor
        def _(pe):
            def split_mm(out, lh, ll, rh, rl, start, stop):
                pe.matmul(out, lh, rh, start=start, stop=False)
                pe.matmul(out, lh, rl, start=False, stop=False)
                return pe.matmul(out, ll, rh, start=False, stop=stop)

            pe.wait_ge(s_const, 2)
            for t in range(NT + 1):
                r = rows(t)
                pe.wait_ge(s_xn, t + 1)
                if t >= 2:
                    pe.wait_ge(s_hl, 2 * (t - 1))
                for k in range(KC):
                    ins = pe.transpose(ps[:, 4 + 2 * (t % 2) + k // 4, r * (k % 4):r * (k % 4) + r],
                                       xt(t)[0:r, P * k:P * k + P], ident[0:r, 0:r])
                ins.then_inc(s_xT, 1)

            def project(g, after=None):
                kind, _, wd = GROUPS[g]
                sh, sl = slot_h[g % 2], slot_l[g % 2]
                pe.wait_ge(s_wl, HALVES_TO[g])
                for (gg, blk, j) in UNITS:
                    if gg != g:
                        continue
                    u = UNIT_AT[(gg, blk, j)]
                    if u >= PB:
                        pe.wait_ge(s_ev[u % PB], u // PB)
                    for k in range(KC):
                        if kind == "T":
                            m = min(P, wd)
                            cs = slice(CH * j, CH * (j + 1))
                            ins = split_mm(ps[0:m, u % PB, 0:CH], sh[:, k, P * blk:P * blk + m],
                                           sl[:, k, P * blk:P * blk + m], hTh[:, k, cs], hTl[:, k, cs],
                                           k == 0, k == KC - 1)
                        else:
                            r = rows(blk)
                            ins = split_mm(ps[0:r, u % PB, :], hTh[:, k, span(blk)], hTl[:, k, span(blk)],
                                           sh[:, k, :], sl[:, k, :], k == 0, k == KC - 1)
                    ins.then_inc(s_mm, 1)
                    if after:
                        after(blk)

            pe.wait_ge(s_hl, 2 * (NT + 1))
            project(GQK)
            project(CODE)
            project(GV)
            pe.wait_ge(s_par, 16 * N_PAR)
            for u in UNITS:
                if u[0] in (CODE, GQK, GV):
                    i = UNIT_AT[u]
                    pe.wait_ge(s_ev[i % PB], i // PB + 1)
            for p in range(2):
                for j in range(3):
                    if p:
                        pe.wait_ge(s_zr, 3)
                        pe.wait_ge(s_oev, NT)
                        pe.wait_ge(s_S, NT)
                        pe.wait_ge(s_scm, NT)
                        pe.wait_ge(s_kdn, NT)
                    pe.matmul(ps[:, 4 + j, 0:CH], wa2[:, P * p:P * p + P], code[:, CH * j:CH * (j + 1)],
                              start=True, stop=True).then_inc(s_z, 1)
                pe.wait_ge(s_prep, p + 1)
                pe.wait_ge(s_zr, 3 * p + 3)
                for c in range(NT + 1):
                    if c < NT:
                        n = p * NT + c
                        bank = 4 + n % 2
                        if n >= 2:
                            pe.wait_ge(s_scm, n - 1)
                            pe.wait_ge(s_kdn, n - 1)
                        kk = ek[:, span(c)]
                        pe.matmul(ps[:, bank, 0:256], kk, qa[:, c].rearrange("p h i -> p (h i)"), start=True, stop=True)
                        pe.matmul(ps[64:P, bank, 256:384], kk[:, 64:P], qb[:, c].rearrange("p h i -> p (h i)"),
                                  start=True, stop=True)
                        pe.transpose(ps[:, n % 2, 0:P], ed[:, span(c)], ident[:]).then_inc(s_sc, 1)
                    if c >= 1:
                        n = p * NT + c - 1
                        bank = 6 + n % 2
                        if n >= 2:
                            pe.wait_ge(s_oev, n - 1)
                        if n:
                            pe.wait_ge(s_S, n)
                        pe.wait_ge(s_scm, n + 1)
                        pe.wait_ge(s_kdn, n + 1)
                        vp = gv[:, c - 1, 256 * p:256 * p + 256]
                        pe.matmul(ps[:, bank, 0:256], qs[:, span(c - 1)], sbd[:, p].rearrange("p h v -> p (h v)"),
                                  start=True, stop=False)
                        for h in range(2):
                            pe.matmul(ps[:, bank, P * h:P * h + P], scb[:, n % 2, h, :], vp[:, P * h:P * h + P],
                                      start=False, stop=h == 1)
                        pe.matmul(ps[:, 2 + n % 2, 0:256], kdn[:, n % 2], vp, start=True, stop=True).then_inc(s_o, 1)
            pe.wait_ge(s_scm, 2 * NT)
            pe.wait_ge(s_kdn, 2 * NT)
            for p in range(2):
                ins = pe.transpose(ps[0:NB, 4, P * p:P * p + P], gk[:, p, SEQ:T], ident[:])
            ins.then_inc(s_ks, 1)
            pe.wait_ge(s_km, 1)
            pe.wait_ge(s_oev, 2 * NT)
            pe.wait_ge(s_S, 2 * NT)
            for m in range(2 * NB):
                p, b = m // NB, m % NB
                if m >= 8 and m % 2 == 0:
                    pe.wait_ge(s_sn, m // 2 - 3)
                ins = pe.matmul(ps[:, 4 + m // 2 % 4, 256 * (m % 2):256 * (m % 2) + 256], kmask[:, b, P * p:P * p + P],
                                gv[0:NB, NT, 256 * p:256 * p + 256], start=True, stop=True)
                if m % 2:
                    ins.then_inc(s_op, 1)
            pe.wait_ge(s_sn, 8)
            for p in range(2):
                for h in range(2):
                    for b in range(NB):
                        ins = pe.matmul(ps[0:NB, 4, DV * (2 * p + h):DV * (2 * p + h) + DV], qmask[:, p, h, b, :],
                                        st[:, p, b, :], start=b == 0, stop=b == NB - 1)
            ins.then_inc(s_ks, 1)

            def mix_transpose(n, t, src, ready, count):
                r = rows(t)
                pe.wait_ge(ready, count)
                if n >= 2:
                    pe.wait_ge(s_ml, n - 1)
                for k in range(4):
                    ins = pe.transpose(ps[:, 4 + n % 2, r * k:r * k + r], src[0:r, P * k:P * k + P], ident[0:r, 0:r])
                ins.then_inc(s_mT, 1)

            def gated_transpose(t):
                if t >= 0:
                    mix_transpose(t, t, gt[:, t % 2], s_mx, t + 1)

            pe.wait_ge(s_osr, 1)
            project(GR, after=lambda blk: gated_transpose(blk - 1))
            gated_transpose(NT)
            project(DQ)
            project(DKG)
            pe.wait_ge(s_ml, NT + 1)
            for u in range(UNIT_AT[(DKG, 3, 2)] - 3, UNIT_AT[(DKG, 3, 2)] + 1):
                pe.wait_ge(s_ev[u % PB], u // PB + 1)
            for t in range(NT + 2):
                r = rows(t)
                if t >= 4:
                    pe.wait_ge(s_knr, t - 3)
                for h in range(H):
                    out = ps[0:r, 4 + t % 4, P * h:P * h + P]
                    hi, lo = (kdh, kdl) if t <= NT else (qdh, qdl)
                    pe.matmul(out, hi[:, h, span(min(t, NT))], ident16[:], start=True, stop=False)
                    ins = pe.matmul(out, lo[:, h, span(min(t, NT))], ident16[:], start=False, stop=True)
                ins.then_inc(s_kn, 1)
            project(DVG)
            for u in range(len(UNITS) - PB, len(UNITS)):
                pe.wait_ge(s_ev[u % PB], u // PB + 1)
            pe.wait_ge(s_knr, NT + 2)
            for u in range(UN + 8):
                if u < UN:
                    i, h = u // H, u % H
                    n = (i + 1) * P
                    for m in range(2):
                        if u >= 2:
                            pe.wait_ge(s_p, 2 * (u - 1) if u < 16 else 2 * (u - 1) + m + 1)
                        hp = slice(DK * m, DK * m + DK)
                        q = slice(P * i, P * i + P)
                        sc = scores(u, m)
                        for c in range(0, n, 512):
                            ks = slice(c, min(n, c + 512))
                            ins = split_mm(sc[:, ks], qdh[hp, h, q], qdl[hp, h, q], kdh[hp, h, ks], kdl[hp, h, ks],
                                           True, True)
                        ins.then_inc(s_qk, 1)
                if 2 <= u < UN + 2:
                    v = u - 2
                    i, h = v // H, v % H
                    pe.wait_ge(s_wTe, FILL0[v + 1])
                    if h == 0 and i >= 2:
                        pe.wait_ge(s_ml, MIXED + i - 1)
                    for j in range(i + 1):
                        ins = pe.matmul(ps[:, 6 + i % 2, DV * h:DV * h + DV], wT[:, v % 2, j], vd[:, j, DV * h:DV * h + DV],
                                        start=j == 0, stop=j == i)
                    ins.then_inc(s_pv, 1)
                if 1 <= u <= UN:
                    v = u - 1
                    i = v // H
                    pe.wait_ge(s_wc, v + 1)
                    for f in range(fills(v)):
                        k = FILL0[v] + f
                        if k >= 2:
                            pe.wait_ge(s_wTe, k - 1)
                        w = min(4, i + 1 - 4 * f)
                        for j in range(w):
                            ins = pe.transpose(ps[:, 4 + k % 2, P * j:P * j + P],
                                               prob[:, v % 2, 0, P * (4 * f + j):P * (4 * f + j) + P], ident[:])
                        ins.then_inc(s_wT, 1)
                if u % H == 1 and 9 <= u < UN + 9:
                    i = (u - 9) // H
                    pe.wait_ge(s_dn, i + 1)
                    for h in range(H):
                        ins = pe.transpose(ps[:, 6 + i % 2, P * h:P * h + P], gt[:, i % 2, P * h:P * h + P], ident[:])
                    ins.then_inc(s_mT, 1)
            pe.wait_ge(s_wol, KC // 2)
            pe.wait_ge(s_ml, MIXED + NT)
            pe.wait_ge(s_p, 2 * UN)
            for t in range(NT + 2):
                if t == NT:
                    pe.wait_ge(s_dec, DEC["normed"])
                    pe.transpose(ps[:, 7, 0:4 * NB], dod[:], ident[0:4 * NB, 0:4 * NB]).then_inc(s_mT, 1)
                    pe.wait_ge(s_mh, MIXED + NT + 1)
                    pe.wait_ge(s_ml, MIXED + NT + 1)
                if t <= NT:
                    r = rows(t)
                    if t >= 2:
                        pe.wait_ge(s_x1, 2 * (t - 1))
                    for half in range(2):
                        cs = slice(512 * half, 512 * half + 512)
                        for k in range(KC):
                            ins = split_mm(ps[0:r, 2 * (t % 2) + half, :], mixh[:, k, span(t)], mixl[:, k, span(t)],
                                           woh[:, k, cs], wol[:, k, cs], k == 0, k == KC - 1)
                        ins.then_inc(s_om, 1)
                if t == 0:
                    pe.wait_ge(s_dec, DEC["sums"])
                    pe.matmul(ps[:, 6, 0:NB * 8], ones[:], dmx[:], start=True, stop=True).then_inc(s_dsa, 1)
                    pe.wait_ge(s_wrs, 1)
                if t >= 1:
                    v = t - 1
                    r = rows(v)
                    pe.wait_ge(s_h2h, v + 1)
                    pe.wait_ge(s_h2l, v + 1)
                    if v:
                        pe.wait_ge(s_hTh, v)
                        pe.wait_ge(s_hTl, v)
                        pe.wait_ge(s_rtr, v)
                    else:
                        pe.wait_ge(s_wTe, FILL0[UN])
                    for lo in range(2):
                        for k in range(KC):
                            ins = pe.transpose(bank16(4 + lo)[:, r * k:r * k + r],
                                               h2s[0:r, v % 2, D * lo + P * k:D * lo + P * k + P], ident16[0:r, 0:r])
                    ins.then_inc(s_h2T, 1)
                    pe.wait_ge(s_hTh, v + 1)
                    pe.wait_ge(s_hTl, v + 1)
                    for k in range(KC):
                        ins = split_mm(ps[0:r, 6, 0:NG + NE], h2T[:, v % 2, 0, k, 0:r], h2T[:, v % 2, 1, k, 0:r],
                                       wrh[:, k], wrl[:, k], k == 0, k == KC - 1)
                    ins.then_inc(s_rt, 1)
                if t < NT:
                    pe.wait_ge(s_wz, t + 1)
                    for n in (2 * t, 2 * t + 1):
                        pe.wait_ge(s_vp[n % 2], 64 * (n // 2 + 1))
                        for g in range(KHALF):
                            ins = pe.matmul(ps[0:4 * NB, 7, :], wz[:, t % 2, KHALF * (n % 2) + g],
                                            kv[:, n % 2, 512 * g:512 * g + 512], start=n == 0 and g == 0, stop=False)
                        ins.then_inc(s_pvd, 1)
                if t == NT - 1:
                    pe.wait_ge(s_dec, DEC["new_weights_spread"])
                    pe.matmul(ps[0:4 * NB, 7, :], wnz[:].rearrange("p b h -> p (b h)"), vd[0:NB, NT, :], start=False,
                              stop=True).then_inc(s_pvd, 1)
            pe.wait_ge(s_x1, 2 * (NT + 1))
            pe.wait_ge(s_re, 3)
            r_a2 = r_a.rearrange("p t e -> p (t e)")
            pe.matmul(ps[:, 0, 0:144], strict[:], r_a2, start=True, stop=True)
            pe.matmul(ps[:, 1, 0:144], ones[:], r_a2, start=True, stop=True).then_inc(s_rc, 1)
            for n in range(18):
                pe.wait_ge(s_rs1, n + 1)
                pe.matmul(ps[:, 2, 0:96], oneh_p[:, n % 2], oneh_c[:, n % 2], start=n == 0, stop=n == 17
                          ).then_inc(s_rsu, 1)
            pe.wait_ge(s_route, 1)

            def transpose_tokens(s, loaded, e4, e2):
                pe.wait_ge(s_gx[s], loaded)
                for f in range(4):
                    lo, kh = f // 2, f % 2
                    if e2 is not None or f >= 2:
                        pe.wait_ge((s_ea, s_ev2)[kh], (0 if e2 is None else e2) + lo)
                    for k in range(4):
                        col = D * lo + P * (4 * kh + k)
                        pe.transpose(bank16(kh)[:, CAP * k:CAP * k + P], xg[:, s, 0, col:col + P], ident16[:])
                        ins = pe.transpose(bank16(kh)[:, CAP * k + P:CAP * k + CAP], xg[0:CAP1, s, 1, col:col + P],
                                           ident16[0:CAP1, 0:CAP1])
                    ins.then_inc(s_eT, 1)

            def expert(i, s, first=False, last=False):
                def at(k, c):
                    return k * 2 * i + (k * s + c)

                pe.wait_ge(s_mfree, at(3, 3))
                pe.wait_ge(s_ea, at(2, 2))
                pe.wait_ge(s_ev2, at(2, 2))
                if not (first and s == 0):
                    pe.wait_ge(s_hf, at(1, 0))
                for bank, wh, wl in ((2, egh[s], egl[s]), (3, euh[s], eul[s])):
                    for ft in range(2):
                        fs = slice(P * ft, P * ft + P)
                        for k in range(KC):
                            ins = split_mm(ps[:, bank, CAP * ft:CAP * ft + CAP], wh[:, k, fs], wl[:, k, fs],
                                           xT[:, s, 0, k], xT[:, s, 1, k], k == 0, k == KC - 1)
                ins.then_inc(s_gup, 1)
                if not (last and s):
                    transpose_tokens(1 - s, 32 * i + (32 if s == 0 else 64), at(4, 4), at(2, 2))
                pe.wait_ge(s_hh2, at(1, 1))
                pe.wait_ge(s_hl2, at(1, 1))
                if not (first and s == 0):
                    pe.wait_ge(s_ya, at(1, 0))
                    pe.wait_ge(s_yv, at(1, 0))
                for g, (r0, r1) in enumerate(((0, P), (P, CAP))):
                    for half in range(2):
                        cs = slice(512 * half, 512 * half + 512)
                        for ft in range(2):
                            ins = split_mm(ps[0:r1 - r0, 4 + 2 * g + half, :], hidh[:, s, ft, r0:r1], hidl[:, s, ft, r0:r1],
                                           edh[s][:, ft, cs], edl[s][:, ft, cs], ft == 0, ft == 1)
                        ins.then_inc(s_down, 1)

            transpose_tokens(0, 32, None, None)
            for s in range(2):
                expert(0, s, first=True)
            with pe.Fori(1, NE // 2 - 1) as i:
                for s in range(2):
                    expert(i, s)
            for s in range(2):
                expert(NE // 2 - 1, s, last=True)

            def overflow():
                with pe.Fori(0, NOV) as j:
                    def v(n):
                        return len(OV_VEC) * j + (1 + OV_VEC[n])

                    def a(n):
                        return len(OV_ACT) * j + OV_ACT[n]

                    pe.wait_ge(s_ovx, 16 * j + 16)
                    for lo in range(2):
                        for k in range(KC):
                            ins = pe.transpose(bank16(lo)[:, P * k:P * k + P],
                                               xg[:, 0, 0, D * lo + P * k:D * lo + P * k + P], ident16[:])
                    ins.then_inc(s_ovp, 1)
                    pe.wait_ge(s_ova, a("tokens_hi"))
                    pe.wait_ge(s_ovv, v("tokens_lo"))
                    for bank, wh, wl in ((2, egh[0], egl[0]), (3, euh[0], eul[0])):
                        for ft in range(2):
                            fs = slice(P * ft, P * ft + P)
                            for k in range(KC):
                                ins = split_mm(ps[:, bank, fs], wh[:, k, fs], wl[:, k, fs], ovxT[:, 0, k], ovxT[:, 1, k],
                                               k == 0, k == KC - 1)
                    ins.then_inc(s_ovp, 1)
                    pe.wait_ge(s_ova, a("hidden_hi"))
                    pe.wait_ge(s_ovv, v("hidden_lo"))
                    for half in range(2):
                        cs = slice(512 * half, 512 * half + 512)
                        for ft in range(2):
                            ins = split_mm(ps[:, 4 + half, :], ovhh[:, ft], ovhl[:, ft], edh[0][:, ft, cs],
                                           edl[0][:, ft, cs], ft == 0, ft == 1)
                    ins.then_inc(s_ovp, 1)

            when_overflow(pe, overflow)


_INS = ["x_prompt", "x_sample", "cache_k", "cache_v", "state_gla", "page_table", "norm1_g", "w_in", "w_a2", "b_a",
        "gla_norm_g", "lambda_q1", "lambda_k1", "lambda_q2", "lambda_k2", "diff_norm_g", "w_out", "norm2_g",
        "w_router_g", "b_router_g", "w_router_e", "b_router_e", "w_gate", "w_up", "w_down", "norm_f_g"]
_OUTS = [("y_prompt", (1, SEQ, D)), ("y_sample", (NB, 1, D)), ("k_prompt", (1, 1, SEQ, H, 2 * DK)),
         ("v_prompt", (1, 1, SEQ, H, DV)), ("gla_prompt", (1, 1, H, DK, DV)), ("k_sample", (1, NB, 1, H, 2 * DK)),
         ("v_sample", (1, NB, 1, H, DV)), ("gla_sample", (1, NB, H, DK, DV))]


def kernel(**inputs):
    import numpy as np
    import concourse.bacc as bacc
    from concourse.bass_utils import run_bass_kernel_spmd

    arrays = {n: np.ascontiguousarray(inputs[n]) for n in _INS}
    nc = bacc.Bacc("TRN2", target_bir_lowering=False, num_devices=1)
    ins = {n: nc.dram_tensor("in_" + n, a.shape, mybir.dt.from_np(a.dtype), kind="ExternalInput").ap()
           for n, a in arrays.items()}
    outs = {n: nc.dram_tensor("out_" + n, shape, F32, kind="ExternalOutput").ap() for n, shape in _OUTS}
    build(nc, ins, outs)
    r = run_bass_kernel_spmd(nc, [{"in_" + n: a for n, a in arrays.items()}], core_ids=[0])
    return tuple(r.results[0]["out_" + n] for n, _ in _OUTS)
```

```python
import math
from contextlib import ExitStack

import concourse.bass as bass
from concourse import mybir

F32 = mybir.dt.float32
F16 = mybir.dt.float16
I32 = mybir.dt.int32
ALU = mybir.AluOpType
ACT = mybir.ActivationFunctionType
AX = mybir.AxisListType.X

P = 128
D = 1024
KC = D // P
SEQ = 1024
NB = 8
T = SEQ + NB
NT = SEQ // P
H = 4
DK, DV = 64, 128
RANK = 16
PAST = 1024
PAGE = 128
NPG = PAST // PAGE
CH = 344
NG, EPG, NE = 4, 4, 16
FF = 256
CAP = 208
CAP1 = CAP - P
NOV = 16
COLS = 2 * NE + NOV
SC = 64.0
ISC2 = 1.0 / (SC * SC)
EPS = 1e-6
TAU = 16.0
LAM_INIT = 0.8 - 0.6 * math.exp(-0.3 * 0)
NEG = -1e30
BIG = 60000.0

GQK, CODE, GV, GR, DQ, DKG, DVG = range(7)
GROUPS = [("T", 0, 512), ("T", 1536, RANK), ("N", 512, 512), ("N", 1024, 512),
          ("T", 1552, 512), ("T", 2064, 512), ("N", 2576, 512)]
HALVES = []
for g, (_, c0, w) in enumerate(GROUPS):
    for o in range(0, w, 256):
        HALVES.append((g, c0 + o, min(256, w - o), o))
HALVES_TO = [max(i for i, h in enumerate(HALVES) if h[0] <= g) + 1 for g in range(len(GROUPS))]


def rows(t):
    return P if t < NT else NB


def span(t):
    return slice(t * P, t * P + rows(t))


def proj_units():
    units = []
    for g, (kind, _, w) in enumerate(GROUPS):
        if kind == "T":
            units += [(g, c, j) for c in range(max(1, w // P)) for j in range(3)]
        else:
            units += [(g, t, 0) for t in range(NT + 1)]
    return units


UNITS = proj_units()
UNIT_AT = {u: i for i, u in enumerate(UNITS)}
UNITS_TO = [sum(1 for u in UNITS if u[0] <= g) for g in range(len(GROUPS))]
DEC = {n: i + 1 for i, n in enumerate(("max", "exp_in", "sums", "new_weights", "out", "normed"))}
OV_ACT = {n: i + 1 for i, n in enumerate(("weights_hi", "tokens_hi", "exp", "hidden_hi", "y"))}
OV_VEC = {n: i + 1 for i, n in enumerate(("weights_lo", "tokens_lo", "plus_one", "sigmoid", "silu", "hidden",
                                          "hidden_lo", "y"))}
OV_PE = {n: i + 1 for i, n in enumerate(("tokens", "gate_up", "down"))}
MIXED = NT + 1
N_PAR = 3 + 1 + 4 + 1 + NG + 3
X_GROUP = [(0, 1)] + [(1, 2)] * 2 + [(2, 3)] * 3 + [(3, 3)] * 3
GR_BANKS = 2
PB = 4


def unit_banks():
    bank, nth, had = [], [], [0] * PB
    for u, (g, t, _) in enumerate(UNITS):
        b = t % GR_BANKS if g == GR else u % PB
        had[b] += 1
        bank.append(b)
        nth.append(had[b])
    return bank, nth


BANK, NTH = unit_banks()


def build(nc, I, O):
    ctx = ExitStack()
    with ctx:
        def sb(name, shape, dt=F32):
            return ctx.enter_context(nc.sbuf_tensor(name, shape, dt))

        def sem(name):
            return ctx.enter_context(nc.semaphore(name))

        ps = ctx.enter_context(nc.psum_tensor("ps", [P, 8, 512], F32))

        hT_reg = sb("hT_reg", [P, 8 * T])
        mix_reg = sb("mix_reg", [P, 8 * T])
        w_reg = sb("w_reg", [P, 2 * 2048 + 2 * 4096])
        dg_reg = sb("dg_reg", [P, 8 * T + 9 * 512])

        hTh = hT_reg[:, 0:4 * T].bitcast(F16).rearrange("p (k t) -> p k t", k=KC)
        hTl = hT_reg[:, 4 * T:8 * T].bitcast(F16).rearrange("p (k t) -> p k t", k=KC)
        xin = mix_reg[:, 0:NT * D].rearrange("p (t d) -> p t d", t=NT)
        mixh = mix_reg[:, 0:4 * T].bitcast(F16).rearrange("p (k t) -> p k t", k=KC)
        mixl = mix_reg[:, 4 * T:8 * T].bitcast(F16).rearrange("p (k t) -> p k t", k=KC)
        stage = [w_reg[:, 2048 * s:2048 * (s + 1)] for s in range(2)]
        slot_h = [w_reg[:, 4096 * (s + 1):4096 * (s + 1) + 2048].bitcast(F16).rearrange(
            "p (k n) -> p k n", k=KC) for s in range(2)]
        slot_l = [w_reg[:, 4096 * (s + 1) + 2048:4096 * (s + 2)].bitcast(F16).rearrange(
            "p (k n) -> p k n", k=KC) for s in range(2)]
        qdh, qdl, kdh, kdl = [dg_reg[:, 2 * T * i:2 * T * (i + 1)].bitcast(F16).rearrange(
            "p (h t) -> p h t", h=H) for i in range(4)]
        vd = dg_reg[:, 8 * T:].rearrange("p (t c) -> p t c", t=9)
        gq = dg_reg[:, 0:2 * T].rearrange("p (a t) -> p a t", a=2)
        gk = dg_reg[:, 2 * T:4 * T].rearrange("p (a t) -> p a t", a=2)
        gv = dg_reg[:, 4 * T:4 * T + 4608].rearrange("p (t c) -> p t c", t=9)
        o = 4 * T + 4608
        ea = dg_reg[:, o:o + 1024]
        qmask = dg_reg[:, o:o + 256].rearrange("p (a h b c) -> p a h b c", a=2, h=2, b=NB)
        ek = dg_reg[:, o + 1024:o + 2048]
        ed = dg_reg[:, o + 2048:o + 3072]
        eb = dg_reg[:, o + 3072:o + 3584]
        bc = mix_reg[:, 0:T]
        la = mix_reg[:, T:2 * T]
        qs = la
        es = mix_reg[:, 2 * T:3 * T]
        qa = mix_reg[:, 3 * T:3 * T + 2048].rearrange("p (c h i) -> p c h i", c=8, h=2)
        qb = mix_reg[:, 3 * T + 2048:3 * T + 3072].rearrange("p (c h i) -> p c h i", c=8, h=2)
        kmask = mix_reg[0:NB, 3 * T:3 * T + 2048].rearrange("p (b c) -> p b c", b=NB)
        st = mix_reg[:, 6 * T:6 * T + 2048].rearrange("p (a b v) -> p a b v", a=2, b=NB)
        code = mix_reg[0:RANK, 6 * T:7 * T]

        ident = sb("ident", [P, P])
        ident16 = sb("ident16", [P, P], F16)
        maskneg = sb("maskneg", [P, P])
        mask_ji = sb("mask_ji", [P, P])
        ones = sb("ones", [P, P])
        gbc = sb("gbc", [P, D])
        ba_col = sb("ba_col", [P, 2])
        glag = sb("glag", [P, DV])
        wa2 = sb("wa2", [RANK, 2 * P])
        gs_reg = sb("gs_reg", [P, 1280])
        sbd = gs_reg[:, 0:512].rearrange("p (a h v) -> p a h v", a=2, h=2)
        scb = gs_reg[:, 512:1024].rearrange("p (s h i) -> p s h i", s=2, h=2)
        kdn = gs_reg[:, 1024:1280].rearrange("p (s c) -> p s c", s=2)
        diagm = sb("diagm", [P, 2, NB, NB])
        junk = sb("junk", [P, D])
        ss = sb("ss", [P, 40])
        rst = sb("rst", [P, 40])
        a_s = sb("a_s", [P, 2, NB])
        gt = sb("gt", [P, 2, 512])
        knat = mix_reg[:, 2 * T:2 * T + 2048].rearrange("p (s c) -> p s c", s=4)
        xs = gt[0:NB].rearrange("p s c -> p (s c)")
        neghalf = sb("neghalf", [P, 40])

        prob = hT_reg[:, 0:6144].rearrange("p (s m n) -> p s m n", s=3, m=2)
        wT = hT_reg[:, 6144:8192].rearrange("p (s j q) -> p s j q", s=2, j=NT)
        kv = sb("kv", [P, 2, 2048])
        dgain = sb("dgain", [P, DV])
        lams = kv[:, 0, 0:4 * DK].rearrange("p (i d) -> p i d", i=4)
        lamw = sb("lamw", [P, 8])
        nlam = lamw[:, 4:5]
        mxn = sb("mxn", [P, 2, 2])
        rsum = sb("rsum", [P, 3, H, 2])
        rinv = sb("rinv", [P, 3, H, 2])
        comb = sb("comb", [P, 1])
        mxs = sb("mxs", [P, 2, 2])
        comb4 = sb("comb4", [P, 2, H])
        qn = gt[0:NB, 0]
        snew = sb("snew", [NB, 8])
        qbc = mix_reg[:, 6 * T:6 * T + 1024].rearrange("p (s c) -> p s c", s=2)
        dsc = mix_reg[:, 6 * T + 1024:6 * T + 1600].rearrange("p (b m g) -> p b m g", b=NB, m=8)
        dw = gs_reg[:, 0:288].rearrange("p (b h g) -> p b h g", b=NB, h=H)
        dacc = w_reg[:, 0:4096].rearrange("p (b c) -> p b c", b=NB)
        dmx = sb("dmx", [P, NB * 8])
        dmb = sb("dmb", [P, NB * 8])
        wn = sb("wn", [NB, H])
        ptab = sb("ptab", [1, NB * NPG], I32)
        vd_new = vd[0:NB, NT]
        dod = gs_reg[0:NB, 512:1024]
        sel = sb("sel", [P, 2 * NB - 1])
        identb = sb("identb", [P, P], F16)
        maskb = sb("maskb", [P, P], F16)
        xr = hT_reg[:, 0:2048].rearrange("p (s d) -> p s d", s=2)
        h2 = hT_reg[:, 2048:4096].rearrange("p (s d) -> p s d", s=2)
        h2s = hT_reg[:, 4096:6144].bitcast(F16).rearrange("p (s d) -> p s d", s=2)
        h2T = hT_reg[:, 6144:8192].bitcast(F16).rearrange("p (s l k t) -> p s l k t", s=2, l=2, k=KC)
        x1 = dg_reg[:, 0:9 * D].rearrange("p (t d) -> p t d", t=9)
        woh = w_reg[:, 4096:8192].bitcast(F16).rearrange("p (k n) -> p k n", k=KC)
        wol = w_reg[:, 8192:12288].bitcast(F16).rearrange("p (k n) -> p k n", k=KC)
        wr = sb("wr", [P, KC, NG + NE])
        wrh = sb("wrh", [P, KC, NG + NE], F16)
        wrl = sb("wrl", [P, KC, NG + NE], F16)
        br = sb("br", [P, NG + NE])
        lg = sb("lg", [P, 9, NG + NE])
        gates = sb("gates", [P, 2, 9])
        ogates = sb("ogates", [P, 2, 9])
        yrow = sb("yrow", [P, 2, 9], I32)
        orow = sb("orow", [P, 2, 9], I32)
        tok = sb("tok", [P, COLS], I32)
        oexp = sb("oexp", [1, NOV + 1], I32)
        iof = sb("iof", [P, P])
        tokid = sb("tokid", [P, 9])
        strict = sb("strict", [P, P])
        mst = [w_reg[:, 6144 * i:6144 * (i + 1)] for i in range(2)]
        gate = [kv[:, t // 4, 512 * (t % 4):512 * (t % 4) + 512] if t < NT else junk[:, 512:1024]
                for t in range(NT + 1)]
        f16 = lambda ap: ap.bitcast(F16)
        gu = [[mix_reg[:, 0:1024], mix_reg[:, 1024:2048], mix_reg[:, 2048:3072], mix_reg[:, 3072:4096],
               mix_reg[:, 4096:5120], mix_reg[:, 5120:6144]],
              [mix_reg[:, 6144:7168], mix_reg[:, 7168:8192], dg_reg[:, 9216:10240], dg_reg[:, 10240:11264],
               dg_reg[:, 11264:12288], gs_reg[:, 0:1024]]]
        egh, egl, euh, eul = [[f16(gu[i][j]).rearrange("p (k f) -> p k f", k=KC) for i in range(2)]
                              for j in range(4)]
        edh, edl = [[f16(gu[i][j]).rearrange("p (k f) -> p k f", k=2) for i in range(2)] for j in (4, 5)]
        xg = hT_reg[:, 0:4096].bitcast(F16).rearrange("p (s g c) -> p s g c", s=2, g=2)
        xT = hT_reg[:, 4096:4096 + 2 * KC * CAP].bitcast(F16).rearrange("p (s l k t) -> p s l k t", s=2, l=2, k=KC)
        yb = kv
        eg = junk[:, 0:2 * CAP]
        hid = junk[:, 2 * CAP:4 * CAP]
        hidh = gt[:, 0, 0:2 * CAP].bitcast(F16).rearrange("p (s f t) -> p s f t", s=2, f=2)
        hidl = gt[:, 1, 0:2 * CAP].bitcast(F16).rearrange("p (s f t) -> p s f t", s=2, f=2)
        gt2 = gt[:].rearrange("p s c -> p (s c)")
        ovxT = xT[:, 0, :, :, 0:P]
        ovhh, ovhl = [v[:, 0, :, 0:P] for v in (hidh, hidl)]
        ove, ovhid = eg[:, 0:2 * P], hid[:, 0:2 * P]
        yg = [(w_reg[:, 2048 * t:2048 * (t + 1)] if t < 6 else mix_reg[:, 2048 * (t - 6):2048 * (t - 5)]).rearrange(
            "p (c d) -> p c d", c=2) for t in range(NT + 1)]
        fin = mix_reg[:, 6144:8192].rearrange("p (s d) -> p s d", s=2)

        def xt(t):
            return xin[:, t, :] if t < NT else xs

        s_x = [sem(f"x_in{i}") for i in range(4)]
        s_g1 = sem("gains_in")
        s_par = sem("parameters_in")
        s_const = sem("consts")
        s_dv = sem("vector_chain")
        s_ac = sem("scalar_chain")
        s_pl = sem("pool_chain")
        s_ss = sem("x_then_gla_squares")
        s_ms = sem("mean_squares")
        s_rs = sem("rstds")
        s_xn = sem("x_normed")
        s_xT = sem("x_transposed")
        s_hh = sem("h_hi")
        s_hl = sem("h_lo")
        s_w = [sem(f"w_stage{i}") for i in range(2)]
        s_wh = sem("w_hi")
        s_wl = sem("w_lo")
        s_mm = sem("proj_unit")
        s_ev = [sem(f"proj_bank_free{i}") for i in range(PB)]
        s_hi = sem("proj_hi")
        s_z = sem("gla_z")
        s_zr = sem("gla_z_read")
        s_ln = sem("gla_ln")
        s_arg = sem("gla_args")
        s_qz = sem("gla_q_zeroed")
        s_exp = sem("gla_exps")
        s_prep = sem("gla_operands")
        s_sc = sem("gla_scores")
        s_scm = sem("gla_scores_masked")
        s_kdn = sem("gla_k_natural")
        s_o = sem("gla_out")
        s_S = sem("gla_state")
        s_oev = sem("gla_out_read")
        s_st = sem("state_in")
        s_ks = sem("gla_sample_k_then_out")
        s_km = sem("gla_sample_kmask")
        s_op = sem("gla_sample_outer")
        s_sn = sem("gla_sample_state")
        s_osr = sem("gla_sample_out_read")
        s_ge = sem("gate_sigmoid")
        s_glag = sem("gla_gains_scaled")
        s_gs = sem("gate_steps_pool")
        s_mx = sem("gla_mixed")
        s_mT = sem("mix_transposed")
        s_mh = sem("mix_hi")
        s_ml = sem("mix_lo")
        s_kn = sem("k_natural")
        s_knr = sem("k_natural_read")
        s_kout = [sem(f"k_out{i}") for i in range(4)]
        s_out = sem("outputs")

        s_ldot = sem("lambda_dots")
        s_lexp = sem("lambda_exps")
        s_spout = sem("state_prompt_out")
        s_qd = sem("q_scratch_out")
        s_snew = sem("new_key_scores")
        s_snin = sem("new_key_scores_placed")
        s_qb = [sem(f"q_broadcast_in{i}") for i in range(2)]
        s_kp = [sem(f"pages_in{i}") for i in range(2)]
        s_kq = sem("pages_times_q")
        s_kh = sem("page_scores")
        s_acc = sem("weighted_values")
        s_acd = sem("weighted_values_vector")
        s_ds = sem("decode_key_sums")
        s_qk = sem("scores")
        s_nm = sem("scores_max")
        s_p = sem("probs")
        s_wc = sem("probs_combined")
        s_wT = sem("probs_transposed")
        s_wTe = sem("probs_transposed_read")
        s_pv = sem("attn_out")
        s_dsq = sem("attn_squares")
        s_dn = sem("attn_normed")
        s_dsz = sem("decode_scores_cleared")
        s_wrs = sem("router_split")
        s_s1 = sem("gate_steps")
        s_wo = [sem(f"w_out_stage{i}") for i in range(2)]
        s_woh = sem("w_out_hi")
        s_wol = sem("w_out_lo")
        s_dec = sem("decode_vector_steps")
        s_deca = sem("decode_exp_and_square")
        s_mbb = sem("decode_max_all")
        s_wni = sem("decode_new_weights_in")
        s_vp = [sem(f"v_pages_in{i}") for i in range(2)]
        s_xr = [sem(f"x_again{i}") for i in range(2)]
        s_om = sem("out_proj")
        s_x1 = sem("x_plus_mixer")
        s_x1q = sem("x1_squares")
        s_h2 = sem("h2_normed")
        s_h2h = sem("h2_hi")
        s_h2l = sem("h2_lo")
        s_h2o = [sem(f"h2_out{i}") for i in range(2)]
        s_h2T = sem("h2_transposed")
        s_hTh = sem("h2T_hi_read")
        s_rt = sem("router_products")
        s_rtr = sem("router_read")
        s_re = sem("route_exp_in")
        s_rex = sem("route_exp")
        s_rc = sem("route_counts")
        s_rs1 = sem("route_onehots")
        s_rsu = sem("route_onehots_used")
        s_route = sem("routed")
        s_mw = [sem(f"gate_up_stage{i}") for i in range(2)]
        s_mwd = [sem(f"down_stage{i}") for i in range(2)]
        s_mh2 = sem("gate_up_hi")
        s_mhd = sem("down_hi")
        s_mlo = sem("gate_up_lo")
        s_mld = sem("down_lo")
        s_gx = [sem(f"tokens_in{i}") for i in range(2)]
        s_eT = sem("tokens_transposed")
        s_ea = sem("tokens_read_act")
        s_ev2 = sem("tokens_read_vec")
        s_gup = sem("gate_up")
        s_sg = sem("gate_exp_moe")
        s_hf = sem("hidden")
        s_hh2 = sem("hidden_hi")
        s_hl2 = sem("hidden_lo")
        s_down = sem("down")
        s_ya = sem("y_read_act")
        s_yv = sem("y_read_vec")
        s_yo = [sem(f"y_out{i}") for i in range(2)]
        s_ovw = sem("overflow_weights_in")
        s_ovx = sem("overflow_tokens_in")
        s_ovy = sem("overflow_out")
        s_ova = sem("overflow_scalar_steps")
        s_ovv = sem("overflow_vector_steps")
        s_ovp = sem("overflow_tensor_steps")
        s_yg = [sem(f"y_gathered{i}") for i in range(3)]
        s_fq = sem("final_sum")
        s_fs = sem("final_square")
        s_fo = sem("final_normed")
        s_fout = [sem(f"final_out{i}") for i in range(2)]

        qd = nc.dram_tensor("q_scratch", [NB, 512], F32, kind="Internal").ap()
        h2d = nc.dram_tensor("h2_scratch", [T, 2 * D], F16, kind="Internal").ap()
        yd = nc.dram_tensor("y_scratch", [NE * CAP, D], F32, kind="Internal").ap()
        od = nc.dram_tensor("overflow_scratch", [NOV * P, D], F32, kind="Internal").ap()
        ck = I["cache_k"][0].rearrange("n p h e -> n p (h e)")
        cv = I["cache_v"][0].rearrange("n p h e -> n p (h e)")
        n_pool = I["cache_k"].shape[1]
        w_o = I["w_out"][0].rearrange("(k p) n -> p k n", p=P)

        UN = NT * H
        KHALF = NPG // 2
        PSEQ = 5
        VSTEPS = (4, 5)

        def value_steps_to(k):
            return sum(VSTEPS[j % 2] for j in range(k + 1))


        WO_AT = (3, 6, 9, 12)

        def fills(u):
            return (u // H + 1 + 3) // 4

        FILL0 = [sum(fills(v) for v in range(u)) for u in range(UN + 1)]

        def score_bank(u, m):
            return 2 * (u % 2) + m if u < 16 else 2 * m

        def scores(u, m):
            n = (u // H + 1) * P
            b = score_bank(u, m)
            return ps[:, b:b + 2].rearrange("p b c -> p (b c)")[:, 0:n] if n > 512 else ps[:, b, 0:n]

        REQ = [("d", i) for i in range(NT)] + [("x", t) for t in range(NB - PSEQ + 2)] + [("dec", 0)] \
            + [("x", t) for t in range(NB - PSEQ + 2, NT + 1)] \
            + [("f", t) for t in range(NT + 1)]

        def rcol(kind, t):
            if kind == "d":
                return slice(0, P), slice(4 * t, 4 * t + 4)
            if kind == "dec":
                return slice(0, NB), slice(36, 40)
            c = {"x": 0, "f": 16}[kind] + t
            return slice(0, rows(t)), slice(c, c + 1)

        kvf = kv[:].rearrange("p s c -> p (s c)")
        taken = [0]

        def work(*shape):
            n = math.prod(shape)
            v = kvf[:, taken[0]:taken[0] + n]
            taken[0] += n
            if len(shape) == 2:
                v = v.rearrange("p (a b) -> p a b", a=shape[0])
            return v

        r_m, r_s, r_pt, r_mi, r_m1, r_m2, dd, r_tokv, r_valid = [work(9) for _ in range(9)]
        eg4, r_cand, ohg, r_le, oh1, oh2 = [work(9, 4) for _ in range(6)]
        r_prod = work(9, 16)
        cho = work(18, 16)
        r_tmp = work(18, 16)
        r_a, r_pos = work(9, 16), work(9, 16)
        r_ne, r_oc, r_inc, r_ost = [work(16) for _ in range(4)]
        r_thr = work(8)
        r_cmp = work(16, 8)
        r_cmj = work(NOV, 16)
        r_r, r_e, r_o, r_g, r_f, r_q, r_p, r_c, r_po, r_co, r_x, r_y = [work(18) for _ in range(12)]
        r_q3 = work(18, 8)
        r_tv = work(18)
        oneh_p = work(18 * P // 2).bitcast(F16).rearrange("p (n q) -> p n q", n=18)
        oneh_c = work(18 * COLS // 2).bitcast(F16).rearrange("p (n c) -> p n c", n=18)
        iom = work(4)
        r_oe = work(NOV + 1)

        def expert_parts(s, lo):
            dst = (egl, eul, edl) if lo else (egh, euh, edh)
            return [(dst[j][s], mst[s][:, 2048 * j:2048 * (j + 1)].rearrange("p (k f) -> p k f", k=2 if j == 2 else KC),
                     (egh, euh, edh)[j][s]) for j in range(3)]

        x_p = I["x_prompt"][0].rearrange("(t p) d -> t p d", p=P)
        x_s = I["x_sample"].rearrange("b l d -> (b l) d")
        w_in = I["w_in"][0].rearrange("(k p) n -> p k n", p=P)
        state = I["state_gla"][0].rearrange("b (a h) k v -> a (h k) b v", a=2)

        def w_stage(n):
            wd = HALVES[n][2]
            return stage[n % 2][:, 0:KC * wd].rearrange("p (k n) -> p k n", k=KC)

        def w_slot(sl, n):
            g, _, wd, off = HALVES[n]
            return sl[g % 2][:, :, off:off + wd]

        def bank16(b):
            return ps[:, b, :].bitcast(F16)

        def plain_target(g, blk, j):
            u = UNIT_AT[(g, blk, j)]
            if g == GQK:
                dst = (gq if blk < 2 else gk)[:, blk % 2, CH * j:CH * (j + 1)]
                return dst, ps[:, BANK[u], 0:CH]
            if g == CODE:
                return code[:, CH * j:CH * (j + 1)], ps[0:RANK, BANK[u], 0:CH]
            r = rows(blk)
            return {GV: gv, DVG: vd}[g][0:r, blk, :], ps[0:r, BANK[u], :]

        def plain_scale(g, blk):
            return ISC2 * (DK ** -0.5 if g == GQK and blk < 2 else 1.0)

        def mix_hi(act, n, t, half):
            r = rows(t)
            act.wait_ge(s_mT, n + 1)
            act.activation(mixh[:, 4 * half:4 * half + 4, span(t)],
                           ps[:, 4 + n % 2, 0:4 * r].rearrange("p (k t) -> p k t", k=4),
                           ACT.Copy).then_inc(s_mh, 1)

        def mix_lo(dve, n, t, half):
            r = rows(t)
            ks = slice(4 * half, 4 * half + 4)
            dve.wait_ge(s_mh, n + 1)
            dve.tensor_tensor(mixl[:, ks, span(t)],
                              ps[:, 4 + n % 2, 0:4 * r].rearrange("p (k t) -> p k t", k=4),
                              mixh[:, ks, span(t)], ALU.subtract).then_inc(s_ml, 1)

        def attn_hi_on(act, i):
            act.wait_ge(s_mT, MIXED + i + 1)
            act.activation(mixh[:, 4:8, span(i)], ps[:, 6 + i % 2, :].rearrange("p (k t) -> p k t", k=4),
                           ACT.Copy).then_inc(s_mh, 1)

        def attn_lo_on(dve, i):
            dve.wait_ge(s_mh, MIXED + i + 1)
            dve.tensor_tensor(mixl[:, 4:8, span(i)], ps[:, 6 + i % 2, :].rearrange("p (k t) -> p k t", k=4),
                              mixh[:, 4:8, span(i)], ALU.subtract).then_inc(s_ml, 1)

        def when_overflow(eng, body):
            eng.wait_ge(s_route, 1)
            eng.wait_ge(s_yo[0], 16 * NE)
            eng.wait_ge(s_yo[1], 16 * NE)
            tiles = eng.value_load(oexp[0:1, NOV:NOV + 1], min_val=0, max_val=NOV)
            with eng.If(tiles > 0):
                body()

        def run_slots(eng, slot):
            for e in range(3):
                slot(0, e, e)
            with eng.Fori(1, NE // 2 - 2) as i:
                slot(i, 1)
                slot(i, 2)
            for e in range(NE - 3, NE + 1):
                slot((e - 1) // 2, e - 2 * ((e - 1) // 2), e)

        block = ctx.enter_context(nc.Block())

        @block.sync
        def _(sp):
            for t in range(NT + 1):
                sp.dma_start(xt(t), x_p[t] if t < NT else x_s).then_inc(s_x[X_GROUP[t][0]], 16)

            def load_half(n):
                if n >= 2:
                    sp.wait_ge(s_wl, n - 1)
                _, c0, wd, _ = HALVES[n]
                sp.dma_start(w_stage(n), w_in[:, :, c0:c0 + wd]).then_inc(s_w[n % 2], 16)

            for n in range(HALVES_TO[DQ]):
                load_half(n)
            sp.wait_ge(s_z, 6)
            for a in range(2):
                sp.dma_start(st[:, a], state[a]).then_inc(s_st, 16)
            for n in range(HALVES_TO[DQ], len(HALVES)):
                load_half(n)
            sp.wait_ge(s_S, 2 * NT)
            for h in range(H):
                hp = slice(64 * (h % 2), 64 * (h % 2) + 64)
                sp.dma_start(O["gla_prompt"][0, 0, h], sbd[hp, h // 2, h % 2, :]).then_inc(s_spout, 16)
            sp.wait_ge(s_sn, NB)
            for a in range(2):
                sp.dma_start(O["gla_sample"][0].rearrange("b (a h) k v -> a (h k) b v", a=2)[a],
                             st[:, a]).then_inc(s_out, 16)
            def pages(cache, n, sems):
                b, half = n // 2, n % 2
                for g in range(KHALF):
                    i = NPG * b + KHALF * half + g
                    page = sp.value_load(ptab[0:1, i:i + 1], min_val=0, max_val=n_pool - 1)
                    sp.dma_start(kv[:, n % 2, 512 * g:512 * g + 512],
                                 cache[bass.ds(page, 1)].rearrange("n p c -> p (n c)")).then_inc(sems[n % 2], 16)

            def load_wo(c):
                if c >= 2:
                    sp.wait_ge(s_wol, c - 1)
                else:
                    sp.wait_ge(s_wl, len(HALVES))
                sp.dma_start(stage[c % 2].rearrange("p (k n) -> p k n", k=2),
                             w_o[:, 2 * c:2 * c + 2]).then_inc(s_wo[c % 2], 16)

            load_wo(0)
            load_wo(1)
            sp.wait_ge(s_par, 16 * N_PAR)
            sp.wait_ge(s_qd, 16)
            sp.wait_ge(s_out, 32)
            for n in range(2 * NB):
                if n >= 2:
                    sp.wait_ge(s_kh, n - 1)
                if n % 2 == 0:
                    if n >= 4:
                        sp.wait_ge(s_kh, n - 2)
                    sp.dma_start(qbc[:, n // 2 % 2], qd[n // 2].partition_broadcast(P)).then_inc(s_qb[n // 2 % 2], 16)
                pages(ck, n, s_kp)
            sp.wait_ge(s_dsz, 1)
            sp.wait_ge(s_snew, 1)
            with nc.allow_non_contiguous_dma(reason="64 scores"):
                sp.dma_start(dsc[0:1, :, :, NPG].rearrange("p b m -> p (b m)"), snew[:]).then_inc(s_snin, 16)
            for t in range(NT + 1):
                u = UNIT_AT[(DVG, t, 0)]
                sp.wait_ge(s_ev[BANK[u]], NTH[u])
                dst = O["v_prompt"][0, 0, t * P:(t + 1) * P].rearrange("p h e -> p (h e)") if t < NT \
                    else O["v_sample"][0, :, 0].rearrange("b h e -> b (h e)")
                sp.dma_start(dst, vd[0:rows(t), t]).then_inc(s_out, 16)
            for n in range(2):
                sp.wait_ge(s_kh, 2 * NB - 1 + n)
                pages(cv, n, s_vp)
            load_wo(2)
            load_wo(3)
            for n in range(2, 2 * NB):
                if n < 2 * PSEQ:
                    sp.wait_ge(s_acc, value_steps_to(n - 2))
                    pages(cv, n, s_vp)
            sp.wait_ge(s_wTe, FILL0[UN])
            sp.wait_ge(s_pv, UN)
            for t in range(-2, NT + 1):
                if t + 2 <= NT:
                    if t >= 0:
                        sp.wait_ge(s_x1, 2 * (t + 1))
                    sp.dma_start(xr[0:rows(t + 2), t % 2], x_p[t + 2] if t + 2 < NT else x_s).then_inc(s_xr[t % 2], 16)
                for n in (2 * PSEQ, 2 * PSEQ + 1) if t == -1 else ():
                    sp.wait_ge(s_acc, value_steps_to(n - 2))
                    pages(cv, n, s_vp)
                for n in (2 * PSEQ + 2 + 2 * t, 2 * PSEQ + 3 + 2 * t):
                    if t >= 0 and n < 2 * NB:
                        sp.wait_ge(s_acd, H * KHALF * (n - 2 * PSEQ - 1))
                        pages(cv, n, s_vp)
                if t >= 0:
                    sp.wait_ge(s_h2h, t + 1)
                    sp.wait_ge(s_h2l, t + 1)
                    sp.dma_start(h2d[t * P:t * P + rows(t)], h2s[0:rows(t), t % 2]).then_inc(s_h2o[t % 2], 16)

            def load(w, sub, e, s, sems):
                src = I[w][0, bass.ds(e, 1)].rearrange("e (k p) f -> p (e k) f", p=P)
                sp.dma_start(mst[s][:, 2048 * sub:2048 * (sub + 1)].rearrange("p (k f) -> p k f", k=src.shape[1]),
                             src).then_inc(sems[s], 16)

            def load_gate_up(e, s):
                load("w_gate", 0, e, s, s_mw)
                load("w_up", 1, e, s, s_mw)

            def load_down(e, s):
                load("w_down", 2, e, s, s_mwd)

            def slot(i, off, e=None):
                s = off % 2
                if e is None or e + 3 < NE:
                    sp.wait_ge(s_mlo, 4 * i + (2 * off + 4))
                    load_gate_up(2 * i + (off + 3), 1 - s)
                if e is None or e + 2 < NE:
                    sp.wait_ge(s_mld, 2 * i + (off + 1))
                    load_down(2 * i + (off + 2), s)
                if e != 0:
                    sp.wait_ge(s_ya, 2 * i + off)
                    sp.wait_ge(s_yv, 2 * i + off)
                    for g, r in ((0, P), (1, CAP1)):
                        sp.dma_start(yd[bass.ds((2 * i + (off - 1)) * CAP + P * g, r)],
                                     yb[0:r, 1 - s, D * g:D * g + D]).then_inc(s_yo[1 - s], 16)

            sp.wait_ge(s_om, 2 * (NT + 1))
            for e in range(2):
                load_gate_up(e, e)
                load_down(e, e)
            sp.wait_ge(s_mlo, 2)
            load_gate_up(2, 0)
            run_slots(sp, slot)
            def overflow():
                sp.wait_ge(s_ovv, 1)
                for j in range(NOV):
                    sp.dma_start(od[P * j:P * j + P], junk[:]).then_inc(s_ovy, 16)
                with sp.Fori(0, NOV) as j:
                    sp.wait_ge(s_ovy, 16 * j + 16 * NOV)
                    e = sp.value_load(oexp[0:1, bass.ds(j, 1)], min_val=0, max_val=NE - 1)
                    for i, w in enumerate((I["w_gate"], I["w_up"], I["w_down"])):
                        src = w[0, bass.ds(e, 1)].rearrange("e (k p) f -> p (e k) f", p=P)
                        sp.dma_start(mst[0][:, 2048 * i:2048 * (i + 1)].rearrange("p (k f) -> p k f", k=src.shape[1]),
                                     src).then_inc(s_ovw, 16)
                    sp.wait_ge(s_ova, len(OV_ACT) * j + OV_ACT["y"])
                    sp.wait_ge(s_ovv, len(OV_VEC) * j + (1 + OV_VEC["y"]))
                    sp.dma_start(od[bass.ds(j * P, P)], yb[:, 0, 0:D]).then_inc(s_ovy, 16)

            when_overflow(sp, overflow)
            for t in range(NT + 1):
                sp.wait_ge(s_fo, t + 1)
                dst = O["y_prompt"][0, t * P:(t + 1) * P] if t < NT else O["y_sample"].rearrange("b l d -> (b l) d")
                sp.dma_start(dst, fin[0:rows(t), t % 2]).then_inc(s_fout[t % 2], 16)
            sp.wait_ge(s_fout[0], 16 * 5)
            sp.wait_ge(s_fout[1], 16 * 4)
            sp.wait_ge(s_out, 16 * (NT + 3))
            sp.wait_ge(s_spout, 16 * H)

        @block.gpsimd
        def _(pool):
            chain = [0]

            def link(ins):
                chain[0] += 1
                ins.then_inc(s_pl, 1)
                pool.wait_ge(s_pl, chain[0])

            for m in (ident, maskneg, gs_reg, diagm, sel):
                pool.memset(m[:], 0.0)
            pool.memset(mask_ji[:], 1.0)
            pool.memset(neghalf[:], -0.5)
            link(pool.memset(ones[:], 1.0))
            pool.affine_select(out=ident[:], in_=ident[:], compare_op=ALU.not_equal, fill=1.0, base=0,
                               pattern=[[-1, P]], channel_multiplier=1)
            pool.affine_select(out=maskneg[:], in_=maskneg[:], compare_op=ALU.is_ge, fill=-BIG, base=0,
                               pattern=[[-1, P]], channel_multiplier=1)
            pool.affine_select(out=mask_ji[:], in_=mask_ji[:], compare_op=ALU.is_ge, fill=0.0, base=0,
                               pattern=[[1, P]], channel_multiplier=-1)
            pool.memset(sel[:, NB - 1:NB], 1.0)
            pool.iota(iof[:], pattern=[[1, P]], base=0, channel_multiplier=0, allow_small_or_imprecise_dtypes=True)
            pool.iota(tokid[:], pattern=[[P, 9]], base=0, channel_multiplier=1, allow_small_or_imprecise_dtypes=True)
            pool.memset(lg[:], 0.0)
            pool.affine_select(out=diagm[:], in_=diagm[:], compare_op=ALU.not_equal, fill=1.0, base=0,
                               pattern=[[0, 2], [1, NB], [-1, NB]], channel_multiplier=0).then_inc(s_const, 1)
            for t in range(NT + 1):
                r = rows(t)
                pool.wait_ge(s_ms, t + 1)
                pool.tensor_tensor(rst[0:r, t:t + 1], rst[0:r, t:t + 1], neghalf[0:r, 0:1],
                                   ALU.pow).then_inc(s_rs, 1)
            pool.wait_ge(s_xT, NT + 1)
            pool.memset(qa, 0.0)
            pool.memset(qb, 0.0).then_inc(s_qz, 1)
            pool.wait_ge(s_par, 16 * N_PAR)
            pool.wait_ge(s_glag, 1)
            for t in range(NT + 1):
                r = rows(t)
                g, e = gate[t][0:r], gt[0:r, t % 2]
                pool.wait_ge(s_ge, t + 1)
                pool.tensor_tensor(g, g, e, ALU.mult).then_inc(s_gs, 1)
                pool.wait_ge(s_gs, 2 * t + 1)
                g4 = g.rearrange("p (h v) -> p h v", h=H)
                pool.tensor_tensor(g4, g4, glag[0:r].unsqueeze(1).to_broadcast([r, H, DV]), ALU.mult).then_inc(s_gs, 1)
            pool.wait_ge(s_ms, NT + 2)
            pool.tensor_tensor(rst[:, 0:32], rst[:, 0:32], neghalf[:, 0:32], ALU.pow).then_inc(s_rs, 1)
            pool.wait_ge(s_ms, NT + 3)
            pool.tensor_tensor(rst[0:NB, 32:36], rst[0:NB, 32:36], neghalf[0:NB, 32:36],
                               ALU.pow).then_inc(s_rs, 1)
            for n in range(2 * NB):
                b = n // 2
                pg = kv[:, n % 2].rearrange("p (g c) -> p g c", g=KHALF)
                pool.wait_ge(s_kp[n % 2], 64 * (n // 2 + 1))
                pool.wait_ge(s_qb[b % 2], 16 * (b // 2 + 1))
                pool.tensor_tensor(pg, pg, qbc[:, b % 2].unsqueeze(1).to_broadcast([P, KHALF, 512]),
                                   ALU.mult).then_inc(s_kq, 1)

            def power(kind, t):
                pool.wait_ge(s_ms, NT + 3 + REQ.index((kind, t)) + 1)
                pr, cr = rcol(kind, t)
                pool.tensor_tensor(rst[pr, cr], rst[pr, cr], neghalf[pr, cr], ALU.pow).then_inc(s_rs, 1)

            pool.wait_ge(s_dec, DEC["max"])
            pool.partition_all_reduce(dmb[:], dmx[:], P, bass.bass_isa.ReduceOp.max).then_inc(s_mbb, 1)
            pool.wait_ge(s_dec, DEC["sums"])
            pool.partition_all_reduce(dmb[:], dmx[:], P, bass.bass_isa.ReduceOp.add).then_inc(s_mbb, 1)
            def value_steps(k):
                b, half = k // 2, k % 2
                pg = kv[:, k % 2].rearrange("p (g h v) -> p g h v", g=KHALF, h=H)
                w = dw[:, b, :, KHALF * half:KHALF * half + KHALF].rearrange("p h g -> p g h")
                two = kv[:, k % 2].rearrange("p (g c) -> p g c", g=KHALF)
                for j in (0, 2):
                    yield pg[:, j:j + 2], pg[:, j:j + 2], w[:, j:j + 2].unsqueeze(3).to_broadcast([P, 2, H, DV]), ALU.mult
                yield two[:, 0:2], two[:, 0:2], two[:, 2:4], ALU.add
                if half == 0:
                    yield dacc[:, b], two[:, 0], two[:, 1], ALU.add
                else:
                    yield two[:, 0], two[:, 0], two[:, 1], ALU.add
                    yield dacc[:, b], dacc[:, b], two[:, 0], ALU.add

            steps = [(k, i == 0, x) for k in range(2 * PSEQ) for i, x in enumerate(value_steps(k))]
            done = 0
            for i in range(NT):
                power("d", i)
                if i == 1:
                    pool.wait_ge(s_wol, KC // 2)
                    pool.wait_ge(s_dec, DEC["new_weights"])
                upto = len(steps) * i // (NT - 2) if i < NT - 1 else len(steps)
                for n in range(done, min(upto, len(steps))):
                    k, first, (out, in0, in1, op) = steps[n]
                    if first:
                        pool.wait_ge(s_vp[k % 2], 64 * (k // 2 + 1))
                    if n:
                        pool.wait_ge(s_acc, n)
                    pool.tensor_tensor(out, in0, in1, op).then_inc(s_acc, 1)
                done = upto
            for r in REQ[NT:REQ.index(("f", 0))]:
                power(*r)

            def split_first(done, s, part):
                dst, src, hi = expert_parts(s, 1)[part]
                pool.tensor_tensor(dst, src, hi, ALU.subtract).then_inc(done, 1)

            for part in range(2):
                pool.wait_ge(s_mh2, part + 1)
                split_first(s_mlo, 0, part)
            pool.wait_ge(s_mhd, 1)
            split_first(s_mld, 0, 2)
            def gather(e):
                if e >= 2:
                    pool.wait_ge(s_eT, 4 * (e - 1))
                for g, r in ((0, P), (1, CAP1)):
                    pool.indirect_dma_start(out=xg[0:r, e % 2, g, :], out_offset=None, in_=h2d[:, :],
                                            in_offset=bass.IndirectOffsetOnAxis(ap=tok[0:r, 2 * e + g:2 * e + g + 1],
                                                                                axis=0)).then_inc(s_gx[e % 2], 16)

            pool.wait_ge(s_route, 1)
            pool.wait_ge(s_h2o[0], 16 * 5)
            pool.wait_ge(s_h2o[1], 16 * 4)
            gather(0)
            gather(1)
            for part in range(2):
                pool.wait_ge(s_mh2, part + 3)
                split_first(s_mlo, 1, part)
            for e in range(2, NE):
                gather(e)

            def overflow():
                for j in range(NOV):
                    pool.wait_ge(s_ovy, 16 * (NOV + j))
                    pool.indirect_dma_start(out=xg[:, 0, 0, :], out_offset=None, in_=h2d[:, :],
                                            in_offset=bass.IndirectOffsetOnAxis(
                                                ap=tok[:, 2 * NE + j:2 * NE + j + 1], axis=0)).then_inc(s_ovx, 16)
                pool.wait_ge(s_ovy, 32 * NOV)
                for t in range(NT + 1):
                    if t:
                        pool.wait_ge(s_ovv, 1 + len(OV_VEC) * NOV + 2 * t)
                    for c in range(2):
                        pool.indirect_dma_start(out=yg[0][0:rows(t), c], out_offset=None, in_=od[:, :],
                                                in_offset=bass.IndirectOffsetOnAxis(ap=orow[0:rows(t), c, t:t + 1],
                                                                                    axis=0)).then_inc(s_ovx, 16)
                pool.wait_ge(s_ovv, 1 + len(OV_VEC) * NOV + 2 * (NT + 1))

            when_overflow(pool, overflow)

            def gather_y(t):
                for c in range(2):
                    pool.indirect_dma_start(out=yg[t][0:rows(t), c], out_offset=None, in_=yd[:, :],
                                            in_offset=bass.IndirectOffsetOnAxis(ap=yrow[0:rows(t), c, t:t + 1], axis=0)
                                            ).then_inc(s_yg[t % 3], 16)

            for t in range(NT + 1):
                if t >= 3:
                    pool.wait_ge(s_yg[t % 3], 32 * (t // 3))
                gather_y(t)
                if t >= 3:
                    power("f", t - 3)
            for t in range(NT - 2, NT + 1):
                power("f", t)

        @block.scalar
        def _(act):
            chain = [0]

            def link(ins):
                chain[0] += 1
                ins.then_inc(s_ac, 1)
                act.wait_ge(s_ac, chain[0])

            with nc.allow_non_contiguous_dma(reason="small parameters"):
                act.dma_start(gbc[:], I["norm1_g"][0].partition_broadcast(P)).then_inc(s_g1, 16)
                act.dma_start(ba_col[:], I["b_a"][0].rearrange("(a p) -> p a", p=P)).then_inc(s_par, 16)
                act.dma_start(glag[:], I["gla_norm_g"][0].partition_broadcast(P)).then_inc(s_par, 16)
                act.dma_start(wa2[:], I["w_a2"][0]).then_inc(s_par, 16)
                act.dma_start(ptab[:], I["page_table"].rearrange("b g -> (b g)").unsqueeze(0)).then_inc(s_par, 16)
                for i, n in enumerate(("lambda_q1", "lambda_k1", "lambda_q2", "lambda_k2")):
                    act.dma_start(lams[:, i], I[n][0].partition_broadcast(P)).then_inc(s_par, 16)
                act.dma_start(dgain[:], I["diff_norm_g"][0].partition_broadcast(P)).then_inc(s_par, 16)
                act.dma_start(wr[:, :, 0:NG], I["w_router_g"][0].rearrange("(k p) g -> p k g", p=P)).then_inc(s_par, 16)
                for g in range(NG):
                    act.dma_start(wr[:, :, NG + EPG * g:NG + EPG * (g + 1)],
                                  I["w_router_e"][0, g].rearrange("(k p) e -> p k e", p=P)).then_inc(s_par, 16)
                act.dma_start(br[:, 0:NG], I["b_router_g"][0].partition_broadcast(P)).then_inc(s_par, 16)
                act.dma_start(br[:, NG:], I["b_router_e"][0].rearrange("g e -> (g e)").partition_broadcast(P)
                              ).then_inc(s_par, 16)

            for t in range(NT + 1):
                r = rows(t)
                act.wait_ge(s_x[X_GROUP[t][0]], 16 * X_GROUP[t][1])
                if t:
                    act.wait_ge(s_ss, t)
                act.activation(junk[0:r, :], xt(t)[0:r], ACT.Square, accum_out=ss[0:r, t:t + 1]).then_inc(s_ss, 1)

            def split_w(n):
                g = HALVES[n][0]
                if g >= 2:
                    act.wait_ge(s_mm, UNITS_TO[g - 2])
                act.wait_ge(s_w[n % 2], 16 * (n // 2 + 1))
                act.activation(w_slot(slot_h, n), w_stage(n), ACT.Copy, scale=SC).then_inc(s_wh, 1)

            def split_group(g):
                for n in range(HALVES_TO[g - 1] if g else 0, HALVES_TO[g]):
                    split_w(n)

            split_group(0)
            for t in range(NT + 1):
                r = rows(t)
                for b in range(2):
                    bank = 4 + 2 * (t % 2) + b
                    act.wait_ge(s_xT, t + 1)
                    act.activation(hTh[:, 4 * b:4 * b + 4, span(t)],
                                   ps[:, bank, 0:4 * r].rearrange("p (k t) -> p k t", k=4),
                                   ACT.Copy).then_inc(s_hh, 1)

            def read_proj(g, blk, j, out, in_, scale, **kw):
                u = UNIT_AT[(g, blk, j)]
                act.wait_ge(s_mm, u + 1)
                return act.activation(out, in_, ACT.Copy, scale=scale, **kw), u

            def plain_reads(g):
                kind, _, wd = GROUPS[g]
                for (gg, blk, j) in UNITS:
                    u = UNIT_AT[(gg, blk, j)]
                    if gg != g or u % 2:
                        continue
                    act.wait_ge(s_mm, u + 1)
                    act.activation(*plain_target(g, blk, j), ACT.Copy,
                                   scale=plain_scale(g, blk)).then_inc(s_ev[BANK[u]], 1)

            act.wait_ge(s_xn, NT + 1)
            act.dma_start(gbc[:], I["norm2_g"][0].partition_broadcast(P)).then_inc(s_g1, 16)
            act.wait_ge(s_ldot, 1)
            act.activation(lamw[:, 2:4], lamw[:, 0:2], ACT.Exp).then_inc(s_lexp, 1)
            split_group(1)
            plain_reads(GQK)
            split_group(2)
            plain_reads(CODE)
            split_group(3)
            plain_reads(GV)

            def gate_read(t):
                r = rows(t)
                u = UNIT_AT[(GR, t, 0)]
                act.wait_ge(s_mm, u + 1)
                if t == 0:
                    act.wait_ge(s_ldot, 1)
                    act.wait_ge(s_xT, NT + 1)
                if t >= 2:
                    act.wait_ge(s_gs, 2 * (t - 1))
                act.activation(gt[0:r, t % 2], ps[0:r, BANK[u], :], ACT.Exp, scale=-ISC2)
                act.activation(gate[t][0:r], ps[0:r, BANK[u], :], ACT.Copy, scale=ISC2).then_inc(s_ev[BANK[u]], 1)
                act.wait_ge(s_ev[BANK[u]], NTH[u])
                link(act.activation(gt[0:r, t % 2], gt[0:r, t % 2], ACT.Ln, bias=1.0))
                act.activation(gt[0:r, t % 2], gt[0:r, t % 2], ACT.Exp, scale=-1.0).then_inc(s_ge, 1)

            for p in range(2):
                act.wait_ge(s_zr, 3 * p + 3)
                if p:
                    act.wait_ge(s_S, NT)
                link(act.activation(es, la, ACT.Abs))
                link(act.activation(es, es, ACT.Exp, scale=-1.0))
                act.activation(es, es, ACT.Ln, bias=1.0).then_inc(s_ln, 1)
                gate_read(4 * p)
                for i, buf in enumerate((ea, ek, eb, ed)):
                    act.wait_ge(s_arg, 4 * p + i + 1)
                    act.activation(buf, buf, ACT.Exp, scale=1.0 / TAU).then_inc(s_exp, 1)
                    if i == 1:
                        gate_read(4 * p + 1)
                act.activation(es, bc, ACT.Exp, scale=1.0 / TAU).then_inc(s_exp, 1)
                gate_read(4 * p + 2)
                gate_read(4 * p + 3)
                for c in range(NT + 1):
                    if c < NT:
                        n = p * NT + c
                        act.wait_ge(s_sc, n + 1)
                        if n >= 2:
                            act.wait_ge(s_o, n - 1)
                        act.activation(kdn[:, n % 2], ps[:, 2, 0:P], ACT.Copy).then_inc(s_kdn, 1)
                    if c >= 1:
                        n = p * NT + c - 1
                        act.wait_ge(s_o, n + 1)
                        act.activation(gv[:, c - 1, 256 * p:256 * p + 256], ps[:, 6 + n % 2, 0:256],
                                       ACT.Copy).then_inc(s_oev, 1)
                if p == 0:
                    split_group(DQ)
            gate_read(NT)
            act.wait_ge(s_ks, 2)
            act.activation(gv[0:NB, NT, :], ps[0:NB, 4, :], ACT.Copy).then_inc(s_osr, 1)
            act.wait_ge(s_oev, 2 * NT)
            act.wait_ge(s_osr, 1)
            for t in range(NT + 1):
                r = rows(t)
                for h in range(H):
                    if t or h:
                        act.wait_ge(s_ss, NT + 1 + H * t + h)
                    act.activation(junk[0:r, 0:DV], gv[0:r, t, DV * h:DV * h + DV], ACT.Square,
                                   accum_out=ss[0:r, H * t + h:H * t + h + 1]).then_inc(s_ss, 1)
            def split_reads(g, hi, after=None):
                for blk in range(4):
                    for j in range(3):
                        u = UNIT_AT[(g, blk, j)]
                        act.wait_ge(s_mm, u + 1)
                        act.activation(hi[:, blk, CH * j:CH * (j + 1)], ps[:, BANK[u], 0:CH], ACT.Copy,
                                       scale=SC * ISC2).then_inc(s_hi, 1)
                        if after:
                            after(3 * blk + j)

            def gated_hi(i):
                if 3 <= i < NT + 4:
                    mix_hi(act, i - 3, i - 3, 0)
                if i == 7:
                    split_group(DKG)

            split_reads(DQ, qdh, after=gated_hi)
            act.wait_ge(s_kn, 1)
            act.wait_ge(s_mT, NT + 1)
            act.activation(qn, ps[0:NB, 4, :], ACT.Copy, scale=1.0 / SC).then_inc(s_knr, 1)
            act.wait_ge(s_knr, 1)
            act.dma_start(qd, qn).then_inc(s_qd, 16)
            split_group(6)
            split_reads(DKG, kdh)
            for t in range(NT + 1):
                r = rows(t)
                u = UNIT_AT[(DVG, t, 0)]
                if u % 2 == 0:
                    act.wait_ge(s_mm, u + 1)
                    act.activation(*plain_target(DVG, t, 0), ACT.Copy, scale=ISC2).then_inc(s_ev[BANK[u]], 1)
                act.wait_ge(s_kn, t + 2)
                if t >= 4:
                    act.wait_ge(s_kout[t % 4], 16 * (t // 4))
                act.activation(knat[0:r, t % 4], ps[0:r, 4 + (t + 1) % 4, :], ACT.Copy,
                               scale=1.0 / SC).then_inc(s_knr, 1)
                act.wait_ge(s_knr, t + 2)
                dst = O["k_prompt"][0, 0, t * P:(t + 1) * P].rearrange("p h e -> p (h e)") if t < NT \
                    else O["k_sample"][0, :, 0].rearrange("b h e -> b (h e)")
                act.dma_start(dst, knat[0:r, t % 4]).then_inc(s_kout[t % 4], 16)
            for i in range(4):
                act.wait_ge(s_kout[i], 16 * (NT // 4 + (i == 0)))
            act.wait_ge(s_qd, 16)
            act.wait_ge(s_snew, 1)

            def split_wo(c):
                act.wait_ge(s_wo[c % 2], 16 * (c // 2 + 1))
                act.activation(woh[:, 2 * c:2 * c + 2], stage[c % 2].rearrange("p (k n) -> p k n", k=2), ACT.Copy,
                               scale=SC).then_inc(s_woh, 1)

            for u in range(UN + 7):
                if u < UN:
                    i, h = u // H, u % H
                    n = (i + 1) * P
                    for m in range(2):
                        act.wait_ge(s_nm, 2 * u + m + 1)
                        if u >= 3 and m == 0:
                            act.wait_ge(s_wT, FILL0[u - 2])
                        act.activation(prob[:, u % 3, m, 0:n], scores(u, m), ACT.Exp, scale=DK ** -0.5 * ISC2,
                                       bias=mxn[:, u % 2, m:m + 1],
                                       accum_out=rsum[:, i % 3, h, m:m + 1]).then_inc(s_p, 1)
                if 2 <= u < UN + 2:
                    v = u - 2
                    i = v // H
                    for f in range(fills(v)):
                        w = min(4, i + 1 - 4 * f)
                        act.wait_ge(s_wT, FILL0[v] + f + 1)
                        if v >= 2 and f == 0:
                            act.wait_ge(s_pv, v - 1)
                        act.activation(wT[:, v % 2, 4 * f:4 * f + w], ps[:, 4 + (FILL0[v] + f) % 2, 0:P * w].rearrange(
                            "p (j q) -> p j q", j=w), ACT.Copy).then_inc(s_wTe, 1)
                if u in WO_AT:
                    split_wo(WO_AT.index(u))
                if u == 4:
                    act.wait_ge(s_dec, DEC["exp_in"])
                    act.activation(dsc, dsc, ACT.Exp, scale=DK ** -0.5).then_inc(s_deca, 1)
                if u == 8:
                    act.wait_ge(s_dec, DEC["new_weights"])
                    with nc.allow_non_contiguous_dma(reason="32 weights"):
                        act.dma_start(wn[:], dmx[0:1, 0:4 * NB]).then_inc(s_wni, 16)
                if u % H == 3 and 7 <= u < UN + 7:
                    i = (u - 7) // H
                    act.wait_ge(s_pv, H * (i + 1))
                    for h in range(H):
                        if i or h:
                            act.wait_ge(s_dsq, H * i + h)
                        act.activation(junk[:, 0:DV], ps[:, 6 + i % 2, DV * h:DV * h + DV], ACT.Square,
                                       scale=rinv[:, i % 3, h, 0:1], accum_out=ss[:, 4 * i + h:4 * i + h + 1]
                                       ).then_inc(s_dsq, 1)
                if u % H == 2 and 10 <= u:
                    attn_hi_on(act, (u - 10) // H)
            for t in range(NT + 2):
                if t <= NT:
                    r = rows(t)
                    act.wait_ge(s_x1, 2 * (t + 1))
                    if t == NB - PSEQ + 2:
                        act.wait_ge(s_deca, 1 + H)
                    elif t:
                        act.wait_ge(s_x1q, t)
                    else:
                        act.wait_ge(s_dsq, UN)
                    act.activation(junk[0:r], x1[0:r, t], ACT.Square, accum_out=ss[0:r, t:t + 1]).then_inc(s_x1q, 1)
                    act.wait_ge(s_h2, t + 1)
                    if t >= 2:
                        act.wait_ge(s_h2o[t % 2], 16 * (t // 2))
                        act.wait_ge(s_h2T, t - 1)
                    act.activation(h2s[0:r, t % 2, 0:D], h2[0:r, t % 2], ACT.Copy).then_inc(s_h2h, 1)
                if t == NB - PSEQ + 1:
                    act.wait_ge(s_dec, DEC["out"])
                    act.wait_ge(s_x1q, t + 1)
                    for h in range(H):
                        if h:
                            act.wait_ge(s_deca, 1 + h)
                        act.activation(junk[0:NB, 0:DV], dod[:, DV * h:DV * h + DV], ACT.Square,
                                       accum_out=ss[0:NB, 36 + h:37 + h]).then_inc(s_deca, 1)
                if t == NB - PSEQ + 3:
                    act.wait_ge(s_mT, MIXED + NT + 1)
                    act.activation(mixh[:, 4:8, SEQ:T], ps[:, 7, 0:4 * NB].rearrange("p (k b) -> p k b", k=4),
                                   ACT.Copy).then_inc(s_mh, 1)
                if t >= 1:
                    v = t - 1
                    r = rows(v)
                    act.wait_ge(s_h2T, v + 1)
                    if v >= 2:
                        act.wait_ge(s_rt, v - 1)
                    act.activation(h2T[:, v % 2, 0, :, 0:r], bank16(4)[:, 0:8 * r].rearrange("p (k t) -> p k t", k=KC),
                                   ACT.Copy)
                    act.activation(h2T[:, v % 2, 1, :, 0:r], bank16(5)[:, 0:8 * r].rearrange("p (k t) -> p k t", k=KC),
                                   ACT.Copy).then_inc(s_hTh, 1)
            act.wait_ge(s_h2, NT + 1)
            act.dma_start(gbc[:], I["norm_f_g"].partition_broadcast(P)).then_inc(s_g1, 16)
            for i in range(2):
                act.wait_ge(s_re, i + 1)
                act.activation(*((eg4, eg4) if i == 0 else (dd, dd)), ACT.Exp).then_inc(s_rex, 1)

            def split_gate_up(s, loaded):
                act.wait_ge(s_mw[s], loaded)
                for dst, src, _ in expert_parts(s, 0)[0:2]:
                    act.activation(dst, src, ACT.Copy, scale=SC).then_inc(s_mh2, 1)

            def split_down(s, loaded):
                act.wait_ge(s_mwd[s], loaded)
                dst, src, _ = expert_parts(s, 0)[2]
                act.activation(dst, src, ACT.Copy, scale=SC).then_inc(s_mhd, 1)

            def read_tokens(s, f, n):
                act.wait_ge(s_eT, n)
                act.activation(xT[:, s, f // 2, 4 * (f % 2):4 * (f % 2) + 4],
                               bank16(0)[:, 0:4 * CAP].rearrange("p (k t) -> p k t", k=4), ACT.Copy).then_inc(s_ea, 1)

            def slot(i, off, e=None):
                s = off % 2

                def at(k, c):
                    return k * 2 * i + (k * off + c)

                if e != NE:
                    act.wait_ge(s_gup, at(1, 1))
                    act.activation(eg, ps[:, 2, 0:2 * CAP], ACT.Exp, scale=-ISC2).then_inc(s_sg, 1)
                    if e != NE - 1:
                        read_tokens(1 - s, 0, at(4, 5))
                        read_tokens(1 - s, 2, at(4, 7))
                    act.wait_ge(s_hf, at(1, 1))
                    act.activation(hidh[:, s], hid.rearrange("p (f t) -> p f t", f=2), ACT.Copy).then_inc(s_hh2, 1)
                if e != 0:
                    if e is None or e >= 3:
                        act.wait_ge(s_yo[1 - s], 32 * i + 32 * ((off - 1) // 2))
                    act.wait_ge(s_down, at(4, -3))
                    act.activation(yb[:, 1 - s, 0:512], ps[:, 4, :], ACT.Copy, scale=ISC2)
                    act.wait_ge(s_down, at(4, -1))
                    act.activation(yb[0:CAP1, 1 - s, D:D + 512], ps[0:CAP1, 6, :], ACT.Copy, scale=ISC2).then_inc(s_ya, 1)
                if e is None or e + 2 < NE:
                    split_gate_up(s, 32 * i + 32 * ((off + 2) // 2 + 1))
                if e is None or e + 1 < NE:
                    if e != 0:
                        act.wait_ge(s_down, at(4, 0))
                    split_down(1 - s, 16 * i + 16 * ((off + 1) // 2 + 1))

            for s, part, loaded, n, done in ((0, 0, s_mw, 32, s_mh2), (0, 1, s_mw, 32, s_mh2), (0, 2, s_mwd, 16, s_mhd),
                                             (1, 0, s_mw, 32, s_mh2), (1, 1, s_mw, 32, s_mh2)):
                act.wait_ge(loaded[s], n)
                dst, src, _ = expert_parts(s, 0)[part]
                act.activation(dst, src, ACT.Copy, scale=SC)
                act.activation(src, src, ACT.Copy, scale=SC).then_inc(done, 1)
            read_tokens(0, 0, 1)
            read_tokens(0, 2, 3)
            run_slots(act, slot)

            def overflow():
                with act.Fori(0, NOV) as j:
                    def v(n):
                        return len(OV_VEC) * j + (1 + OV_VEC[n])

                    def p(n):
                        return len(OV_PE) * j + OV_PE[n]

                    act.wait_ge(s_ovw, 48 * j + 48)
                    for dst, src, _ in expert_parts(0, 0):
                        ins = act.activation(dst, src, ACT.Copy, scale=SC)
                    ins.then_inc(s_ova, 1)
                    act.wait_ge(s_ovp, p("tokens"))
                    act.activation(ovxT[:, 0], bank16(0).rearrange("p (k t) -> p k t", k=KC), ACT.Copy).then_inc(s_ova, 1)
                    act.wait_ge(s_ovp, p("gate_up"))
                    act.activation(ove, ps[:, 2, 0:2 * P], ACT.Exp, scale=-ISC2).then_inc(s_ova, 1)
                    act.wait_ge(s_ovv, v("hidden"))
                    act.activation(ovhh, ovhid.rearrange("p (f t) -> p f t", f=2), ACT.Copy).then_inc(s_ova, 1)
                    act.wait_ge(s_ovp, p("down"))
                    act.activation(yb[:, 0, 0:512], ps[:, 4, :], ACT.Copy, scale=ISC2).then_inc(s_ova, 1)

            when_overflow(act, overflow)
            for t in range(NT + 1):
                act.wait_ge(s_fq, t + 1)
                if t:
                    act.wait_ge(s_fs, t)
                act.activation(gt2[0:rows(t)], x1[0:rows(t), t], ACT.Square,
                               accum_out=ss[0:rows(t), 16 + t:17 + t]).then_inc(s_fs, 1)

        @block.vector
        def _(dve):
            chain = [0]

            def link(ins):
                chain[0] += 1
                ins.then_inc(s_dv, 1)
                dve.wait_ge(s_dv, chain[0])

            dve.wait_ge(s_const, 1)
            dve.memset(diagm[64:P, 0], 0.0)
            dve.memset(diagm[0:64, 1], 0.0)
            dve.tensor_copy(ident16[:], ident[:])
            dve.tensor_scalar(identb[:], ident[:], BIG, None, ALU.mult)
            dve.tensor_copy(maskb[:], maskneg[:]).then_inc(s_const, 1)
            dve.wait_ge(s_g1, 16)
            link(dve.tensor_scalar(gbc[:], gbc[:], SC, None, ALU.mult))
            for t in range(NT + 1):
                r = rows(t)
                dve.wait_ge(s_ss, t + 1)
                dve.tensor_scalar(rst[0:r, t:t + 1], ss[0:r, t:t + 1], 1.0 / D, EPS, ALU.mult,
                                  ALU.add).then_inc(s_ms, 1)
            dve.wait_ge(s_par, 16 * N_PAR)
            dve.tensor_scalar(glag[:], glag[:], SC, None, ALU.mult).then_inc(s_glag, 1)

            def x_norm(t):
                r = rows(t)
                dve.wait_ge(s_rs, t + 1)
                dve.scalar_tensor_tensor(xt(t)[0:r], xt(t)[0:r], rst[0:r, t:t + 1], gbc[0:r, :], ALU.mult,
                                         ALU.mult).then_inc(s_xn, 1)

            def split_w(n):
                dve.wait_ge(s_wh, n + 1)
                dve.scalar_tensor_tensor(w_slot(slot_l, n), w_stage(n), SC, w_slot(slot_h, n), ALU.mult,
                                         ALU.subtract).then_inc(s_wl, 1)

            def split_group(g):
                for n in range(HALVES_TO[g - 1] if g else 0, HALVES_TO[g]):
                    split_w(n)

            x_norm(0)
            x_norm(1)
            split_group(0)
            dve.wait_ge(s_par, 16 * N_PAR)
            for i in range(2):
                ins = dve.tensor_tensor_reduce(kv[:, 1, DK * i:DK * i + DK], lams[:, 2 * i], lams[:, 2 * i + 1], 1.0, 0.0,
                                               ALU.mult, ALU.add, lamw[:, i:i + 1])
            ins.then_inc(s_ldot, 1)
            for t in range(NT + 1):
                r = rows(t)
                if t + 2 <= NT:
                    x_norm(t + 2)
                for b in range(2):
                    bank = 4 + 2 * (t % 2) + b
                    dve.wait_ge(s_hh, 2 * t + b + 1)
                    dve.tensor_tensor(hTl[:, 4 * b:4 * b + 4, span(t)],
                                      ps[:, bank, 0:4 * r].rearrange("p (k t) -> p k t", k=4),
                                      hTh[:, 4 * b:4 * b + 4, span(t)], ALU.subtract).then_inc(s_hl, 1)

            def plain_reads(g, after=()):
                after = list(after)
                for (gg, blk, j) in UNITS:
                    u = UNIT_AT[(gg, blk, j)]
                    if gg != g or u % 2 == 0:
                        continue
                    dve.wait_ge(s_mm, u + 1)
                    dve.tensor_scalar(*plain_target(g, blk, j), plain_scale(g, blk), None,
                                      ALU.mult).then_inc(s_ev[BANK[u]], 1)
                    for n in after.pop(0) if after else ():
                        page_scores(n)
                for ns in after:
                    for n in ns:
                        page_scores(n)

            split_group(1)
            plain_reads(GQK)
            split_group(2)
            plain_reads(CODE)
            split_group(3)
            plain_reads(GV)

            def per_chunk(buf, n=P):
                return buf.rearrange("p (c i) -> p c i", c=NT)

            dve.wait_ge(s_par, 16 * N_PAR)
            for p in range(2):
                for j in range(3):
                    cs = slice(CH * j, CH * (j + 1))
                    dve.wait_ge(s_z, 3 * p + j + 1)
                    dve.tensor_scalar(la[:, cs], ps[:, 4 + j, 0:CH], ba_col[:, p:p + 1], None,
                                      ALU.add).then_inc(s_zr, 1)
                dve.wait_ge(s_ln, p + 1)
                dve.wait_ge(s_zr, 3 * p + 3)
                link(dve.scalar_tensor_tensor(la, la, 0.0, es, ALU.min, ALU.subtract))
                for c in range(NT):
                    dve.tensor_tensor_scan(bc[:, span(c)], ones[:], la[:, span(c)], 0.0, ALU.mult, ALU.add)
                link(dve.tensor_copy(bc[:, SEQ:T], la[:, SEQ:T]))
                b3 = per_chunk(bc[:, 0:SEQ])
                m0 = b3[:, :, 31:32]
                m1 = b3[:, :, 95:96]
                last = b3[:, :, 127:128]
                k3 = per_chunk(ek)
                dve.tensor_tensor(per_chunk(ea), b3, m0.to_broadcast([P, NT, P]), ALU.subtract).then_inc(s_arg, 1)
                dve.tensor_tensor(k3[:, :, 0:64], m0.to_broadcast([P, NT, 64]), b3[:, :, 0:64], ALU.subtract)
                dve.tensor_tensor(k3[:, :, 64:P], m1.to_broadcast([P, NT, 64]), b3[:, :, 64:P],
                                  ALU.subtract).then_inc(s_arg, 1)
                dve.tensor_tensor(per_chunk(eb), b3[:, :, 64:P], m1.to_broadcast([P, NT, 64]),
                                  ALU.subtract).then_inc(s_arg, 1)
                dve.tensor_tensor(per_chunk(ed), last.to_broadcast([P, NT, P]), b3, ALU.subtract).then_inc(s_arg, 1)
                q3 = per_chunk(gq[:, p, 0:SEQ])
                dve.wait_ge(s_exp, 5 * p + 1)
                if p == 0:
                    dve.wait_ge(s_qz, 1)
                else:
                    dve.wait_ge(s_o, NT)
                for h in range(2):
                    hp = slice(64 * h, 64 * h + 64)
                    dve.tensor_tensor(qa[hp, :, h, :], q3[hp], per_chunk(ea)[hp], ALU.mult)
                dve.wait_ge(s_exp, 5 * p + 2)
                dve.tensor_tensor(ek, ek, gk[:, p, 0:SEQ], ALU.mult)
                dve.wait_ge(s_exp, 5 * p + 3)
                for h in range(2):
                    hp = slice(64 * h, 64 * h + 64)
                    dve.tensor_tensor(qb[hp, :, h, :], q3[hp, :, 64:P], per_chunk(eb)[hp], ALU.mult)
                dve.wait_ge(s_exp, 5 * p + 4)
                dve.tensor_tensor(ed, ed, gk[:, p, 0:SEQ], ALU.mult)
                dve.wait_ge(s_exp, 5 * p + 5)
                dve.tensor_copy(a_s[:, p], es[:, SEQ:T])
                dve.tensor_tensor(qs[:, 0:SEQ], gq[:, p, 0:SEQ], es[:, 0:SEQ], ALU.mult).then_inc(s_prep, 1)
                for c in range(NT + 1):
                    if c < NT:
                        n = p * NT + c
                        bank = 4 + n % 2
                        dve.wait_ge(s_sc, n + 1)
                        if n >= 2:
                            dve.wait_ge(s_o, n - 1)
                        dve.tensor_tensor(scb[0:64, n % 2], ps[0:64, bank, 0:256].rearrange("p (h i) -> p h i", h=2),
                                          mask_ji[0:64].unsqueeze(1).to_broadcast([64, 2, P]), ALU.mult)
                        dve.tensor_tensor(scb[64:P, n % 2, :, 64:P],
                                          ps[64:P, bank, 256:384].rearrange("p (h i) -> p h i", h=2),
                                          mask_ji[64:P, 64:P].unsqueeze(1).to_broadcast([64, 2, 64]),
                                          ALU.mult).then_inc(s_scm, 1)
                    if c >= 1:
                        n = p * NT + c - 1
                        dve.wait_ge(s_o, n + 1)
                        if c >= 2:
                            dve.wait_ge(s_S, n)
                        for h in range(2):
                            hp = slice(64 * h, 64 * h + 64)
                            ins = dve.scalar_tensor_tensor(
                                sbd[hp, p, h, :], sbd[hp, p, h, :], es[hp, P * c - 1:P * c],
                                ps[hp, 3, P * h:P * h + P], ALU.mult, ALU.add)
                        ins.then_inc(s_S, 1)
                if p == 0:
                    split_group(DQ)
            dve.wait_ge(s_ks, 1)
            for p in range(2):
                dve.tensor_tensor(kmask[:, :, P * p:P * p + P],
                                  ps[0:NB, 4, P * p:P * p + P].unsqueeze(1).to_broadcast([NB, NB, P]),
                                  ident[0:NB, 0:NB].unsqueeze(2).to_broadcast([NB, NB, P]), ALU.mult)
            for p in range(2):
                ins = dve.tensor_tensor(
                    qmask[:, p], gq[:, p, SEQ:T].unsqueeze(1).unsqueeze(1).to_broadcast([P, 2, NB, NB]),
                    diagm[:], ALU.mult)
            ins.then_inc(s_km, 1)
            dve.wait_ge(s_st, 32)
            for m in range(2 * NB):
                p, b = m // NB, m % NB
                dve.wait_ge(s_op, m // 2 + 1)
                for h in range(2):
                    hp = slice(64 * h, 64 * h + 64)
                    ins = dve.scalar_tensor_tensor(
                        st[hp, p, b, :], st[hp, p, b, :], a_s[hp, p, b:b + 1],
                        ps[hp, 4 + m // 2 % 4, 256 * (m % 2) + P * h:256 * (m % 2) + P * h + P], ALU.mult, ALU.add)
                if m % 2:
                    ins.then_inc(s_sn, 1)
            dve.wait_ge(s_ss, NT + 1 + H * (NT + 1))
            dve.tensor_scalar(rst[:, 0:32], ss[:, 0:32], 1.0 / DV, EPS, ALU.mult, ALU.add).then_inc(s_ms, 1)
            dve.tensor_scalar(rst[0:NB, 32:36], ss[0:NB, 32:36], 1.0 / DV, EPS, ALU.mult, ALU.add).then_inc(s_ms, 1)
            def gated(i):
                t = i - 2
                if 0 <= t <= NT:
                    r = rows(t)
                    dve.wait_ge(s_gs, 2 * (NT + 1))
                    if t >= 2:
                        dve.wait_ge(s_mT, t - 1)
                    if t == 0:
                        dve.wait_ge(s_rs, NT + 3)
                    for h in range(H):
                        hs = slice(DV * h, DV * h + DV)
                        ins = dve.scalar_tensor_tensor(gt[0:r, t % 2, hs], gv[0:r, t, hs],
                                                       rst[0:r, H * t + h:H * t + h + 1], gate[t][0:r, hs], ALU.mult,
                                                       ALU.mult)
                    ins.then_inc(s_mx, 1)
                if 0 <= t - 1 <= NT:
                    mix_lo(dve, t - 1, t - 1, 0)
                if i == 7:
                    split_group(DKG)

            def split_reads(g, hi, lo, prev, after=None):
                for blk in range(4):
                    for j in range(3):
                        u = UNIT_AT[(g, blk, j)]
                        cs = slice(CH * j, CH * (j + 1))
                        dve.wait_ge(s_hi, prev + 3 * blk + j + 1)
                        dve.scalar_tensor_tensor(lo[:, blk, cs], ps[:, BANK[u], 0:CH], SC * ISC2, hi[:, blk, cs],
                                                 ALU.mult, ALU.subtract).then_inc(s_ev[BANK[u]], 1)
                        if after:
                            after(3 * blk + j)

            split_reads(DQ, qdh, qdl, 0, after=gated)
            split_group(6)

            def page_scores(n):
                b, half = n // 2, n % 2
                dve.wait_ge(s_kq, n + 1)
                dve.tensor_reduce(dsc[:, b, :, KHALF * half:KHALF * half + KHALF].rearrange("p m g -> p g m"),
                                  kv[:, n % 2].rearrange("p (g m d) -> p g m d", g=KHALF, m=8), AX,
                                  ALU.add).then_inc(s_kh, 1)

            dve.wait_ge(s_out, 32)
            dve.memset(dsc, NEG).then_inc(s_dsz, 1)
            dve.wait_ge(s_dsz, 1)
            split_reads(DKG, kdh, kdl, 12, after=lambda j: page_scores(j - 5) if j >= 5 else None)
            plain_reads(DVG, after=[(7, 8), (9, 10), (11, 12), (13, 14), (15,)])
            dve.wait_ge(s_knr, NT + 2)
            qk = gt[0:NB, 1]
            link(dve.tensor_tensor(qk, qn, knat[0:NB, NT % 4], ALU.mult))
            dve.tensor_reduce(snew[:], qk.rearrange("p (m d) -> p m d", m=8), AX, ALU.add).then_inc(s_snew, 1)
            dve.wait_ge(s_lexp, 1)
            link(dve.scalar_tensor_tensor(nlam, lamw[:, 3:4], -LAM_INIT, lamw[:, 2:3], ALU.add, ALU.subtract))
            dve.wait_ge(s_par, 16 * N_PAR)
            dve.wait_ge(s_g1, 32)
            link(dve.tensor_scalar(dgain[:], dgain[:], SC * (1.0 - LAM_INIT), None, ALU.mult))
            link(dve.tensor_scalar(gbc[:], gbc[:], SC, None, ALU.mult))

            def split_wo(c):
                dve.wait_ge(s_woh, c + 1)
                dve.scalar_tensor_tensor(wol[:, 2 * c:2 * c + 2], stage[c % 2].rearrange("p (k n) -> p k n", k=2), SC,
                                         woh[:, 2 * c:2 * c + 2], ALU.mult, ALU.subtract).then_inc(s_wol, 1)

            def normed(kind, t, n):
                pr, cr = rcol(kind, t)
                k = REQ.index((kind, t))
                dve.tensor_scalar(rst[pr, cr], ss[pr, cr], 1.0 / n, EPS, ALU.mult, ALU.add).then_inc(s_ms, 1)
                dve.wait_ge(s_rs, NT + 3 + k + 1)

            def maxima(u):
                maps = (slice(0, 2),) if u < 16 else (slice(0, 1), slice(1, 2))
                for ms in maps:
                    dve.wait_ge(s_qk, 2 * u + ms.stop)
                    if u < 16:
                        sc = ps[:, score_bank(u, 0):score_bank(u, 0) + 2, 0:(u // H + 1) * P]
                    else:
                        sc = scores(u, ms.start)
                    link(dve.tensor_reduce(mxs[:, u % 2, ms], sc, AX, ALU.max))
                    dve.tensor_scalar(mxn[:, u % 2, ms], mxs[:, u % 2, ms], -DK ** -0.5 * ISC2, None,
                                      ALU.mult).then_inc(s_nm, ms.stop - ms.start)

            d3 = dsc.rearrange("p b m g -> p (b m) g")
            for u in range(UN + 8):
                if u % H == 3 and 11 <= u:
                    attn_lo_on(dve, (u - 11) // H)
                if u < UN:
                    maxima(u)
                if 1 <= u <= UN:
                    v = u - 1
                    i, h = v // H, v % H
                    n = (i + 1) * P
                    dve.wait_ge(s_p, 2 * v + 2)
                    link(dve.reciprocal(rinv[:, i % 3, h], rsum[:, i % 3, h]))
                    link(dve.scalar_tensor_tensor(comb[:, 0:1], rinv[:, i % 3, h, 1:2], rsum[:, i % 3, h, 0:1], nlam,
                                                  ALU.mult, ALU.mult))
                    dve.scalar_tensor_tensor(prob[:, v % 3, 0, 0:n], prob[:, v % 3, 1, 0:n], comb[:, 0:1],
                                             prob[:, v % 3, 0, 0:n], ALU.mult, ALU.add).then_inc(s_wc, 1)
                if u in WO_AT:
                    split_wo(WO_AT.index(u))
                if u == 0:
                    dve.wait_ge(s_snin, 16)
                    dve.wait_ge(s_kh, 2 * NB)
                    dve.tensor_reduce(dmx[:], d3, AX, ALU.max).then_inc(s_dec, 1)
                if u == 3:
                    dve.wait_ge(s_mbb, 1)
                    dve.tensor_tensor(d3, d3, dmb[:].unsqueeze(2).to_broadcast([P, NB * 8, NPG + 1]),
                                      ALU.subtract).then_inc(s_dec, 1)
                if u == 5:
                    dve.wait_ge(s_deca, 1)
                    dve.tensor_reduce(dmx[:], d3, AX, ALU.add).then_inc(s_dec, 1)
                if u == 7:
                    dve.wait_ge(s_mbb, 2)
                    dve.wait_ge(s_spout, 16 * H)
                    link(dve.reciprocal(dmb[:], dmb[:]))
                    r2 = dmb[:].rearrange("p (b m) -> p b m", m=2)
                    link(dve.tensor_scalar(r2[:, :, 1], r2[:, :, 1], nlam, None, ALU.mult))
                    link(dve.tensor_tensor(d3, d3, dmb[:].unsqueeze(2).to_broadcast([P, NB * 8, NPG + 1]), ALU.mult))
                    d4 = dsc.rearrange("p b (h m) g -> p (b h) m g", m=2)
                    link(dve.tensor_tensor(dw.rearrange("p b h g -> p (b h) g"), d4[:, :, 0, :], d4[:, :, 1, :], ALU.add))
                    dve.tensor_copy(dmx[0:1, 0:4 * NB], dw[0:1, :, :, NPG].rearrange("p b h -> p (b h)")
                                    ).then_inc(s_dec, 1)
                if u % H == 0 and u >= 8:
                    i = (u - 8) // H
                    dve.wait_ge(s_dsq, H * (i + 1))
                    normed("d", i, DV)
                    f = comb4[:, i % 2]
                    link(dve.tensor_tensor(f, rst[:, 4 * i:4 * i + 4], rinv[:, i % 3, :, 0], ALU.mult))
                    if i >= 2:
                        dve.wait_ge(s_mT, MIXED + i - 1)
                    for h in range(H):
                        hs = slice(DV * h, DV * h + DV)
                        ins = dve.scalar_tensor_tensor(gt[:, i % 2, hs], ps[:, 6 + i % 2, hs], f[:, h:h + 1], dgain[:],
                                                       ALU.mult, ALU.mult)
                    ins.then_inc(s_dn, 1)
            dve.wait_ge(s_par, 16 * N_PAR)
            link(dve.tensor_scalar(wrh[:], wr[:], SC, None, ALU.mult))
            dve.scalar_tensor_tensor(wrl[:], wr[:], SC, wrh[:], ALU.mult, ALU.subtract).then_inc(s_wrs, 1)

            def values(k):
                b = k // 2
                dve.wait_ge(s_vp[k % 2], 64 * (k // 2 + 1))
                for g in range(KHALF):
                    page = KHALF * (k % 2) + g
                    for h in range(H):
                        v = kv[:, k % 2, 512 * g + DV * h:512 * g + DV * h + DV]
                        w = dw[:, b, h, page:page + 1]
                        acc = dacc[:, b, DV * h:DV * h + DV]
                        if page == 0:
                            ins = dve.tensor_scalar(acc, v, w, None, ALU.mult)
                        else:
                            dve.wait_ge(s_acd, H * (NPG * (b - PSEQ) + page - 1) + h + 1)
                            ins = dve.scalar_tensor_tensor(acc, v, w, acc, ALU.mult, ALU.add)
                        ins.then_inc(s_acd, 1)

            for t in range(NT + 3):
                if t <= NT:
                    r = rows(t)
                    dve.wait_ge(s_xr[t % 2], 16 * (t // 2 + 1))
                    for half in range(2):
                        cs = slice(512 * half, 512 * half + 512)
                        dve.wait_ge(s_om, 2 * t + half + 1)
                        dve.scalar_tensor_tensor(x1[0:r, t, cs], ps[0:r, 2 * (t % 2) + half, :], ISC2, xr[0:r, t % 2, cs],
                                                 ALU.mult, ALU.add).then_inc(s_x1, 1)
                    if 2 * PSEQ + 2 * t < 2 * NB:
                        values(2 * PSEQ + 2 * t)
                    dve.wait_ge(s_x1q, t + 1)
                    normed("x", t, D)
                    dve.scalar_tensor_tensor(h2[0:r, t % 2], x1[0:r, t], rst[0:r, t:t + 1], gbc[0:r], ALU.mult,
                                             ALU.mult).then_inc(s_h2, 1)
                    if 2 * PSEQ + 2 * t < 2 * NB:
                        values(2 * PSEQ + 2 * t + 1)
                    if t >= 2:
                        dve.wait_ge(s_h2o[t % 2], 16 * (t // 2))
                        dve.wait_ge(s_h2T, t - 1)
                    dve.wait_ge(s_h2h, t + 1)
                    dve.tensor_tensor(h2s[0:r, t % 2, D:2 * D], h2[0:r, t % 2], h2s[0:r, t % 2, 0:D],
                                      ALU.subtract).then_inc(s_h2l, 1)
                if t == NB - PSEQ + 1:
                    dve.wait_ge(s_ds, 1)
                    dve.wait_ge(s_wni, 16)
                    for h in range(H):
                        hs = slice(DV * h, DV * h + DV)
                        ins = dve.scalar_tensor_tensor(dod[:, hs], vd_new[:, hs], wn[:, h:h + 1], ps[0:NB, 7, hs],
                                                       ALU.mult, ALU.add)
                    ins.then_inc(s_dec, 1)
                    dve.wait_ge(s_deca, 1 + H)
                    normed("dec", 0, DV)
                    for h in range(H):
                        hs = slice(DV * h, DV * h + DV)
                        ins = dve.scalar_tensor_tensor(dod[:, hs], dod[:, hs], rst[0:NB, 36 + h:37 + h], dgain[0:NB],
                                                       ALU.mult, ALU.mult)
                    ins.then_inc(s_dec, 1)
                if t == NB - PSEQ + 3:
                    dve.wait_ge(s_mh, MIXED + NT + 1)
                    dve.tensor_tensor(mixl[:, 4:8, SEQ:T], ps[:, 7, 0:4 * NB].rearrange("p (k b) -> p k b", k=4),
                                      mixh[:, 4:8, SEQ:T], ALU.subtract).then_inc(s_ml, 1)
                if t >= 2:
                    v = t - 2
                    r = rows(v)
                    dve.wait_ge(s_rt, v + 1)
                    dve.scalar_tensor_tensor(lg[0:r, v], ps[0:r, 6, 0:NG + NE], ISC2, br[0:r], ALU.mult,
                                             ALU.add).then_inc(s_rtr, 1)
            dve.wait_ge(s_rtr, NT + 1)
            link(dve.tensor_scalar(iom, iof[:, 0:4], -64.0, None, ALU.add))

            def first_max(x, m, out):
                link(dve.tensor_tensor(r_cand, x, m.unsqueeze(2).to_broadcast([P, 9, 4]), ALU.is_ge))
                link(dve.tensor_tensor(r_cand, r_cand, iom.unsqueeze(1).to_broadcast([P, 9, 4]), ALU.mult))
                link(dve.tensor_reduce(r_mi, r_cand, AX, ALU.min))
                link(dve.tensor_tensor(out, r_cand, r_mi.unsqueeze(2).to_broadcast([P, 9, 4]), ALU.is_equal))

            lgg = lg[:, :, 0:NG]
            link(dve.tensor_reduce(r_m, lgg, AX, ALU.max))
            dve.tensor_tensor(eg4, lgg, r_m.unsqueeze(2).to_broadcast([P, 9, 4]), ALU.subtract).then_inc(s_re, 1)
            first_max(lgg, r_m, ohg)
            prod4 = r_prod.rearrange("p t (g e) -> p t g e", g=NG)
            link(dve.tensor_tensor(prod4, lg[:, :, NG:].rearrange("p t (g e) -> p t g e", g=NG),
                                   ohg.unsqueeze(3).to_broadcast([P, 9, NG, EPG]), ALU.mult))
            link(dve.tensor_reduce(r_le, r_prod.rearrange("p t (g e) -> p t e g", g=NG), AX, ALU.add))
            link(dve.tensor_reduce(r_m1, r_le, AX, ALU.max))
            first_max(r_le, r_m1, oh1)
            link(dve.scalar_tensor_tensor(r_le, oh1, NEG, r_le, ALU.mult, ALU.add))
            link(dve.tensor_reduce(r_m2, r_le, AX, ALU.max))
            dve.tensor_tensor(dd, r_m2, r_m1, ALU.subtract).then_inc(s_re, 1)
            first_max(r_le, r_m2, oh2)
            link(dve.tensor_scalar(r_valid, tokid[:], float(T), None, ALU.is_lt))
            link(dve.tensor_tensor(ohg, ohg, r_valid.unsqueeze(2).to_broadcast([P, 9, 4]), ALU.mult))
            for c, oh in enumerate((oh1, oh2)):
                link(dve.tensor_tensor(cho[:, 9 * c:9 * c + 9].rearrange("p t (g e) -> p t g e", g=NG),
                                       ohg.unsqueeze(3).to_broadcast([P, 9, NG, EPG]),
                                       oh.unsqueeze(2).to_broadcast([P, 9, NG, EPG]), ALU.mult))
            link(dve.tensor_tensor(strict[:], mask_ji[:], ident[:], ALU.subtract))
            dve.tensor_tensor(r_a, cho[:, 0:9], cho[:, 9:18], ALU.add).then_inc(s_re, 1)
            dve.wait_ge(s_rex, 2)
            link(dve.tensor_reduce(r_s, eg4, AX, ALU.add))
            link(dve.reciprocal(r_pt, r_s))
            link(dve.tensor_scalar(r_s, dd, 1.0, None, ALU.add))
            link(dve.reciprocal(r_s, r_s))
            link(dve.tensor_tensor(gates[:, 0], r_s, r_pt, ALU.mult))
            link(dve.tensor_tensor(gates[:, 1], gates[:, 0], dd, ALU.mult))
            dve.wait_ge(s_rc, 1)
            link(dve.tensor_copy(r_pos, ps[:, 0, 0:144].rearrange("p (t e) -> p t e", t=9)))
            link(dve.memset(r_ne, 0.0))
            for t in range(NT + 1):
                link(dve.tensor_tensor(r_pos[:, t], r_pos[:, t], r_ne, ALU.add))
                link(dve.tensor_tensor(r_ne, r_ne, ps[:, 1, 16 * t:16 * t + 16], ALU.add))
            link(dve.tensor_scalar(r_thr, iof[:, 0:8], float(P), float(CAP), ALU.mult, ALU.add))
            link(dve.tensor_tensor(r_cmp, r_ne.unsqueeze(2).to_broadcast([P, 16, 8]),
                                   r_thr.unsqueeze(1).to_broadcast([P, 16, 8]), ALU.is_gt))
            link(dve.tensor_reduce(r_oc, r_cmp, AX, ALU.add))
            link(dve.tensor_tensor_scan(r_inc, ones[:, 0:16], r_oc, 0.0, ALU.mult, ALU.add))
            link(dve.tensor_tensor(r_ost, r_inc, r_oc, ALU.subtract))
            for dst, src in ((r_r, None), (r_e, iof[:, 0:16]), (r_o, r_ost)):
                for c in range(2):
                    in1 = r_pos if src is None else src.unsqueeze(1).to_broadcast([P, 9, 16])
                    link(dve.tensor_tensor(r_tmp[:, 9 * c:9 * c + 9], cho[:, 9 * c:9 * c + 9], in1, ALU.mult))
                link(dve.tensor_reduce(dst, r_tmp, AX, ALU.add))
            link(dve.tensor_scalar(r_g, r_r, float(P), None, ALU.is_ge))
            link(dve.tensor_scalar(r_f, r_r, float(CAP), None, ALU.is_ge))
            link(dve.tensor_tensor(r_q3, r_r.unsqueeze(2).to_broadcast([P, 18, 8]),
                                   r_thr.unsqueeze(1).to_broadcast([P, 18, 8]), ALU.is_ge))
            link(dve.tensor_reduce(r_q, r_q3, AX, ALU.add))
            link(dve.scalar_tensor_tensor(r_p, r_g, -float(P), r_r, ALU.mult, ALU.add))
            link(dve.scalar_tensor_tensor(r_c, r_e, 2.0, r_g, ALU.mult, ALU.add))
            link(dve.scalar_tensor_tensor(r_po, r_q, -float(P), r_r, ALU.mult, ALU.add))
            link(dve.tensor_scalar(r_po, r_po, float(P - CAP), None, ALU.add))
            link(dve.tensor_tensor(r_co, r_o, r_q, ALU.add))
            link(dve.tensor_scalar(r_co, r_co, float(2 * NE - 1), None, ALU.add))
            link(dve.scalar_tensor_tensor(r_x, r_e, float(CAP), r_r, ALU.mult, ALU.add))
            link(dve.tensor_tensor(r_y, r_x, r_f, ALU.mult))
            link(dve.tensor_tensor(yrow[:].rearrange("p c t -> p (c t)"), r_x, r_y, ALU.subtract))
            link(dve.scalar_tensor_tensor(r_x, r_co, float(P), r_po, ALU.mult, ALU.add))
            link(dve.tensor_scalar(r_x, r_x, float(-2 * NE * P), None, ALU.add))
            link(dve.tensor_tensor(orow[:].rearrange("p c t -> p (c t)"), r_x, r_f, ALU.mult))
            link(dve.tensor_tensor(ogates[:], gates[:], r_f.rearrange("p (c t) -> p c t", c=2), ALU.mult))
            link(dve.tensor_tensor(gates[:], gates[:], ogates[:], ALU.subtract))
            for a, b in ((r_p, r_po), (r_c, r_co)):
                link(dve.tensor_tensor(b, b, a, ALU.subtract))
                link(dve.tensor_tensor(b, b, r_f, ALU.mult))
                link(dve.tensor_tensor(a, a, b, ALU.add))
            link(dve.tensor_tensor(r_cmj, iof[:, 0:NOV].unsqueeze(2).to_broadcast([P, NOV, 16]),
                                   r_inc.unsqueeze(1).to_broadcast([P, NOV, 16]), ALU.is_ge))
            link(dve.tensor_reduce(r_oe[:, 0:NOV], r_cmj, AX, ALU.add))
            link(dve.tensor_scalar(r_oe[:, 0:NOV], r_oe[:, 0:NOV], float(NE - 1), None, ALU.min))
            link(dve.tensor_copy(r_oe[:, NOV:NOV + 1], r_inc[:, 15:16]))
            link(dve.tensor_copy(oexp[:], r_oe[0:1]))
            for c in range(2):
                link(dve.tensor_tensor(r_tv[:, 9 * c:9 * c + 9], tokid[:], r_valid, ALU.mult))
            link(dve.tensor_tensor(oneh_c, iof[:, 0:COLS].unsqueeze(1).to_broadcast([P, 18, COLS]),
                                   r_c.unsqueeze(2).to_broadcast([P, 18, COLS]), ALU.is_equal))
            link(dve.tensor_tensor(oneh_c, oneh_c, r_tv.unsqueeze(2).to_broadcast([P, 18, COLS]), ALU.mult))
            for n in (0, 9):
                dve.tensor_tensor(oneh_p[:, n:n + 9], iof[:].unsqueeze(1).to_broadcast([P, 9, P]),
                                  r_p[:, n:n + 9].unsqueeze(2).to_broadcast([P, 9, P]), ALU.is_equal).then_inc(s_rs1, 1)
            dve.wait_ge(s_rsu, 1)
            dve.tensor_copy(tok[:], ps[:, 2, 0:COLS]).then_inc(s_route, 1)

            def split_gate_up(s, n):
                for j, (dst, src, hi) in enumerate(expert_parts(s, 1)[0:2]):
                    dve.wait_ge(s_mh2, n + (j + 1))
                    dve.scalar_tensor_tensor(dst, src, SC, hi, ALU.mult, ALU.subtract).then_inc(s_mlo, 1)

            def split_down(s, n):
                dve.wait_ge(s_mhd, n + 1)
                dst, src, hi = expert_parts(s, 1)[2]
                dve.scalar_tensor_tensor(dst, src, SC, hi, ALU.mult, ALU.subtract).then_inc(s_mld, 1)

            def read_tokens(s, f, n):
                dve.wait_ge(s_eT, n)
                dve.tensor_copy(xT[:, s, f // 2, 4 * (f % 2):4 * (f % 2) + 4],
                                bank16(1)[:, 0:4 * CAP].rearrange("p (k t) -> p k t", k=4)).then_inc(s_ev2, 1)

            def slot(i, off, e=None):
                s = off % 2

                def at(k, c):
                    return k * 2 * i + (k * off + c)

                if e != NE:
                    dve.wait_ge(s_sg, at(1, 1))
                    dve.tensor_scalar(eg, eg, 1.0, None, ALU.add).then_inc(s_s1, 1)
                    dve.wait_ge(s_s1, at(3, 1))
                    if e != NE - 1:
                        read_tokens(1 - s, 1, at(4, 6))
                    dve.reciprocal(eg, eg).then_inc(s_s1, 1)
                    dve.wait_ge(s_s1, at(3, 2))
                    dve.scalar_tensor_tensor(eg, ps[:, 2, 0:2 * CAP], ISC2, eg, ALU.mult, ALU.mult).then_inc(s_s1, 1)
                    dve.wait_ge(s_s1, at(3, 3))
                    dve.scalar_tensor_tensor(hid, ps[:, 3, 0:2 * CAP], ISC2 * SC, eg, ALU.mult,
                                             ALU.mult).then_inc(s_hf, 1)
                    if e != NE - 1:
                        read_tokens(1 - s, 3, at(4, 8))
                    dve.wait_ge(s_hf, at(1, 1))
                    dve.wait_ge(s_hh2, at(1, 1))
                    dve.tensor_tensor(hidl[:, s], hid.rearrange("p (f t) -> p f t", f=2), hidh[:, s],
                                      ALU.subtract).then_inc(s_hl2, 1)
                if e != 0:
                    if e is None or e >= 3:
                        dve.wait_ge(s_yo[1 - s], 32 * i + 32 * ((off - 1) // 2))
                    dve.wait_ge(s_down, at(4, -2))
                    dve.tensor_scalar(yb[:, 1 - s, 512:D], ps[:, 5, :], ISC2, None, ALU.mult)
                    dve.wait_ge(s_down, at(4, 0))
                    dve.tensor_scalar(yb[0:CAP1, 1 - s, D + 512:2 * D], ps[0:CAP1, 7, :], ISC2, None,
                                      ALU.mult).then_inc(s_yv, 1)
                if e is None or e + 2 < NE:
                    split_gate_up(s, at(2, 4))
                if e is None or e + 1 < NE:
                    split_down(1 - s, at(1, 1))

            read_tokens(0, 1, 2)
            read_tokens(0, 3, 4)
            dve.wait_ge(s_mlo, 4)
            dve.wait_ge(s_mld, 1)
            run_slots(dve, slot)

            def overflow():
                dve.memset(junk[:], 0.0).then_inc(s_ovv, 1)
                with dve.Fori(0, NOV) as j:
                    def v(n):
                        return len(OV_VEC) * j + (1 + OV_VEC[n])

                    def a(n):
                        return len(OV_ACT) * j + OV_ACT[n]

                    def p(n):
                        return len(OV_PE) * j + OV_PE[n]

                    dve.wait_ge(s_ova, a("weights_hi"))
                    for dst, src, hi in expert_parts(0, 1):
                        ins = dve.scalar_tensor_tensor(dst, src, SC, hi, ALU.mult, ALU.subtract)
                    ins.then_inc(s_ovv, 1)
                    dve.wait_ge(s_ovp, p("tokens"))
                    dve.tensor_copy(ovxT[:, 1], bank16(1).rearrange("p (k t) -> p k t", k=KC)).then_inc(s_ovv, 1)
                    dve.wait_ge(s_ova, a("exp"))
                    dve.tensor_scalar(ove, ove, 1.0, None, ALU.add).then_inc(s_ovv, 1)
                    dve.wait_ge(s_ovv, v("plus_one"))
                    dve.reciprocal(ove, ove).then_inc(s_ovv, 1)
                    dve.wait_ge(s_ovv, v("sigmoid"))
                    dve.scalar_tensor_tensor(ove, ps[:, 2, 0:2 * P], ISC2, ove, ALU.mult, ALU.mult).then_inc(s_ovv, 1)
                    dve.wait_ge(s_ovv, v("silu"))
                    dve.scalar_tensor_tensor(ovhid, ps[:, 3, 0:2 * P], ISC2 * SC, ove, ALU.mult,
                                             ALU.mult).then_inc(s_ovv, 1)
                    dve.wait_ge(s_ova, a("hidden_hi"))
                    dve.wait_ge(s_ovv, v("hidden"))
                    dve.tensor_tensor(ovhl, ovhid.rearrange("p (f t) -> p f t", f=2), ovhh,
                                      ALU.subtract).then_inc(s_ovv, 1)
                    dve.wait_ge(s_ovp, p("down"))
                    dve.tensor_scalar(yb[:, 0, 512:D], ps[:, 5, :], ISC2, None, ALU.mult).then_inc(s_ovv, 1)
                n = 1 + len(OV_VEC) * NOV
                for t in range(NT + 1):
                    r = rows(t)
                    dve.wait_ge(s_ovx, 16 * NOV + 32 * (t + 1))
                    for c in range(2):
                        dve.scalar_tensor_tensor(x1[0:r, t], yg[0][0:r, c], ogates[0:r, c, t:t + 1], x1[0:r, t],
                                                 ALU.mult, ALU.add).then_inc(s_ovv, 1)
                        dve.wait_ge(s_ovv, n + 2 * t + c + 1)

            when_overflow(dve, overflow)
            def gather_sum(t):
                r = rows(t)
                dve.wait_ge(s_yg[t % 3], 32 * (t // 3 + 1))
                link(dve.scalar_tensor_tensor(x1[0:r, t], yg[t][0:r, 0], gates[0:r, 0, t:t + 1], x1[0:r, t],
                                              ALU.mult, ALU.add))
                dve.scalar_tensor_tensor(x1[0:r, t], yg[t][0:r, 1], gates[0:r, 1, t:t + 1], x1[0:r, t],
                                         ALU.mult, ALU.add).then_inc(s_fq, 1)

            gather_sum(0)
            gather_sum(1)
            dve.wait_ge(s_g1, 48)
            for t in range(NT + 1):
                r = rows(t)
                if t + 2 <= NT:
                    gather_sum(t + 2)
                dve.wait_ge(s_fs, t + 1)
                normed("f", t, D)
                if t >= 2:
                    dve.wait_ge(s_fout[t % 2], 16 * (t // 2))
                dve.scalar_tensor_tensor(fin[0:r, t % 2], x1[0:r, t], rst[0:r, 16 + t:17 + t], gbc[0:r], ALU.mult,
                                         ALU.mult).then_inc(s_fo, 1)

        @block.tensor
        def _(pe):
            def split_mm(out, lh, ll, rh, rl, start, stop):
                pe.matmul(out, lh, rh, start=start, stop=False)
                pe.matmul(out, lh, rl, start=False, stop=False)
                return pe.matmul(out, ll, rh, start=False, stop=stop)

            pe.wait_ge(s_const, 2)
            for t in range(NT + 1):
                r = rows(t)
                pe.wait_ge(s_xn, t + 1)
                if t >= 2:
                    pe.wait_ge(s_hl, 2 * (t - 1))
                for k in range(KC):
                    ins = pe.transpose(ps[:, 4 + 2 * (t % 2) + k // 4, r * (k % 4):r * (k % 4) + r],
                                       xt(t)[0:r, P * k:P * k + P], ident[0:r, 0:r])
                ins.then_inc(s_xT, 1)

            def project(g, after=None, only=None):
                kind, _, wd = GROUPS[g]
                sh, sl = slot_h[g % 2], slot_l[g % 2]
                pe.wait_ge(s_wl, HALVES_TO[g])
                for (gg, blk, j) in UNITS:
                    if gg != g or (only is not None and blk not in only):
                        continue
                    u = UNIT_AT[(gg, blk, j)]
                    if NTH[u] > 1:
                        pe.wait_ge(s_ev[BANK[u]], NTH[u] - 1)
                    for k in range(KC):
                        if kind == "T":
                            m = min(P, wd)
                            cs = slice(CH * j, CH * (j + 1))
                            ins = split_mm(ps[0:m, BANK[u], 0:CH], sh[:, k, P * blk:P * blk + m],
                                           sl[:, k, P * blk:P * blk + m], hTh[:, k, cs], hTl[:, k, cs],
                                           k == 0, k == KC - 1)
                        else:
                            r = rows(blk)
                            ins = split_mm(ps[0:r, BANK[u], :], hTh[:, k, span(blk)], hTl[:, k, span(blk)],
                                           sh[:, k, :], sl[:, k, :], k == 0, k == KC - 1)
                    ins.then_inc(s_mm, 1)
                    if after:
                        after(blk, j)

            pe.wait_ge(s_hl, 2 * (NT + 1))
            project(GQK)
            project(CODE)
            project(GV)
            pe.wait_ge(s_par, 16 * N_PAR)
            for u in UNITS:
                if u[0] in (CODE, GQK, GV):
                    i = UNIT_AT[u]
                    pe.wait_ge(s_ev[BANK[i]], NTH[i])
            for p in range(2):
                for j in range(3):
                    if p:
                        pe.wait_ge(s_zr, 3)
                        pe.wait_ge(s_oev, NT)
                        pe.wait_ge(s_S, NT)
                        pe.wait_ge(s_scm, NT)
                        pe.wait_ge(s_kdn, NT)
                    pe.matmul(ps[:, 4 + j, 0:CH], wa2[:, P * p:P * p + P], code[:, CH * j:CH * (j + 1)],
                              start=True, stop=True).then_inc(s_z, 1)
                project(GR, only=range(4 * p, 4 * p + 4))
                pe.wait_ge(s_prep, p + 1)
                pe.wait_ge(s_zr, 3 * p + 3)
                for c in range(NT + 1):
                    if c < NT:
                        n = p * NT + c
                        bank = 4 + n % 2
                        if n >= 2:
                            pe.wait_ge(s_scm, n - 1)
                            pe.wait_ge(s_kdn, n - 1)
                        kk = ek[:, span(c)]
                        pe.matmul(ps[:, bank, 0:256], kk, qa[:, c].rearrange("p h i -> p (h i)"), start=True, stop=True)
                        pe.matmul(ps[64:P, bank, 256:384], kk[:, 64:P], qb[:, c].rearrange("p h i -> p (h i)"),
                                  start=True, stop=True)
                        if n:
                            pe.wait_ge(s_kdn, n)
                        pe.transpose(ps[:, 2, 0:P], ed[:, span(c)], ident[:]).then_inc(s_sc, 1)
                    if c >= 1:
                        n = p * NT + c - 1
                        bank = 6 + n % 2
                        if n >= 2:
                            pe.wait_ge(s_oev, n - 1)
                        if n:
                            pe.wait_ge(s_S, n)
                        pe.wait_ge(s_scm, n + 1)
                        pe.wait_ge(s_kdn, n + 1)
                        vp = gv[:, c - 1, 256 * p:256 * p + 256]
                        pe.matmul(ps[:, bank, 0:256], qs[:, span(c - 1)], sbd[:, p].rearrange("p h v -> p (h v)"),
                                  start=True, stop=False)
                        for h in range(2):
                            pe.matmul(ps[:, bank, P * h:P * h + P], scb[:, n % 2, h, :], vp[:, P * h:P * h + P],
                                      start=False, stop=h == 1)
                        pe.matmul(ps[:, 3, 0:256], kdn[:, n % 2], vp, start=True, stop=True).then_inc(s_o, 1)
            project(GR, only=(NT,))
            pe.wait_ge(s_scm, 2 * NT)
            pe.wait_ge(s_kdn, 2 * NT)
            for p in range(2):
                ins = pe.transpose(ps[0:NB, 4, P * p:P * p + P], gk[:, p, SEQ:T], ident[:])
            ins.then_inc(s_ks, 1)
            pe.wait_ge(s_km, 1)
            pe.wait_ge(s_oev, 2 * NT)
            pe.wait_ge(s_S, 2 * NT)
            for m in range(2 * NB):
                p, b = m // NB, m % NB
                if m >= 8 and m % 2 == 0:
                    pe.wait_ge(s_sn, m // 2 - 3)
                ins = pe.matmul(ps[:, 4 + m // 2 % 4, 256 * (m % 2):256 * (m % 2) + 256], kmask[:, b, P * p:P * p + P],
                                gv[0:NB, NT, 256 * p:256 * p + 256], start=True, stop=True)
                if m % 2:
                    ins.then_inc(s_op, 1)
            pe.wait_ge(s_sn, 8)
            for p in range(2):
                for h in range(2):
                    for b in range(NB):
                        ins = pe.matmul(ps[0:NB, 4, DV * (2 * p + h):DV * (2 * p + h) + DV], qmask[:, p, h, b, :],
                                        st[:, p, b, :], start=b == 0, stop=b == NB - 1)
            ins.then_inc(s_ks, 1)

            def mix_transpose(n, t, src, ready, count):
                r = rows(t)
                pe.wait_ge(ready, count)
                if n >= 2:
                    pe.wait_ge(s_ml, n - 1)
                for k in range(4):
                    ins = pe.transpose(ps[:, 4 + n % 2, r * k:r * k + r], src[0:r, P * k:P * k + P], ident[0:r, 0:r])
                ins.then_inc(s_mT, 1)

            def gated_transpose(blk, j):
                t = 3 * blk + j - 3
                if 0 <= t <= NT:
                    mix_transpose(t, t, gt[:, t % 2], s_mx, t + 1)

            project(DQ, after=gated_transpose)

            def natural(n, t, hi, lo):
                r = rows(t)
                if n >= 4:
                    pe.wait_ge(s_knr, n - 3)
                for h in range(H):
                    out = ps[0:r, 4 + n % 4, P * h:P * h + P]
                    pe.matmul(out, hi[:, h, span(t)], ident16[:], start=True, stop=False)
                    ins = pe.matmul(out, lo[:, h, span(t)], ident16[:], start=False, stop=True)
                ins.then_inc(s_kn, 1)

            pe.wait_ge(s_ml, NT + 1)
            for u in range(UNIT_AT[(DQ, 3, 2)] - 3, UNIT_AT[(DQ, 3, 2)] + 1):
                pe.wait_ge(s_ev[BANK[u]], NTH[u])
            natural(0, NT, qdh, qdl)
            project(DKG)
            for u in range(UNIT_AT[(DKG, 3, 2)] - 3, UNIT_AT[(DKG, 3, 2)] + 1):
                pe.wait_ge(s_ev[BANK[u]], NTH[u])
            project(DVG, after=lambda t, _: natural(t + 1, t, kdh, kdl))

            def attn_transpose(i):
                pe.wait_ge(s_dn, i + 1)
                for h in range(H):
                    ins = pe.transpose(ps[:, 6 + i % 2, P * h:P * h + P], gt[:, i % 2, P * h:P * h + P], ident[:])
                ins.then_inc(s_mT, 1)

            def product(t):
                r = rows(t)
                pe.wait_ge(s_wol, KC // 2)
                pe.wait_ge(s_ml, MIXED + t + 1)
                pe.wait_ge(s_p, 2 * UN)
                if t >= 2:
                    pe.wait_ge(s_x1, 2 * (t - 1))
                for half in range(2):
                    cs = slice(512 * half, 512 * half + 512)
                    for k in range(KC):
                        ins = split_mm(ps[0:r, 2 * (t % 2) + half, :], mixh[:, k, span(t)], mixl[:, k, span(t)],
                                       woh[:, k, cs], wol[:, k, cs], k == 0, k == KC - 1)
                    ins.then_inc(s_om, 1)

            for u in range(len(UNITS) - PB, len(UNITS)):
                pe.wait_ge(s_ev[BANK[u]], NTH[u])
            pe.wait_ge(s_knr, NT + 2)
            for u in range(UN + 7):
                if u < UN:
                    i, h = u // H, u % H
                    n = (i + 1) * P
                    for m in range(2):
                        if u >= 2:
                            pe.wait_ge(s_p, 2 * (u - 1) if u < 16 else 2 * (u - 1) + m + 1)
                        hp = slice(DK * m, DK * m + DK)
                        q = slice(P * i, P * i + P)
                        sc = scores(u, m)
                        for c in range(0, n, 512):
                            ks = slice(c, min(n, c + 512))
                            own = ks.stop == n
                            ins = split_mm(sc[:, ks], qdh[hp, h, q], qdl[hp, h, q], kdh[hp, h, ks], kdl[hp, h, ks],
                                           True, not own)
                            if own:
                                ins = pe.matmul(sc[:, P * i:P * i + P], identb[:], maskb[:], start=False, stop=True)
                        ins.then_inc(s_qk, 1)
                if 2 <= u < UN + 2:
                    v = u - 2
                    i = v // H
                    pe.wait_ge(s_wc, v + 1)
                    for f in range(fills(v)):
                        k = FILL0[v] + f
                        if k >= 2:
                            pe.wait_ge(s_wTe, k - 1)
                        w = min(4, i + 1 - 4 * f)
                        for j in range(w):
                            ins = pe.transpose(ps[:, 4 + k % 2, P * j:P * j + P],
                                               prob[:, v % 3, 0, P * (4 * f + j):P * (4 * f + j) + P], ident[:])
                        ins.then_inc(s_wT, 1)
                if 3 <= u < UN + 3:
                    v = u - 3
                    i, h = v // H, v % H
                    pe.wait_ge(s_wTe, FILL0[v + 1])
                    if h == 0 and i >= 2:
                        pe.wait_ge(s_ml, MIXED + i - 1)
                    for j in range(i + 1):
                        ins = pe.matmul(ps[:, 6 + i % 2, DV * h:DV * h + DV], wT[:, v % 2, j], vd[:, j, DV * h:DV * h + DV],
                                        start=j == 0, stop=j == i)
                    ins.then_inc(s_pv, 1)
                if u % H == 2 and u >= 10:
                    attn_transpose((u - 10) // H)
                if u in (UN + 2, UN + 4):
                    product((u - UN - 2) // 2)
            for t in range(NT + 3):
                if t == NB - PSEQ + 3:
                    pe.wait_ge(s_dec, DEC["normed"])
                    for h in range(H):
                        ins = pe.transpose(ps[:, 7, NB * h:NB * h + NB], dod[:, DV * h:DV * h + DV], ident[0:NB, 0:NB])
                    ins.then_inc(s_mT, 1)
                if 2 <= t <= NT:
                    product(t)
                if 1 <= t <= NT + 1:
                    v = t - 1
                    r = rows(v)
                    pe.wait_ge(s_h2h, v + 1)
                    pe.wait_ge(s_h2l, v + 1)
                    if v:
                        pe.wait_ge(s_hTh, v)
                    else:
                        pe.wait_ge(s_wTe, FILL0[UN])
                    for lo in range(2):
                        for k in range(KC):
                            ins = pe.transpose(bank16(4 + lo)[:, r * k:r * k + r],
                                               h2s[0:r, v % 2, D * lo + P * k:D * lo + P * k + P], ident16[0:r, 0:r])
                    ins.then_inc(s_h2T, 1)
                if t >= 2:
                    v = t - 2
                    r = rows(v)
                    if v == 0:
                        pe.wait_ge(s_wrs, 1)
                    else:
                        pe.wait_ge(s_rtr, v)
                    pe.wait_ge(s_hTh, v + 1)
                    for k in range(KC):
                        ins = split_mm(ps[0:r, 6, 0:NG + NE], h2T[:, v % 2, 0, k, 0:r], h2T[:, v % 2, 1, k, 0:r],
                                       wrh[:, k], wrl[:, k], k == 0, k == KC - 1)
                    ins.then_inc(s_rt, 1)
                if t == NB - PSEQ:
                    pe.wait_ge(s_acc, value_steps_to(2 * PSEQ - 1))
                    pe.wait_ge(s_acd, H * NPG * (NB - PSEQ))
                    pe.wait_ge(s_ml, MIXED + NT)
                    for b in range(NB):
                        ins = pe.matmul(ps[0:NB, 7, :], sel[:, NB - 1 - b:2 * NB - 1 - b], dacc[:, b], start=b == 0,
                                        stop=b == NB - 1)
                    ins.then_inc(s_ds, 1)
            pe.wait_ge(s_x1, 2 * (NT + 1))
            pe.wait_ge(s_re, 3)
            r_a2 = r_a.rearrange("p t e -> p (t e)")
            pe.matmul(ps[:, 0, 0:144], strict[:], r_a2, start=True, stop=True)
            pe.matmul(ps[:, 1, 0:144], ones[:], r_a2, start=True, stop=True).then_inc(s_rc, 1)
            for n in range(18):
                pe.wait_ge(s_rs1, n // 9 + 1)
                ins = pe.matmul(ps[:, 2, 0:COLS], oneh_p[:, n], oneh_c[:, n], start=n == 0, stop=n == 17)
            ins.then_inc(s_rsu, 1)
            pe.wait_ge(s_route, 1)

            def transpose_tokens(s, loaded, e4, e2):
                pe.wait_ge(s_gx[s], loaded)
                for f in range(4):
                    lo, kh = f // 2, f % 2
                    if e2 is not None or f >= 2:
                        pe.wait_ge((s_ea, s_ev2)[kh], (0 if e2 is None else e2) + lo)
                    for k in range(4):
                        col = D * lo + P * (4 * kh + k)
                        pe.transpose(bank16(kh)[:, CAP * k:CAP * k + P], xg[:, s, 0, col:col + P], ident16[:])
                        ins = pe.transpose(bank16(kh)[:, CAP * k + P:CAP * k + CAP], xg[0:CAP1, s, 1, col:col + P],
                                           ident16[0:CAP1, 0:CAP1])
                    ins.then_inc(s_eT, 1)

            def slot(i, off, e=None):
                s = off % 2

                def at(k, c):
                    return k * 2 * i + (k * off + c)

                if e != NE:
                    pe.wait_ge(s_mlo, at(2, 2))
                    pe.wait_ge(s_ea, at(2, 2))
                    pe.wait_ge(s_ev2, at(2, 2))
                    if e != 0:
                        pe.wait_ge(s_hf, at(1, 0))
                    for bank, wh, wl in ((2, egh[s], egl[s]), (3, euh[s], eul[s])):
                        for ft in range(2):
                            fs = slice(P * ft, P * ft + P)
                            for k in range(KC):
                                ins = split_mm(ps[:, bank, CAP * ft:CAP * ft + CAP], wh[:, k, fs], wl[:, k, fs],
                                               xT[:, s, 0, k], xT[:, s, 1, k], k == 0, k == KC - 1)
                    ins.then_inc(s_gup, 1)
                    if e != NE - 1:
                        transpose_tokens(1 - s, 32 * i + 32 * ((off + 1) // 2 + 1), at(4, 4), at(2, 2))
                if e != 0:
                    pe.wait_ge(s_hh2, at(1, 0))
                    pe.wait_ge(s_hl2, at(1, 0))
                    pe.wait_ge(s_mld, at(1, 0))
                    if e is None or e >= 2:
                        pe.wait_ge(s_ya, at(1, -1))
                        pe.wait_ge(s_yv, at(1, -1))
                    for g, (r0, r1) in enumerate(((0, P), (P, CAP))):
                        for half in range(2):
                            cs = slice(512 * half, 512 * half + 512)
                            for ft in range(2):
                                ins = split_mm(ps[0:r1 - r0, 4 + 2 * g + half, :], hidh[:, 1 - s, ft, r0:r1],
                                               hidl[:, 1 - s, ft, r0:r1], edh[1 - s][:, ft, cs], edl[1 - s][:, ft, cs],
                                               ft == 0, ft == 1)
                            ins.then_inc(s_down, 1)

            transpose_tokens(0, 32, None, None)
            run_slots(pe, slot)

            def overflow():
                with pe.Fori(0, NOV) as j:
                    def v(n):
                        return len(OV_VEC) * j + (1 + OV_VEC[n])

                    def a(n):
                        return len(OV_ACT) * j + OV_ACT[n]

                    pe.wait_ge(s_ovx, 16 * j + 16)
                    for lo in range(2):
                        for k in range(KC):
                            ins = pe.transpose(bank16(lo)[:, P * k:P * k + P],
                                               xg[:, 0, 0, D * lo + P * k:D * lo + P * k + P], ident16[:])
                    ins.then_inc(s_ovp, 1)
                    pe.wait_ge(s_ova, a("tokens_hi"))
                    pe.wait_ge(s_ovv, v("tokens_lo"))
                    for bank, wh, wl in ((2, egh[0], egl[0]), (3, euh[0], eul[0])):
                        for ft in range(2):
                            fs = slice(P * ft, P * ft + P)
                            for k in range(KC):
                                ins = split_mm(ps[:, bank, fs], wh[:, k, fs], wl[:, k, fs], ovxT[:, 0, k], ovxT[:, 1, k],
                                               k == 0, k == KC - 1)
                    ins.then_inc(s_ovp, 1)
                    pe.wait_ge(s_ova, a("hidden_hi"))
                    pe.wait_ge(s_ovv, v("hidden_lo"))
                    for half in range(2):
                        cs = slice(512 * half, 512 * half + 512)
                        for ft in range(2):
                            ins = split_mm(ps[:, 4 + half, :], ovhh[:, ft], ovhl[:, ft], edh[0][:, ft, cs],
                                           edl[0][:, ft, cs], ft == 0, ft == 1)
                    ins.then_inc(s_ovp, 1)

            when_overflow(pe, overflow)


_INS = ["x_prompt", "x_sample", "cache_k", "cache_v", "state_gla", "page_table", "norm1_g", "w_in", "w_a2", "b_a",
        "gla_norm_g", "lambda_q1", "lambda_k1", "lambda_q2", "lambda_k2", "diff_norm_g", "w_out", "norm2_g",
        "w_router_g", "b_router_g", "w_router_e", "b_router_e", "w_gate", "w_up", "w_down", "norm_f_g"]
_OUTS = [("y_prompt", (1, SEQ, D)), ("y_sample", (NB, 1, D)), ("k_prompt", (1, 1, SEQ, H, 2 * DK)),
         ("v_prompt", (1, 1, SEQ, H, DV)), ("gla_prompt", (1, 1, H, DK, DV)), ("k_sample", (1, NB, 1, H, 2 * DK)),
         ("v_sample", (1, NB, 1, H, DV)), ("gla_sample", (1, NB, H, DK, DV))]


def kernel(**inputs):
    import numpy as np
    import concourse.bacc as bacc
    from concourse.bass_utils import run_bass_kernel_spmd

    arrays = {n: np.ascontiguousarray(inputs[n]) for n in _INS}
    nc = bacc.Bacc("TRN2", target_bir_lowering=False, num_devices=1)
    ins = {n: nc.dram_tensor("in_" + n, a.shape, mybir.dt.from_np(a.dtype), kind="ExternalInput").ap()
           for n, a in arrays.items()}
    outs = {n: nc.dram_tensor("out_" + n, shape, F32, kind="ExternalOutput").ap() for n, shape in _OUTS}
    build(nc, ins, outs)
    r = run_bass_kernel_spmd(nc, [{"in_" + n: a for n, a in arrays.items()}], core_ids=[0])
    return tuple(r.results[0]["out_" + n] for n, _ in _OUTS)
```
